# Optimizing a Trainium2 kernel written in Bass

```python
import math
import jax, jax.numpy as jnp
from jax import lax
import numpy as np

"""One inference step of a 2-layer hybrid decoder trunk. Every layer: RMSNorm -> one combined
input projection whose columns are split into three parallel head groups (gated DeltaNet |
Mamba-2 SSD | short gated convolution) -> concat -> one output projection -> residual;
then RMSNorm -> hierarchical MoE (top-1 expert group, top-2 experts inside it) -> residual.
16 learned meta tokens are prepended to every prompt sequence; a final RMSNorm is applied.

Inputs:
  x_prompt       (BATCH, SEQ, D_MODEL)
  x_sample       (DEC_BATCH, DEC_SEQ, D_MODEL)
  state_gdn      (DEPTH, DEC_BATCH, H_A, DK_A, DV_A)          gated-delta matrix state
  state_gdn_conv (DEPTH, DEC_BATCH, CONV_A-1, D_QKV_A)        last pre-conv q/k/v rows
  state_ssd      (DEPTH, DEC_BATCH, H_B, P_B, N_B)            SSD state
  state_ssd_conv (DEPTH, DEC_BATCH, CONV_B-1, D_XBC)          last pre-conv x/B/C rows
  state_sconv    (DEPTH, DEC_BATCH, CONV_C-1, D_C)            last gated conv-input rows
  weights stacked over DEPTH, meta_tokens (N_META, D_MODEL), final_norm_w (D_MODEL,)
Returns the tuple
  (y_prompt (BATCH, SEQ, D_MODEL), y_sample (DEC_BATCH, DEC_SEQ, D_MODEL),
   new_gdn_p (DEPTH,BATCH,H_A,DK_A,DV_A), new_gdn_conv_p (DEPTH,BATCH,CONV_A-1,D_QKV_A),
   new_ssd_p (DEPTH,BATCH,H_B,P_B,N_B), new_ssd_conv_p (DEPTH,BATCH,CONV_B-1,D_XBC),
   new_sconv_p (DEPTH,BATCH,CONV_C-1,D_C),
   new_gdn_s, new_gdn_conv_s, new_ssd_s, new_ssd_conv_s, new_sconv_s  (same with DEC_BATCH))
"""

D_MODEL = 1024
BATCH = 1
SEQ = 1024
DEPTH = 1
DEC_BATCH = 8
DEC_SEQ = 8
PAST_LEN = 8192
PAGE_SIZE = 128

N_META = 16
H_A = 4
DK_A = 128
DV_A = 128
D_QK_A = H_A * DK_A
D_A = H_A * DV_A
D_QKV_A = 2 * D_QK_A + D_A
CONV_A = 4
H_B = 8
P_B = 64
D_B = H_B * P_B
G_B = 2
N_B = 128
D_XBC = D_B + 2 * G_B * N_B
CONV_B = 4
D_C = 512
CONV_C = 3
D_MIX = D_A + D_B + D_C
CHUNK = 64
PROJ_SPLITS = (D_QKV_A, D_A, H_A, H_A, D_XBC, D_B, H_B, D_C, D_C, D_C)
D_PROJ = D_QKV_A + D_A + 2 * H_A + D_XBC + D_B + H_B + 3 * D_C
N_EGROUPS = 4
EXP_PER_GROUP = 4
N_EXPERTS = N_EGROUPS * EXP_PER_GROUP
TOP_K = 2
D_FF_E = 256
EPS = 1e-6

kernel_name = "hymba_gdn_ssd_shortconv_hmoe_step"

def rmsnorm(x, w):
    xf = x.astype(jnp.float32)
    y = xf * lax.rsqrt(jnp.mean(xf * xf, axis=-1, keepdims=True) + EPS)
    return (y * w.astype(jnp.float32)).astype(x.dtype)

def l2norm(x):
    return x * lax.rsqrt(jnp.sum(x * x, axis=-1, keepdims=True) + EPS)

def causal_conv(u, hist, w):
    width, L = w.shape[0], u.shape[1]
    up = jnp.concatenate([hist.astype(u.dtype), u], axis=1)
    y = up[:, 0:L] * w[0]
    for i in range(1, width):
        y = y + up[:, i:i + L] * w[i]
    return y, up[:, L:]

def chunk_len(L):
    return CHUNK if L % CHUNK == 0 else L

def to_chunks(t, c):
    b, L, h = t.shape[:3]
    return t.reshape(b, L // c, c, h, *t.shape[3:]).swapaxes(2, 3)

def from_chunks(t):
    b, n, h, c = t.shape[:4]
    return t.swapaxes(2, 3).reshape(b, n * c, h, *t.shape[4:])

def decay_matrix(G):
    c = G.shape[-1]
    mask = jnp.tril(jnp.ones((c, c), bool))
    return jnp.exp(jnp.where(mask, G[..., :, None] - G[..., None, :], -jnp.inf))

def gdn_chunked(q, k, v, beta, g, S0):
    c = chunk_len(q.shape[1])
    q, k, v, beta, g = (to_chunks(t, c) for t in (q, k, v, beta, g))
    G = jnp.cumsum(g, axis=-1)
    dec = decay_matrix(G)
    strict = jnp.tril(jnp.ones((c, c), q.dtype), -1)
    kb = k * beta[..., None]
    A = jnp.eye(c, dtype=q.dtype) + jnp.einsum('bnhid,bnhjd->bnhij', kb, k) * dec * strict
    rhs = jnp.concatenate([v * beta[..., None], kb * jnp.exp(G)[..., None]], axis=-1)
    sol = lax.linalg.triangular_solve(A, rhs, left_side=True, lower=True, unit_diagonal=True)
    dv = v.shape[-1]
    U, Wk = sol[..., :dv], sol[..., dv:]
    qk = jnp.einsum('bnhid,bnhjd->bnhij', q, k) * dec
    qg = q * jnp.exp(G)[..., None]
    g_last = G[..., -1]
    kd = k * jnp.exp(g_last[..., None] - G)[..., None]

    def step(S, xs):
        u, wk, qg_c, qk_c, kd_c, gl = xs
        w = u - jnp.einsum('bhck,bhkv->bhcv', wk, S)
        o = jnp.einsum('bhck,bhkv->bhcv', qg_c, S) + jnp.einsum('bhij,bhjv->bhiv', qk_c, w)
        S = jnp.exp(gl)[..., None, None] * S + jnp.einsum('bhck,bhcv->bhkv', kd_c, w)
        return S, o

    xs = tuple(jnp.moveaxis(t, 1, 0) for t in (U, Wk, qg, qk, kd, g_last))
    S, o = lax.scan(step, S0, xs)
    return from_chunks(jnp.moveaxis(o, 0, 1)), S

def ssd_chunked(xdt, g, Bh, Ch, h0):
    c = chunk_len(xdt.shape[1])
    xdt, g, Bh, Ch = (to_chunks(t, c) for t in (xdt, g, Bh, Ch))
    G = jnp.cumsum(g, axis=-1)
    dec = decay_matrix(G)
    cb = jnp.einsum('bnhis,bnhjs->bnhij', Ch, Bh) * dec
    y_diag = jnp.einsum('bnhij,bnhjp->bnhip', cb, xdt)
    g_last = G[..., -1]
    dS = jnp.einsum('bnhjs,bnhjp->bnhps', Bh * jnp.exp(g_last[..., None] - G)[..., None], xdt)

    def step(h, xs):
        ds, gl = xs
        return jnp.exp(gl)[..., None, None] * h + ds, h

    hT, h_starts = lax.scan(step, h0, (jnp.moveaxis(dS, 1, 0), jnp.moveaxis(g_last, 1, 0)))
    h_starts = jnp.moveaxis(h_starts, 0, 1)
    y = y_diag + jnp.einsum('bnhis,bnhps->bnhip', Ch * jnp.exp(G)[..., None], h_starts)
    return from_chunks(y), hT

def run_segments(core, seq_args, state, seg_lens):
    outs, start = [], 0
    for L in seg_lens:
        o, state = core(*(a[:, start:start + L] for a in seq_args), state)
        outs.append(o)
        start += L
    return jnp.concatenate(outs, axis=1), state

def token_mixers(hn, hist_a, hist_b, hist_c, s_a, s_b, seg_lens, w_in, conv_a_w, a_log_a,
                 dt_bias_a, onorm_a_w, conv_b_w, conv_b_b, a_log_b, dt_bias_b, d_skip_b,
                 onorm_b_w, conv_c_w, w_out):
    f32 = jnp.float32
    bsz, L, _ = hn.shape
    proj = jnp.einsum('bld,dp->blp', hn, w_in)
    qkv_a, z_a, b_a, a_a, xbc_b, z_b, dt_b, h_c, c_c, b_c = jnp.split(
        proj, np.cumsum(PROJ_SPLITS)[:-1].tolist(), axis=-1)

    qkv, new_hist_a = causal_conv(qkv_a, hist_a, conv_a_w)
    qkv = jax.nn.silu(qkv).astype(f32)
    q, k, v = jnp.split(qkv, [D_QK_A, 2 * D_QK_A], axis=-1)
    q = l2norm(q.reshape(bsz, L, H_A, DK_A)) * (DK_A ** -0.5)
    k = l2norm(k.reshape(bsz, L, H_A, DK_A))
    v = v.reshape(bsz, L, H_A, DV_A)
    beta = jax.nn.sigmoid(b_a.astype(f32))
    g_a = -jnp.exp(a_log_a.astype(f32)) * jax.nn.softplus(a_a.astype(f32) + dt_bias_a.astype(f32))
    o_a, s_a = run_segments(gdn_chunked, (q, k, v, beta, g_a), s_a.astype(f32), seg_lens)
    o_a = rmsnorm(o_a, onorm_a_w) * jax.nn.silu(z_a.astype(f32).reshape(bsz, L, H_A, DV_A))
    o_a = o_a.reshape(bsz, L, D_A).astype(hn.dtype)

    xbc, new_hist_b = causal_conv(xbc_b, hist_b, conv_b_w)
    xbc = jax.nn.silu(xbc + conv_b_b).astype(f32)
    xs, Bm, Cm = jnp.split(xbc, [D_B, D_B + G_B * N_B], axis=-1)
    xs = xs.reshape(bsz, L, H_B, P_B)
    Bh = jnp.repeat(Bm.reshape(bsz, L, G_B, N_B), H_B // G_B, axis=2)
    Ch = jnp.repeat(Cm.reshape(bsz, L, G_B, N_B), H_B // G_B, axis=2)
    dt = jax.nn.softplus(dt_b.astype(f32) + dt_bias_b.astype(f32))
    g_b = -jnp.exp(a_log_b.astype(f32)) * dt
    y_b, s_b = run_segments(ssd_chunked, (xs * dt[..., None], g_b, Bh, Ch), s_b.astype(f32), seg_lens)
    y_b = (y_b + d_skip_b.astype(f32)[:, None] * xs).reshape(bsz, L, D_B) * jax.nn.silu(z_b.astype(f32))
    y_b = rmsnorm(y_b.reshape(bsz, L, G_B, D_B // G_B), onorm_b_w.reshape(G_B, D_B // G_B))
    y_b = y_b.reshape(bsz, L, D_B).astype(hn.dtype)

    y_c, new_hist_c = causal_conv(c_c * h_c, hist_c, conv_c_w)
    y_c = b_c * y_c

    mixed = jnp.concatenate([o_a, y_b, y_c], axis=-1)
    out = jnp.einsum('blm,md->bld', mixed, w_out)
    return out, new_hist_a, new_hist_b, new_hist_c, s_a, s_b

def hier_moe(h, w_router_g, w_router_e, w_gate, w_up, w_down):
    f32 = jnp.float32
    p_grp = jax.nn.softmax(jnp.einsum('bld,dg->blg', h, w_router_g).astype(f32), axis=-1)
    g_idx = jnp.argmax(p_grp, axis=-1)
    g_hot = jax.nn.one_hot(g_idx, N_EGROUPS, dtype=f32)
    p_top = jnp.sum(p_grp * g_hot, axis=-1)
    le = jnp.einsum('bld,de->ble', h, w_router_e).astype(f32)
    le = le.reshape(*le.shape[:2], N_EGROUPS, EXP_PER_GROUP)
    le_sel = jnp.einsum('blge,blg->ble', le, g_hot)
    top_v, top_i = lax.top_k(jax.nn.softmax(le_sel, axis=-1), TOP_K)
    top_v = top_v / jnp.sum(top_v, axis=-1, keepdims=True)
    e_idx = g_idx[..., None] * EXP_PER_GROUP + top_i
    comb = jnp.einsum('blke,blk->ble', jax.nn.one_hot(e_idx, N_EXPERTS, dtype=f32),
                      top_v * p_top[..., None])
    hg = jnp.einsum('bld,edf->blef', h, w_gate)
    hu = jnp.einsum('bld,edf->blef', h, w_up)
    act = jax.nn.silu(hg) * hu * comb.astype(h.dtype)[..., None]
    return jnp.einsum('blef,efd->bld', act, w_down)

def trunk_layer(x, hist_a, hist_b, hist_c, s_a, s_b, seg_lens, mix_w, moe_w, norm1_w, norm2_w):
    m, hist_a, hist_b, hist_c, s_a, s_b = token_mixers(
        rmsnorm(x, norm1_w), hist_a, hist_b, hist_c, s_a, s_b, seg_lens, *mix_w)
    x = x + m
    x = x + hier_moe(rmsnorm(x, norm2_w), *moe_w)
    return x, (s_a.astype(x.dtype), hist_a, s_b.astype(x.dtype), hist_b, hist_c)

def stack_layers(states, i):
    return jnp.stack([s[i] for s in states], axis=0)

def setup_inputs(seed: int = 0) -> dict:
    key = jax.random.key(seed)
    ks = iter(jax.random.split(key, 40))
    f32 = jnp.float32

    def nrm(shape, scale):
        return jax.random.normal(next(ks), shape, f32) * scale

    def gain(shape):
        return 1.0 + nrm(shape, 0.02)

    def a_log(shape):
        return jnp.log(jax.random.uniform(next(ks), shape, f32, 1.0, 16.0))

    def dt_bias(shape):
        dt = jnp.exp(jax.random.uniform(next(ks), shape, f32, math.log(1e-3), math.log(1e-1)))
        return dt + jnp.log(-jnp.expm1(-dt))

    return {
        'x_prompt': nrm((BATCH, SEQ, D_MODEL), 1.0),
        'x_sample': nrm((DEC_BATCH, DEC_SEQ, D_MODEL), 1.0),
        'state_gdn': nrm((DEPTH, DEC_BATCH, H_A, DK_A, DV_A), 0.5),
        'state_gdn_conv': nrm((DEPTH, DEC_BATCH, CONV_A - 1, D_QKV_A), 1.0),
        'state_ssd': nrm((DEPTH, DEC_BATCH, H_B, P_B, N_B), 0.5),
        'state_ssd_conv': nrm((DEPTH, DEC_BATCH, CONV_B - 1, D_XBC), 1.0),
        'state_sconv': nrm((DEPTH, DEC_BATCH, CONV_C - 1, D_C), 1.0),
        'meta_tokens': nrm((N_META, D_MODEL), 1.0),
        'norm1_w': gain((DEPTH, D_MODEL)),
        'w_in': nrm((DEPTH, D_MODEL, D_PROJ), D_MODEL ** -0.5),
        'conv_a_w': nrm((DEPTH, CONV_A, D_QKV_A), CONV_A ** -0.5),
        'a_log_a': a_log((DEPTH, H_A)),
        'dt_bias_a': dt_bias((DEPTH, H_A)),
        'onorm_a_w': gain((DEPTH, DV_A)),
        'conv_b_w': nrm((DEPTH, CONV_B, D_XBC), CONV_B ** -0.5),
        'conv_b_b': nrm((DEPTH, D_XBC), 0.02),
        'a_log_b': a_log((DEPTH, H_B)),
        'dt_bias_b': dt_bias((DEPTH, H_B)),
        'd_skip_b': gain((DEPTH, H_B)),
        'onorm_b_w': gain((DEPTH, D_B)),
        'conv_c_w': nrm((DEPTH, CONV_C, D_C), CONV_C ** -0.5),
        'w_out': nrm((DEPTH, D_MIX, D_MODEL), D_MIX ** -0.5),
        'norm2_w': gain((DEPTH, D_MODEL)),
        'w_router_g': nrm((DEPTH, D_MODEL, N_EGROUPS), D_MODEL ** -0.5),
        'w_router_e': nrm((DEPTH, D_MODEL, N_EXPERTS), D_MODEL ** -0.5),
        'w_gate': nrm((DEPTH, N_EXPERTS, D_MODEL, D_FF_E), D_MODEL ** -0.5),
        'w_up': nrm((DEPTH, N_EXPERTS, D_MODEL, D_FF_E), D_MODEL ** -0.5),
        'w_down': nrm((DEPTH, N_EXPERTS, D_FF_E, D_MODEL), D_FF_E ** -0.5),
        'final_norm_w': gain((D_MODEL,)),
    }

def reference(x_prompt, x_sample, state_gdn, state_gdn_conv, state_ssd, state_ssd_conv, state_sconv,
              meta_tokens, norm1_w, w_in, conv_a_w, a_log_a, dt_bias_a, onorm_a_w, conv_b_w, conv_b_b,
              a_log_b, dt_bias_b, d_skip_b, onorm_b_w, conv_c_w, w_out, norm2_w, w_router_g,
              w_router_e, w_gate, w_up, w_down, final_norm_w):
    bp = x_prompt.shape[0]
    dtp = x_prompt.dtype
    meta = jnp.broadcast_to(meta_tokens.astype(dtp)[None], (bp, N_META, x_prompt.shape[2]))
    x_p = jnp.concatenate([meta, x_prompt], axis=1)
    x_s = x_sample
    seg_p = (N_META, x_prompt.shape[1])
    seg_s = (x_sample.shape[1],)
    new_p, new_s = [], []
    for l in range(DEPTH):
        mix_w = (w_in[l], conv_a_w[l], a_log_a[l], dt_bias_a[l], onorm_a_w[l], conv_b_w[l], conv_b_b[l],
                 a_log_b[l], dt_bias_b[l], d_skip_b[l], onorm_b_w[l], conv_c_w[l], w_out[l])
        moe_w = (w_router_g[l], w_router_e[l], w_gate[l], w_up[l], w_down[l])
        x_p, st_p = trunk_layer(
            x_p, jnp.zeros((bp, CONV_A - 1, D_QKV_A), dtp), jnp.zeros((bp, CONV_B - 1, D_XBC), dtp),
            jnp.zeros((bp, CONV_C - 1, D_C), dtp), jnp.zeros((bp, H_A, DK_A, DV_A), jnp.float32),
            jnp.zeros((bp, H_B, P_B, N_B), jnp.float32), seg_p, mix_w, moe_w, norm1_w[l], norm2_w[l])
        x_s, st_s = trunk_layer(
            x_s, state_gdn_conv[l], state_ssd_conv[l], state_sconv[l], state_gdn[l], state_ssd[l],
            seg_s, mix_w, moe_w, norm1_w[l], norm2_w[l])
        new_p.append(st_p)
        new_s.append(st_s)
    y_prompt = rmsnorm(x_p, final_norm_w)[:, N_META:]
    y_sample = rmsnorm(x_s, final_norm_w)
    return (y_prompt, y_sample,
            stack_layers(new_p, 0), stack_layers(new_p, 1), stack_layers(new_p, 2),
            stack_layers(new_p, 3), stack_layers(new_p, 4),
            stack_layers(new_s, 0), stack_layers(new_s, 1), stack_layers(new_s, 2),
            stack_layers(new_s, 3), stack_layers(new_s, 4))


_drawn_inputs = setup_inputs


def setup_inputs(seed=0):
    import zlib

    import numpy as np

    out = dict(_drawn_inputs(seed))
    spreads = {}
    factors = {'onorm_a_w': 5.591,
     'd_skip_b': 6.497,
     'onorm_b_w': 3.195,
     'norm2_w': 2.756,
     'final_norm_w': 2.739}
    for name, (base, spread) in spreads.items():
        noise = np.random.default_rng([zlib.crc32(name.encode()), seed]).standard_normal(out[name].shape)
        drawn = base * np.exp(spread * noise) if base else spread * noise
        out[name] = __import__('jax').numpy.asarray(drawn.astype(out[name].dtype))
    for name, factor in factors.items():
        out[name] = (out[name] * factor).astype(out[name].dtype)
    return out
```

```python
from contextlib import ExitStack

import numpy as np

import concourse.bass as bass
from concourse import mybir

F32 = mybir.dt.float32
ALU = mybir.AluOpType
ACT = mybir.ActivationFunctionType
AX = mybir.AxisListType

P = 128
D = 1024
KD = D // P
N_META, SEQ = 16, 1024
TP = N_META + SEQ
NSEQ, LSEQ = 8, 8
TS = NSEQ * LSEQ
T = TP + TS
NT, TW = 3, T // 3
HA, DK = 4, 128
HB, PB, GB, NB = 8, 64, 2, 128
CH = 104
NCH = TP // CH
W_A, W_C = 4, 3
NCONV, NZ, NC = 20, 8, 4
HIST = W_A - 1
RAW = HIST + TP + NSEQ * (HIST + LSEQ)
CONVW = RAW - HIST
HISTC = W_C - 1
RAWC = HISTC + TP + NSEQ * (HISTC + LSEQ)
CONVWC = RAWC - HISTC
NPAIR = 2
NE, NG, EPG, FF = 16, 4, 4, 256
NMIX = 12
EPS = 1e-6
NEG = -1e30
ROW_G = 32
NR = 12
TAIL = TP - 2 * TW


def samples(ap, base, stride, lo, hi):
    return ap[:, base:base + NSEQ * stride].rearrange("p (b s) -> p b s", s=stride)[:, :, lo:hi]


def one(ap, b):
    names = "xyz"[:len(ap.shape) - 2]
    return ap[:, bass.ds(b, 1)].rearrange(f"p a {' '.join(names)} -> p (a {names[0]}) {' '.join(names[1:])}")


class Memory:

    def __init__(self, nc, stack):
        self.nc, self.stack = nc, stack

    def sb(self, name, shape, dt=F32):
        return self.stack.enter_context(self.nc.sbuf_tensor(name, shape, dt))

    def ps(self, name, shape, dt=F32):
        return self.stack.enter_context(self.nc.psum_tensor(name, shape, dt))

    def sem(self, name):
        return self.stack.enter_context(self.nc.semaphore(name))


def norm1_phase(nc, io, hn, ones, masks):
    with ExitStack() as stack:
        m = Memory(nc, stack)
        w1 = m.sb("n1_w", [P, KD])
        sq = m.sb("n1_sq", [P, 2, T])
        rb = m.sb("n1_rb", [P, T])
        ss = m.ps("n1_ss", [P, NT, 512])
        loaded, ones_set = m.sem("n1_loaded"), m.sem("n1_ones")
        squared, summed = m.sem("n1_squared"), m.sem("n1_summed")
        mean_ready, scaled = m.sem("n1_mean"), m.sem("n1_scaled")
        block = stack.enter_context(nc.Block())

        @block.sync
        def _(sp):
            sp.dma_start(w1[:], io["norm1_w"]).then_inc(loaded, 16)
            sp.dma_start(masks[:], io["masks"]).then_inc(loaded, 16)
            for k in range(KD):
                sp.dma_start(hn[:, k, :], io["xT"][:, k, :]).then_inc(loaded, 16)

        @block.scalar
        def _(act):
            act.wait_ge(loaded, 16 * (KD + 2))
            for k in range(KD):
                if k >= 2:
                    act.wait_ge(summed, k - 1)
                act.activation(sq[:, k % 2, :], hn[:, k, :], ACT.Square).then_inc(squared, 1)
            act.wait_ge(mean_ready, 1)
            act.activation(rb[:], rb[:], ACT.Sqrt).then_inc(mean_ready, 1)

        @block.tensor
        def _(pe):
            pe.wait_ge(ones_set, 1)
            for k in range(KD):
                pe.wait_ge(squared, k + 1)
                for n in range(NT):
                    mm = pe.matmul(ss[:, n, 0:TW], ones[:], sq[:, k % 2, n * TW:(n + 1) * TW],
                                   start=(k == 0), stop=(k == KD - 1))
                mm.then_inc(summed, 1)

        @block.vector
        def _(dve):
            dve.memset(ones[:], 1.0).then_inc(ones_set, 1)
            dve.wait_ge(summed, KD)
            dve.tensor_scalar(rb[:].rearrange("p (n t) -> p n t", n=NT), ss[:, :, 0:TW], 1.0 / D, EPS,
                              ALU.mult, ALU.add).then_inc(mean_ready, 1)
            dve.wait_ge(mean_ready, 2)
            dve.reciprocal(rb[:], rb[:]).then_inc(mean_ready, 1)
            dve.wait_ge(mean_ready, 3)
            for k in range(KD):
                dve.scalar_tensor_tensor(hn[:, k, :], hn[:, k, :], w1[:, k:k + 1], rb[:],
                                         ALU.mult, ALU.mult).then_inc(scaled, 1)


def gates_phase(nc, io, hn, rows_a, rows_b, rows_c, g_dram):
    with ExitStack() as stack:
        m = Memory(nc, stack)
        wg = m.sb("g_w", [P, KD, 64])
        bias = m.sb("g_bias", [64, 1])
        a_log = m.sb("g_alog", [64, 1])
        neg_a = m.sb("g_nega", [64, 1])
        mask = m.sb("g_mask", [64, T])
        y = m.sb("g_y", [64, T])
        u = m.sb("g_u", [64, T])
        d = m.sb("g_d", [64, T])
        ps = m.ps("g_ps", [P, NT, 512])
        loaded, set_, proj = m.sem("g_loaded"), m.sem("g_set"), m.sem("g_proj")
        act_step, dve_step, out = m.sem("g_act"), m.sem("g_dve"), m.sem("g_out")
        block = stack.enter_context(nc.Block())
        gr = slice(ROW_G, ROW_G + NR)

        def tiles(ap):
            return ap.rearrange("p (n t) -> p n t", n=NT)

        @block.sync
        def _(sp):
            sp.dma_start(wg[:], io["w_gates"]).then_inc(loaded, 16)
            sp.dma_start(bias[:], io["gate_bias"]).then_inc(loaded, 16)
            sp.dma_start(a_log[:], io["gate_alog"]).then_inc(loaded, 16)
            sp.wait_ge(dve_step, 13)
            sp.dma_start(g_dram, rows_a[gr, :]).then_inc(out, 16)
            sp.wait_ge(out, 16)

        @block.tensor
        def _(pe):
            pe.wait_ge(loaded, 48)
            for n in range(NT):
                for k in range(KD):
                    mm = pe.matmul(ps[0:64, n, 0:TW], wg[:, k, :], hn[:, k, n * TW:(n + 1) * TW],
                                   start=(k == 0), stop=(k == KD - 1))
            mm.then_inc(proj, 1)

        @block.scalar
        def _(act):
            act.wait_ge(proj, 1)
            act.wait_ge(set_, 4)
            act.activation(tiles(rows_a[0:HA, :]), ps[0:HA, :, 0:TW], ACT.Exp, scale=-1.0).then_inc(act_step, 1)
            act.activation(neg_a[gr, :], a_log[gr, :], ACT.Exp).then_inc(act_step, 1)
            act.wait_ge(dve_step, 3)
            act.activation(y[gr, :], u[gr, :], ACT.Exp).then_inc(act_step, 1)
            act.wait_ge(dve_step, 5)
            act.activation(d[gr, :], u[gr, :], ACT.Ln).then_inc(act_step, 1)

        @block.vector
        def _(dve):
            dve.memset(rows_a[:], 0.0).then_inc(set_, 1)
            dve.memset(rows_b[:], 0.0).then_inc(set_, 1)
            dve.memset(rows_c[:], 0.0).then_inc(set_, 1)
            dve.memset(mask[:], 1.0).then_inc(set_, 1)
            dve.wait_ge(set_, 4)
            dve.memset(mask[:, 0:TP].rearrange("p (c t) -> p c t", t=CH)[:, :, 0:1], 0.0).then_inc(set_, 1)
            dve.memset(samples(mask, TP, LSEQ, 0, 1), 0.0).then_inc(set_, 1)
            dve.wait_ge(proj, 1)
            dve.wait_ge(loaded, 48)
            dve.tensor_scalar(tiles(rows_c[gr, :]), ps[gr, :, 0:TW], bias[gr, :], None,
                              ALU.add).then_inc(dve_step, 1)
            dve.wait_ge(dve_step, 1)
            dve.tensor_scalar(d[gr, :], rows_c[gr, :], -1.0, None, ALU.mult).then_inc(dve_step, 1)
            dve.wait_ge(dve_step, 2)
            dve.tensor_tensor(u[gr, :], rows_c[gr, :], d[gr, :], ALU.min).then_inc(dve_step, 1)
            dve.wait_ge(act_step, 1)
            dve.tensor_scalar(rows_a[0:HA, :], rows_a[0:HA, :], 1.0, None, ALU.add).then_inc(dve_step, 1)
            dve.wait_ge(act_step, 3)
            dve.tensor_scalar(u[gr, :], y[gr, :], 1.0, None, ALU.add).then_inc(dve_step, 1)
            dve.wait_ge(dve_step, 5)
            dve.scalar_tensor_tensor(y[gr, :], u[gr, :], -1.0, y[gr, :], ALU.add, ALU.subtract,
                                     ).then_inc(dve_step, 1)
            dve.reciprocal(rows_a[0:HA, :], rows_a[0:HA, :]).then_inc(dve_step, 1)
            dve.wait_ge(act_step, 4)
            dve.reciprocal(u[gr, :], u[gr, :]).then_inc(dve_step, 1)
            dve.wait_ge(dve_step, 8)
            dve.tensor_tensor(y[gr, :], y[gr, :], u[gr, :], ALU.mult).then_inc(dve_step, 1)
            dve.wait_ge(dve_step, 9)
            dve.tensor_tensor(d[gr, :], d[gr, :], y[gr, :], ALU.subtract).then_inc(dve_step, 1)
            dve.wait_ge(dve_step, 10)
            dve.scalar_tensor_tensor(rows_c[gr, :], rows_c[gr, :], 0.0, d[gr, :], ALU.max,
                                     ALU.add).then_inc(dve_step, 1)
            dve.wait_ge(dve_step, 11)
            dve.tensor_scalar(y[gr, :], rows_c[gr, :], neg_a[gr, :], -1.0, ALU.mult,
                              ALU.mult).then_inc(dve_step, 1)
            dve.wait_ge(dve_step, 12)
            dve.wait_ge(set_, 6)
            dve.tensor_tensor_scan(rows_a[gr, :], mask[gr, :], y[gr, :], 0.0, ALU.mult,
                                   ALU.add).then_inc(dve_step, 1)
            dve.wait_ge(dve_step, 13)
            for start, length in ((0, CH), (TP, LSEQ)):
                end = TP if start == 0 else T
                g = rows_a[gr, start:end].rearrange("p (c t) -> p c t", t=length)
                o = rows_b[gr, start:end].rearrange("p (c t) -> p c t", t=length)
                dve.tensor_tensor(o, g[:, :, length - 1:length].to_broadcast(list(g.shape)), g,
                                  ALU.subtract).then_inc(dve_step, 1)


def put_raw(op, dst, src, hist_n):
    op(dst[:, hist_n:hist_n + TW], src[:, 0, 0:TW], (0, TW))
    op(dst[:, hist_n + TW:hist_n + 2 * TW], src[:, 1, 0:TW], (TW, 2 * TW))
    op(dst[:, hist_n + 2 * TW:hist_n + TP], src[:, 2, 0:TAIL], (2 * TW, TP))
    return op(samples(dst, hist_n + TP, hist_n + LSEQ, hist_n, hist_n + LSEQ),
              src[:, 2, TAIL:TW].rearrange("p (b t) -> p b t", t=LSEQ), (TP, T))


def keep_tail(eng, tails, b, raw, hist_n):
    tail = one(tails, b)
    eng.tensor_copy(tail[:, 0, :], raw[:, TP:TP + hist_n])
    return eng.tensor_copy(tail[:, 1:, :], samples(raw, hist_n + TP, hist_n + LSEQ, LSEQ, hist_n + LSEQ))


def projection_phase(nc, io, hn, act_out, z_dram, yc_dram):
    with ExitStack() as stack:
        m = Memory(nc, stack)
        w = m.sb("c_w", [P, 2, KD, P])
        raw = m.sb("c_raw", [P, 2, RAW])
        y = m.sb("c_y", [P, 2, RAW])
        out = m.sb("c_out", [P, 2, T])
        taps = m.sb("c_taps", [P, NCONV, W_A + 1])
        hist = m.sb("c_hist", [P, NCONV, NSEQ, HIST])
        tails = m.sb("c_tails", [P, NCONV, 1 + NSEQ, HIST])
        taps_c = m.sb("c_tapsc", [P, NC, W_C])
        hist_c = m.sb("c_histc", [P, NC, NSEQ, HISTC])
        tails_c = m.sb("c_tailsc", [P, NC, 1 + NSEQ, HISTC])
        ps = m.ps("c_ps", [P, 2, NT, 512])

        def pair(name):
            return [m.sem(f"c_{name}{h}") for h in range(2)]

        consts, kept = m.sem("c_consts"), m.sem("c_kept")
        w_loaded, proj_done = pair("wloaded"), pair("proj")
        ps_free, raw_done, hist_done, tail_done = pair("psfree"), pair("raw"), pair("hist"), pair("tail")
        tapped, conv_done, silu_done = pair("tapped"), pair("conv"), pair("silu")
        z_done, z_sent, yc_sent, out_free = pair("z"), pair("zsent"), pair("ycsent"), pair("outfree")
        h_done, craw_done, ctapped, yc_done = m.sem("c_h"), m.sem("c_craw"), m.sem("c_ctapped"), m.sem("c_yc")
        chist_done, ctail_done = m.sem("c_chist"), m.sem("c_ctail")
        NB_ALL = NCONV + NZ + 3 * NC

        with nc.Block() as block:
            @block.sync
            def _(sp):
                sp.dma_start(taps[:], io["taps"]).then_inc(consts, 16)
                sp.dma_start(hist[:], io["hist_ab"]).then_inc(consts, 16)
                sp.dma_start(taps_c[:], io["taps_c"]).then_inc(consts, 16)
                sp.dma_start(hist_c[:], io["hist_c"]).then_inc(consts, 16)
                for h in range(2):
                    sp.dma_start(w[:, h], io["w_in"][h]).then_inc(w_loaded[h], 16)
                with sp.Fori(0, NB_ALL // 2 - 1) as i:
                    for h in range(2):
                        sp.wait_ge(proj_done[h], i + 1)
                        sp.dma_start(w[:, h], io["w_in"][bass.ds(i * 2 + (2 + h), 1)].rearrange(
                            "a p k c -> (a p) k c")).then_inc(w_loaded[h], 16)
                for h in range(2):
                    sp.wait_ge(z_sent[h], 16 * (NZ // 2))
                    sp.wait_ge(yc_sent[h], 16 * NPAIR)
                sp.wait_ge(kept, 32)

            @block.tensor
            def _(pe):
                with pe.Fori(0, NB_ALL // 2) as i:
                    for h in range(2):
                        pe.wait_ge(w_loaded[h], i * 16 + 16)
                        pe.wait_ge(ps_free[h], i + 1)
                        for n in range(NT):
                            for k in range(KD):
                                mm = pe.matmul(ps[:, h, n, 0:TW], w[:, h, k, :], hn[:, k, n * TW:(n + 1) * TW],
                                               start=(k == 0), stop=(k == KD - 1))
                        mm.then_inc(proj_done[h], 1)

            @block.scalar
            def _(act):
                for h in range(2):
                    act.sem_inc(ps_free[h], 1)
                    act.sem_inc(raw_done[h], 1)
                    act.sem_inc(silu_done[h], 1)
                with act.Fori(0, NCONV // 2) as i:
                    for h in range(2):
                        act.wait_ge(proj_done[h], i + 1)
                        act.wait_ge(conv_done[h], i + 1)
                        act.wait_ge(tail_done[h], i + 1)
                        put_raw(lambda o, s, _: act.copy(o, s), raw[:, h, :], ps[:, h], HIST).then_inc(raw_done[h], 1)
                        act.wait_ge(raw_done[h], i + 2)
                        act.sem_inc(ps_free[h], 1)
                        act.wait_ge(conv_done[h], i + 2)
                        dst = one(act_out, i * 2 + h)
                        act.activation(dst[:, 0:TP], y[:, h, 0:TP], ACT.Silu)
                        act.activation(dst[:, TP:T].rearrange("p (b t) -> p b t", t=LSEQ),
                                       samples(y[:, h], TP, HIST + LSEQ, HIST, HIST + LSEQ),
                                       ACT.Silu).then_inc(silu_done[h], 1)
                with act.Fori(0, NZ // 2) as i:
                    for h in range(2):
                        act.wait_ge(proj_done[h], i + (NCONV // 2 + 1))
                        act.wait_ge(out_free[h], i + 1)
                        act.activation(out[:, h, :].rearrange("p (n t) -> p n t", n=NT), ps[:, h, :, 0:TW],
                                       ACT.Silu).then_inc(z_done[h], 1)
                        act.wait_ge(z_done[h], i + 1)
                        act.sem_inc(ps_free[h], 1)
                act.wait_ge(conv_done[0], NCONV // 2 + 1)
                act.wait_ge(tail_done[0], NCONV // 2 + 1)
                with act.Fori(0, NPAIR) as i:
                    for c in range(2):
                        act.wait_ge(proj_done[c], i * 3 + (NCONV + NZ) // 2 + 1 + c)
                        act.wait_ge(craw_done, i * 2 + (1 + c))
                        act.copy(raw[:, 0, 0:T].rearrange("p (n t) -> p n t", n=NT),
                                 ps[:, c, :, 0:TW]).then_inc(h_done, 1)
                        act.wait_ge(h_done, i * 2 + (1 + c))
                        act.sem_inc(ps_free[c], 1)

            @block.gpsimd
            def _(pool):
                for h in range(2):
                    pool.sem_inc(out_free[h], 1)
                    pool.sem_inc(tail_done[h], 1)
                    pool.memset(raw[:, h, 0:HIST], 0.0).then_inc(hist_done[h], 1)
                pool.wait_ge(consts, 64)
                with pool.Fori(0, NCONV // 2) as i:
                    for h in range(2):
                        pool.wait_ge(conv_done[h], i + 1)
                        pool.wait_ge(tail_done[h], i + 1)
                        pool.wait_ge(hist_done[h], i + 1)
                        pool.tensor_copy(samples(raw[:, h], HIST + TP, HIST + LSEQ, 0, HIST),
                                         one(hist, i * 2 + h)).then_inc(hist_done[h], 1)
                        pool.wait_ge(raw_done[h], i + 2)
                        keep_tail(pool, tails, i * 2 + h, raw[:, h], HIST).then_inc(tail_done[h], 1)
                for h in range(2):
                    pool.wait_ge(tail_done[h], NCONV // 2 + 1)
                pool.dma_start(io["new_hist_ab"], tails[:]).then_inc(kept, 16)
                with pool.Fori(0, NZ // 2) as i:
                    for h in range(2):
                        pool.wait_ge(z_done[h], i + 1)
                        pool.dma_start(z_dram[bass.ds(i * 2 + h, 1)].rearrange("a p t -> (a p) t"),
                                       out[:, h, :]).then_inc(z_sent[h], 16)
                        pool.wait_ge(z_sent[h], i * 16 + 16)
                        pool.sem_inc(out_free[h], 1)
                for h in range(2):
                    pool.wait_ge(conv_done[h], NCONV // 2 + 1)
                pool.memset(raw[:, 1, 0:HISTC], 0.0).then_inc(chist_done, 1)
                with pool.Fori(0, NPAIR) as i:
                    for c in range(2):
                        pool.wait_ge(yc_done, i * 2 + (1 + c))
                        pool.wait_ge(ctail_done, i * 2 + (1 + c))
                        pool.wait_ge(chist_done, i * 2 + (1 + c))
                        pool.tensor_copy(samples(raw[:, 1], HISTC + TP, HISTC + LSEQ, 0, HISTC),
                                         one(hist_c, i * 2 + c)).then_inc(chist_done, 1)
                        pool.wait_ge(craw_done, i * 2 + (2 + c))
                        keep_tail(pool, tails_c, i * 2 + c, raw[:, 1], HISTC).then_inc(ctail_done, 1)
                        pool.wait_ge(yc_done, i * 2 + (2 + c))
                        pool.dma_start(yc_dram[bass.ds(i * 2 + c, 1)].rearrange("a p t -> (a p) t"),
                                       out[:, c, :]).then_inc(yc_sent[c], 16)
                        pool.wait_ge(yc_sent[c], i * 16 + 16)
                        pool.sem_inc(out_free[c], 1)
                pool.wait_ge(ctail_done, NC + 1)
                pool.dma_start(io["new_hist_c"], tails_c[:]).then_inc(kept, 16)

            @block.vector
            def _(dve):
                dve.sem_inc(conv_done[0], 1)
                dve.sem_inc(conv_done[1], 1)
                dve.sem_inc(craw_done, 1)
                dve.sem_inc(yc_done, 1)
                dve.sem_inc(ctail_done, 1)
                dve.wait_ge(consts, 64)
                with dve.Fori(0, NCONV // 2) as i:
                    for h in range(2):
                        dve.wait_ge(raw_done[h], i + 2)
                        dve.wait_ge(hist_done[h], i + 2)
                        dve.wait_ge(silu_done[h], i + 1)
                        tap = taps[:, bass.ds(i * 2 + h, 1), :].rearrange("p a t -> p (a t)")
                        dve.tensor_scalar(y[:, h, 0:CONVW], raw[:, h, 0:CONVW], tap[:, 0:1],
                                          tap[:, W_A:W_A + 1], ALU.mult, ALU.add).then_inc(tapped[h], 1)
                        for j in range(1, W_A):
                            dve.wait_ge(tapped[h], i * (W_A - 1) + j)
                            op = dve.scalar_tensor_tensor(y[:, h, 0:CONVW], raw[:, h, j:j + CONVW], tap[:, j:j + 1],
                                                          y[:, h, 0:CONVW], ALU.mult, ALU.add)
                            op.then_inc(tapped[h] if j < W_A - 1 else conv_done[h], 1)
                dve.wait_ge(silu_done[0], NCONV // 2 + 1)
                dve.wait_ge(tail_done[1], NCONV // 2 + 1)
                with dve.Fori(0, NPAIR) as i:
                    for c in range(2):
                        at_c, at_b = (1 + 3 * c) // 2, (2 + 3 * c) // 2
                        half_c, half_b = (1 + 3 * c) % 2, (2 + 3 * c) % 2
                        dve.wait_ge(proj_done[half_c], i * 3 + ((NCONV + NZ) // 2 + 1 + at_c))
                        dve.wait_ge(h_done, i * 2 + (1 + c))
                        dve.wait_ge(ctail_done, i * 2 + (1 + c))
                        put_raw(lambda o, s, t: dve.tensor_tensor(o, raw[:, 0, t[0]:t[1]] if t[1] <= TP else
                                                                  raw[:, 0, TP:T].rearrange("p (b t) -> p b t", t=LSEQ),
                                                                  s, ALU.mult),
                                raw[:, 1], ps[:, half_c], HISTC).then_inc(craw_done, 1)
                        dve.wait_ge(craw_done, i * 2 + (2 + c))
                        dve.sem_inc(ps_free[half_c], 1)
                        dve.wait_ge(chist_done, i * 2 + (2 + c))
                        tap = taps_c[:, bass.ds(i * 2 + c, 1), :].rearrange("p a t -> p (a t)")
                        dve.tensor_scalar(y[:, 0, 0:CONVWC], raw[:, 1, 0:CONVWC], tap[:, 0:1], None,
                                          ALU.mult).then_inc(ctapped, 1)
                        for j in range(1, W_C):
                            dve.wait_ge(ctapped, i * (2 * W_C) + (c * W_C + j))
                            dve.scalar_tensor_tensor(y[:, 0, 0:CONVWC], raw[:, 1, j:j + CONVWC], tap[:, j:j + 1],
                                                     y[:, 0, 0:CONVWC], ALU.mult, ALU.add).then_inc(ctapped, 1)
                        dve.wait_ge(ctapped, i * (2 * W_C) + (c * W_C + W_C))
                        dve.wait_ge(proj_done[half_b], i * 3 + ((NCONV + NZ) // 2 + 1 + at_b))
                        dve.wait_ge(out_free[c], i + (NZ // 2 + 1))
                        dve.tensor_tensor(out[:, c, 0:2 * TW].rearrange("p (n t) -> p n t", n=2),
                                          y[:, 0, 0:2 * TW].rearrange("p (n t) -> p n t", n=2),
                                          ps[:, half_b, 0:2, 0:TW], ALU.mult)
                        dve.tensor_tensor(out[:, c, 2 * TW:TP], y[:, 0, 2 * TW:TP], ps[:, half_b, 2, 0:TAIL], ALU.mult)
                        dve.tensor_tensor(out[:, c, TP:T].rearrange("p (b t) -> p b t", t=LSEQ),
                                          samples(y[:, 0], TP, HISTC + LSEQ, HISTC, HISTC + LSEQ),
                                          ps[:, half_b, 2, TAIL:TW].rearrange("p (b t) -> p b t", t=LSEQ),
                                          ALU.mult).then_inc(yc_done, 1)
                        dve.wait_ge(yc_done, i * 2 + (2 + c))
                        dve.sem_inc(ps_free[half_b], 1)


class Steps:

    def __init__(self, m, name, names):
        self.sem, self.names, self.n = m.sem(name), names, len(names)

    def start(self, eng):
        eng.sem_inc(self.sem, self.n)

    def at(self, r, name, back=0):
        return r * self.n + (self.n * (1 - back) + self.names.index(name) + 1)


def bc(col, n):
    return col.unsqueeze(2).to_broadcast([col.shape[0], col.shape[1], n])


def qk_norm_phase(nc, act_out, ones):
    with ExitStack() as stack:
        m = Memory(nc, stack)
        sq = m.sb("n_sq", [P, T])
        r = m.sb("n_r", [P, T])
        ps = m.ps("n_ps", [P, NT, 512])
        a = Steps(m, "n_act", ["square", "root"])
        p = Steps(m, "n_pe", ["sum"])
        v = Steps(m, "n_dve", ["sum", "inverse", "scaled"])
        block = stack.enter_context(nc.Block())

        @block.scalar
        def _(act):
            a.start(act)
            with act.Fori(0, 2 * HA) as b:
                act.wait_ge(p.sem, p.at(b, "sum", 1))
                act.activation(sq[:], one(act_out, b), ACT.Square).then_inc(a.sem, 1)
                act.wait_ge(v.sem, v.at(b, "sum"))
                act.activation(r[:], r[:], ACT.Sqrt).then_inc(a.sem, 1)

        @block.tensor
        def _(pe):
            p.start(pe)
            with pe.Fori(0, 2 * HA) as b:
                pe.wait_ge(a.sem, a.at(b, "square"))
                pe.wait_ge(v.sem, v.at(b, "sum", 1))
                for n in range(NT):
                    mm = pe.matmul(ps[:, n, 0:TW], ones[:], sq[:, n * TW:(n + 1) * TW], start=True, stop=True)
                mm.then_inc(p.sem, 1)

        @block.vector
        def _(dve):
            v.start(dve)
            for part, scale in ((0, DK ** -0.5), (1, 1.0)):
                with dve.Fori(part * HA, (part + 1) * HA) as b:
                    dve.wait_ge(p.sem, p.at(b, "sum"))
                    dve.wait_ge(v.sem, v.at(b, "scaled", 1))
                    dve.tensor_scalar(r[:].rearrange("p (n t) -> p n t", n=NT), ps[:, :, 0:TW], EPS, None,
                                      ALU.add).then_inc(v.sem, 1)
                    dve.wait_ge(a.sem, a.at(b, "root"))
                    dve.reciprocal(r[:], r[:]).then_inc(v.sem, 1)
                    dve.wait_ge(v.sem, v.at(b, "inverse"))
                    x = one(act_out, b)
                    dve.scalar_tensor_tensor(x, x, scale, r[:], ALU.mult, ALU.mult).then_inc(v.sem, 1)


GDN_PE = ["rows", "k", "v", "kk", "qk", "mt", "m2", "m2t", "m4", "m4t", "r1", "m8", "r2", "r3",
          "td", "y", "yt", "y2", "y2t", "y4", "z1", "z2", "tt", "u", "wk", "w", "o", "ds"]
GDN_DVE = ["diff_t", "masked_t", "diff", "masked", "kb", "kbg", "kd", "vb", "qkt", "qg",
           "mk", "m", "m16", "lm", "r0", "m2t", "m4t", "r1", "r2", "r3", "yt", "vv", "y2t", "z1", "z2", "u", "w",
           "s_decayed", "s"]
GDN_ACT = ["rows_st", "cols", "ecol", "ercol", "eb", "dec_t", "dec", "mt", "m2", "m4", "m8", "td", "y", "y2", "y4", "tt",
           "wk", "o"]
GDN_POOL = ["k_st", "v_st"]
SAMPLE_ONLY_OUT = {"m8", "r3", "td", "y", "yt", "y2", "y2t", "y4", "z1", "z2", "tt", "vv", "lm", "m4t", "m16"}


def gdn_phase(nc, io, act_out, rows, g_dram, masks, sampled):
    L = TS if sampled else CH
    rounds = 1 if sampled else NCH
    tag = "ds" if sampled else "dp"
    with ExitStack() as stack:
        m = Memory(nc, stack)
        out = SAMPLE_ONLY_OUT if sampled else set()
        names_p = [x for x in GDN_PE if x not in out]
        names_v = [x for x in GDN_DVE if x not in out]
        names_a = [x for x in GDN_ACT if x not in out]
        if sampled:
            names_p = names_p[:names_p.index("w")] + ["w_state", "w_turned", "o", "o_state"] + [
                f"ds{h}" for h in range(HA)]
            names_v = names_v[:names_v.index("w")] + ["w", "o"] + [
                f"{x}{h}" for h in range(HA) for x in ("spread", "decayed", "s")]
            names_a = names_a[:-1] + ["w_state", "o_state"]
        p, v, a = Steps(m, tag + "_pe", names_p), Steps(m, tag + "_dve", names_v), Steps(m, tag + "_act", names_a)
        q = Steps(m, tag + "_pool", GDN_POOL)
        gb_loaded, state_loaded, state_out = m.sem(tag + "_gb"), m.sem(tag + "_state"), m.sem(tag + "_out")

        def sb(name, shape):
            return m.sb(f"{tag}_{name}", shape)

        heads = [L, HA, L]
        kst, vst = sb("kst", [P, HA, L]), sb("vst", [P, HA, L])
        rst = sb("rst", [P, 3, L])
        gb, eb = sb("gb", [P, HA, L]), sb("eb", [P, HA, L])
        cols, ecol, ercol, kb = sb("cols", [L, 3, 64]), sb("ecol", [L, NR]), sb("ercol", [L, NR]), sb("kb", [L, HA])
        diff_t, diff = sb("difft", heads), sb("diff", heads)
        kbg, kd, vb = sb("kbg", [L, HA, DK]), sb("kd", [L, HA, DK]), sb("vb", [L, HA, DK])
        qkt, qg = sb("qkt", heads), sb("qg", [P, HA, L])
        M = sb("m", heads)
        M16 = M if sampled else sb("m16", heads)
        mt, r0, r1, r2 = sb("mt", heads), sb("r0", heads), sb("r1", heads), sb("r2", heads)
        m2, m2t, m4 = sb("m2", heads), sb("m2t", heads), sb("m4", heads)
        if not sampled:
            lm, m4t, m8, r3, td = sb("lm", heads), sb("m4t", heads), sb("m8", heads), sb("r3", heads), sb("td", heads)
            y, yt, vv, y2, y2t = sb("y", heads), sb("yt", heads), sb("vv", heads), sb("y2", heads), sb("y2t", heads)
            y4, z1, z2, tt = sb("y4", heads), sb("z1", heads), sb("z2", heads), sb("tt", heads)
            S = sb("s", [P, HA, DK])
            S1 = sb("s1", [P, HA, DK])
        else:
            tt = r2
            S = sb("s", [P, NSEQ, HA, DK])
            S1 = sb("s1", [P, 2, NSEQ, DK])
            wst, ost = sb("wst", [P, HA, L]), sb("ost", [P, HA, L])
            spread = sb("spread", [L, 2, NSEQ, DK])
        U, wk, w = sb("u", [L, HA, DK]), sb("wk", [P, HA, L]), sb("w", [L, HA, DK])
        bank = [m.ps(f"{tag}_ps{i}", [P, 512]) for i in range(8)]

        def sq_(i):
            return bank[i][0:L, 0:HA * L].rearrange("p (h t) -> p h t", h=HA)

        def wide(i):
            return bank[i][0:L, :].rearrange("p (h t) -> p h t", h=HA)

        def tall(i):
            return bank[i][:, 0:HA * L].rearrange("p (h t) -> p h t", h=HA)

        ident = masks[0:L, 0, 0:L]
        neg_t, neg = (masks[0:L, 4, 0:L], masks[0:L, 5, 0:L]) if sampled else (masks[0:L, 1, 0:L], masks[0:L, 2, 0:L])
        same16 = masks[0:L, 3, 0:L]
        col_g, col_b = cols[:, 0, ROW_G:ROW_G + HA], cols[:, 0, 0:HA]

        def over_heads(mask):
            return mask.unsqueeze(1).to_broadcast(heads)

        def tokens(ap, c):
            return ap[:, :, TP:T] if sampled else ap[:, :, bass.ds(c * CH, CH)]

        def loop(eng):
            return eng.Fori(0, NCH)

        block = stack.enter_context(nc.Block())

        @block.sync
        def _(sp):
            if sampled:
                sp.dma_start(S[:], io["state_gdn"]).then_inc(state_loaded, 16)
                sp.dma_start(gb[:], g_dram[0:HA, TP:T].partition_broadcast(P)).then_inc(gb_loaded, 16)
                sp.wait_ge(v.sem, v.at(0, f"s{HA - 1}"))
                sp.dma_start(io["new_gdn_s"], S[:]).then_inc(state_out, 16)
            else:
                with loop(sp) as c:
                    sp.wait_ge(v.sem, v.at(c, "diff", 1))
                    sp.wait_ge(a.sem, a.at(c, "eb", 1))
                    sp.dma_start(gb[:], g_dram[0:HA, bass.ds(c * CH, CH)].partition_broadcast(P)
                                 ).then_inc(gb_loaded, 16)
                sp.wait_ge(v.sem, v.at(NCH - 1, "s"))
                sp.dma_start(io["new_gdn_p"], S[:]).then_inc(state_out, 16)
            sp.wait_ge(state_out, 16)

        @block.gpsimd
        def _(pool):
            q.start(pool)

            def chunk(c):
                pool.wait_ge(p.sem, p.at(c, "qk", 1))
                pool.tensor_copy(kst[:], tokens(act_out[:, HA:2 * HA], c)).then_inc(q.sem, 1)
                pool.tensor_copy(vst[:], tokens(act_out[:, 2 * HA:3 * HA], c)).then_inc(q.sem, 1)

            if sampled:
                chunk(0)
            else:
                with loop(pool) as c:
                    chunk(c)

        @block.scalar
        def _(act):
            a.start(act)

            def wait(steps, c, name, back=0):
                act.wait_ge(steps.sem, steps.at(c, name, back))

            def copy(dst, src):
                act.copy(dst, src).then_inc(a.sem, 1)

            def exp(dst, src):
                act.activation(dst, src, ACT.Exp).then_inc(a.sem, 1)

            def chunk(c):
                wait(p, c, "rows", 1)
                for i, row in enumerate(rows):
                    src = row[:, TP:T] if sampled else row[:, bass.ds(c * CH, CH)]
                    ins = act.copy(rst[:, i, :], src)
                ins.then_inc(a.sem, 1)
                wait(p, c, "rows")
                wait(v, c, "m", 1)
                copy(cols[:], bank[0][0:L, 0:3 * P].rearrange("p (r c) -> p r c", r=3)[:, :, 0:64])
                wait(a, c, "cols")
                exp(ecol[:], cols[:, 0, ROW_G:ROW_G + NR])
                exp(ercol[:], cols[:, 1, ROW_G:ROW_G + NR])
                act.wait_ge(gb_loaded, c * 16 + 16)
                if not sampled:
                    wait(v, c, "s_decayed", 1)
                exp(eb[:], gb[:])
                wait(v, c, "masked_t")
                exp(diff_t[:], diff_t[:])
                wait(v, c, "masked")
                exp(diff[:], diff[:])
                wait(p, c, "mt")
                copy(mt[:], sq_(5))
                wait(p, c, "m2")
                copy(m2[:], sq_(6))
                wait(p, c, "m4")
                copy(m4[:], sq_(6))
                if not sampled:
                    wait(p, c, "m8")
                    copy(m8[:], sq_(6))
                    wait(p, c, "td")
                    copy(td[:], sq_(6))
                    wait(p, c, "y")
                    copy(y[:], sq_(7))
                    wait(p, c, "y2")
                    copy(y2[:], sq_(6))
                    wait(p, c, "y4")
                    copy(y4[:], sq_(6))
                    wait(p, c, "tt")
                    copy(tt[:], sq_(6))
                wait(p, c, "wk")
                act.mul(wk[:], tall(7), -1.0).then_inc(a.sem, 1)
                if not sampled:
                    wait(p, c, "o")
                    copy(tokens(act_out[:, 0:HA], c), tall(1))
                else:
                    wait(p, c, "w_state")
                    copy(wst[:], tall(0))
                    wait(p, c, "o_state")
                    copy(ost[:], tall(4))

            if sampled:
                chunk(0)
            else:
                with loop(act) as c:
                    chunk(c)

        @block.vector
        def _(dve):
            v.start(dve)
            if not sampled:
                dve.memset(S[:], 0.0).then_inc(state_loaded, 16)

            def wait(steps, c, name, back=0):
                dve.wait_ge(steps.sem, steps.at(c, name, back))

            def tt_(dst, x, z, op):
                dve.tensor_tensor(dst, x, z, op).then_inc(v.sem, 1)

            def chunk(c):
                dve.wait_ge(gb_loaded, c * 16 + 16)
                wait(a, c, "cols")
                wait(v, c, "qkt", 1)
                g = bc(col_g, L)
                tt_(diff_t[:], gb[0:L], g, ALU.subtract)
                wait(v, c, "diff_t")
                tt_(diff_t[:], diff_t[:], over_heads(neg_t), ALU.add)
                tt_(diff[:], g, gb[0:L], ALU.subtract)
                wait(v, c, "diff")
                tt_(diff[:], diff[:], over_heads(neg), ALU.add)
                wait(a, c, "ecol")
                tt_(kb[:], col_b, ecol[:, 0:HA], ALU.mult)
                wait(v, c, "kb")
                wait(p, c, "k")
                tt_(kbg[:], wide(1), bc(kb[:], DK), ALU.mult)
                wait(a, c, "ercol")
                tt_(kd[:], wide(1), bc(ercol[:, 0:HA], DK), ALU.mult)
                wait(p, c, "v")
                tt_(vb[:], wide(2), bc(col_b, DK), ALU.mult)
                wait(a, c, "dec_t")
                wait(p, c, "qk")
                tt_(qkt[:], sq_(4), diff_t[:], ALU.mult)
                wait(a, c, "eb")
                tt_(qg[:], tokens(act_out[:, 0:HA], c), eb[:], ALU.mult)
                wait(a, c, "dec")
                wait(p, c, "kk")
                dve.scalar_tensor_tensor(M[:], sq_(3), -1.0, diff[:], ALU.mult, ALU.mult).then_inc(v.sem, 1)
                wait(v, c, "mk")
                tt_(M[:], M[:], bc(col_b, L), ALU.mult)
                wait(v, c, "m")
                if not sampled:
                    tt_(M16[:], M[:], over_heads(same16), ALU.mult)
                    wait(v, c, "m16")
                    tt_(lm[:], M[:], M16[:], ALU.subtract)
                wait(a, c, "mt")
                tt_(r0[:], mt[:], over_heads(ident), ALU.add)
                wait(p, c, "m2t")
                dve.tensor_copy(m2t[:], sq_(7)).then_inc(v.sem, 1)
                if not sampled:
                    wait(p, c, "m4t")
                    dve.tensor_copy(m4t[:], sq_(7)).then_inc(v.sem, 1)
                wait(p, c, "r1")
                tt_(r1[:], sq_(5), r0[:], ALU.add)
                wait(v, c, "r1")
                wait(p, c, "r2")
                tt_(r2[:], sq_(7), r1[:], ALU.add)
                if not sampled:
                    wait(v, c, "r2")
                    wait(p, c, "r3")
                    tt_(r3[:], sq_(5), r2[:], ALU.add)
                    wait(p, c, "yt")
                    dve.tensor_copy(yt[:], sq_(5)).then_inc(v.sem, 1)
                    tt_(vv[:], sq_(5), over_heads(ident), ALU.add)
                    wait(p, c, "y2t")
                    dve.tensor_copy(y2t[:], sq_(7)).then_inc(v.sem, 1)
                    wait(p, c, "z1")
                    tt_(z1[:], sq_(5), vv[:], ALU.add)
                    wait(v, c, "z1")
                    wait(p, c, "z2")
                    tt_(z2[:], sq_(7), z1[:], ALU.add)
                wait(p, c, "u")
                dve.tensor_copy(U[:], wide(5)).then_inc(v.sem, 1)
                wait(v, c, "u")
                if not sampled:
                    wait(p, c, "w")
                    tt_(w[:], wide(0), U[:], ALU.add)
                    wait(p, c, "o")
                    tt_(S1[:], S[:], eb[:, :, L - 1:L].to_broadcast([P, HA, DK]), ALU.mult)
                    wait(v, c, "s_decayed")
                    wait(p, c, "ds")
                    tt_(S[:], bank[3][:].rearrange("p (h t) -> p h t", h=HA), S1[:], ALU.add)
                else:
                    wait(p, c, "w_turned")
                    tt_(w[:], wide(1), U[:], ALU.add)
                    wait(a, c, "o_state")
                    wait(p, c, "o")
                    tt_(act_out[:, 0:HA, TP:T], tall(2), ost[:], ALU.add)
                    wait(v, c, "w")
                    for h in range(HA):
                        seq = masks[0:TS, 6, 0:NSEQ].unsqueeze(2).to_broadcast([TS, NSEQ, DK])
                        if h >= 2:
                            wait(p, c, f"ds{h - 2}")
                        tt_(spread[:, h % 2], w[:, h, :].unsqueeze(1).to_broadcast([TS, NSEQ, DK]), seq, ALU.mult)
                        if h >= 2:
                            wait(v, c, f"s{h - 2}")
                        last = eb[:, h, :].rearrange("p (b t) -> p b t", t=LSEQ)[:, :, LSEQ - 1:LSEQ]
                        tt_(S1[:, h % 2], S[:, :, h, :], last.to_broadcast([P, NSEQ, DK]), ALU.mult)
                        wait(v, c, f"decayed{h}")
                        wait(p, c, f"ds{h}")
                        for half in range(2):
                            ins = dve.tensor_tensor(
                                S[:, 4 * half:4 * half + 4, h, :],
                                bank[(h % 2) * 2 + 4 + half][:].rearrange("p (b t) -> p b t", t=DK),
                                S1[:, h % 2, 4 * half:4 * half + 4], ALU.add)
                        ins.then_inc(v.sem, 1)

            if sampled:
                dve.wait_ge(state_loaded, 16)
                chunk(0)
            else:
                dve.wait_ge(state_loaded, 16)
                with loop(dve) as c:
                    chunk(c)

        @block.tensor
        def _(pe):
            p.start(pe)

            def wait(steps, c, name, back=0):
                pe.wait_ge(steps.sem, steps.at(c, name, back))

            def each(dst, lhs, rhs):
                for h in range(HA):
                    mm = pe.matmul(dst[:, h, :], lhs(h), rhs(h), start=True, stop=True)
                mm.then_inc(p.sem, 1)

            def prod(dst, lhs, rhs):
                each(dst, lambda h: lhs[:, h, :], lambda h: rhs[:, h, :])

            def turn(dst, src, ident_):
                for h in range(HA):
                    mm = pe.transpose(dst[:, h, :], src[:, h, :], ident_)
                mm.then_inc(p.sem, 1)

            def chunk(c):
                full = masks[:, 0, :]
                wait(a, c, "rows_st")
                for i in range(3):
                    mm = pe.transpose(bank[0][0:L, i * P:(i + 1) * P], rst[:, i, :], full)
                mm.then_inc(p.sem, 1)
                wait(q, c, "k_st")
                wait(v, c, "kd", 1)
                wait(a, c, "o" if not sampled else "o_state", 1)
                turn(wide(1), kst, full)
                wait(q, c, "v_st")
                turn(wide(2), vst, full)
                wait(v, c, "s" if not sampled else f"s{HA - 1}", 1)
                prod(sq_(3), kst, kst)
                each(sq_(4), lambda h: kst[:, h, :],
                     lambda h: act_out[:, h, TP:T] if sampled else act_out[:, h, bass.ds(c * CH, CH)])
                wait(v, c, "m" if sampled else "m16")
                turn(sq_(5), M16, ident)
                wait(a, c, "mt")
                prod(sq_(6), mt, M16)
                prod(sq_(7), M16, mt)
                wait(a, c, "m2")
                wait(v, c, "m2t")
                prod(sq_(6), m2t, m2)
                if not sampled:
                    prod(sq_(7), m2, m2t)
                wait(v, c, "r0")
                prod(sq_(5), m2, r0)
                wait(a, c, "m4")
                if not sampled:
                    wait(v, c, "m4t")
                    prod(sq_(6), m4t, m4)
                wait(v, c, "r1")
                prod(sq_(7), m4, r1)
                if not sampled:
                    wait(a, c, "m8")
                    wait(v, c, "r2")
                    prod(sq_(5), m8, r2)
                    wait(v, c, "r3")
                    turn(sq_(6), r3, ident)
                    wait(v, c, "lm")
                    prod(sq_(7), r3, lm)
                    prod(sq_(5), lm, r3)
                    wait(a, c, "y")
                    wait(v, c, "vv")
                    wait(a, c, "td")
                    prod(sq_(6), yt, y)
                    prod(sq_(7), y, yt)
                    wait(a, c, "y2")
                    wait(v, c, "y2t")
                    prod(sq_(6), y2t, y2)
                    prod(sq_(5), y2, vv)
                    wait(a, c, "y4")
                    wait(v, c, "z1")
                    prod(sq_(7), y4, z1)
                    wait(v, c, "z2")
                    prod(sq_(6), td, z2)
                    wait(a, c, "tt")
                else:
                    wait(v, c, "r2")
                wait(v, c, "vb")
                prod(wide(5), tt, vb)
                wait(v, c, "kbg")
                prod(tall(7), kbg, tt)
                if not sampled:
                    pe.wait_ge(state_loaded, 16)
                    wait(a, c, "wk")
                    wait(v, c, "s", 1)
                    prod(wide(0), wk, S)
                    wait(v, c, "w")
                    wait(v, c, "qg")
                    for h in range(HA):
                        pe.matmul(tall(1)[:, h, :], S[:, h, :], qg[:, h, :], start=True, stop=False)
                        mm = pe.matmul(tall(1)[:, h, :], w[:, h, :], qkt[:, h, :], start=False, stop=True)
                    mm.then_inc(p.sem, 1)
                    prod(bank[3][:].rearrange("p (h t) -> p h t", h=HA), kd, w)
                else:
                    wait(a, c, "wk")
                    for dst, src in ((0, wk), (4, qg)):
                        if dst == 4:
                            wait(a, c, "w_state")
                            turn(wide(1), wst, full)
                            wait(v, c, "w")
                            prod(tall(2), w, qkt)
                        for h in range(HA):
                            for b in range(NSEQ):
                                cut = slice(b * LSEQ, (b + 1) * LSEQ)
                                mm = pe.matmul(tall(dst)[:, h, cut], S[:, b, h, :], src[:, h, cut],
                                               start=True, stop=True)
                        mm.then_inc(p.sem, 1)
                    wait(a, c, "o_state")
                    for h in range(HA):
                        wait(v, c, f"spread{h}")
                        if h >= 2:
                            wait(v, c, f"s{h - 2}")
                        for half in range(2):
                            mm = pe.matmul(bank[(h % 2) * 2 + 4 + half][:], kd[:, h, :],
                                           spread[:, h % 2, 4 * half:4 * half + 4, :].rearrange("p b t -> p (b t)"),
                                           start=True, stop=True)
                        mm.then_inc(p.sem, 1)

            if sampled:
                pe.wait_ge(state_loaded, 16)
                chunk(0)
            else:
                with loop(pe) as c:
                    chunk(c)


SSD_PE = ["rows", "bt", "xt", "cb", "y", "ds"]
SSD_DVE = ["diff_t", "masked_t", "xdt", "xdd", "cbt", "cs", "y", "s_decayed", "s"]
SSD_ACT = ["rows_st", "cols", "ercol", "bt", "eb", "dec_t"]
SSD_POOL = ["b_st", "x_st"]
AT_X, AT_B, AT_C = 3 * HA, 3 * HA + 4, 3 * HA + 6


def ssd_phase(nc, io, act_out, rows, g_dram, masks, sampled):
    L = TS if sampled else CH
    tag = "ss" if sampled else "sp"
    HPG = HB // GB
    W = HPG * PB
    with ExitStack() as stack:
        m = Memory(nc, stack)
        names_p, names_v, names_a = list(SSD_PE), list(SSD_DVE), list(SSD_ACT)
        if sampled:
            names_p = ["rows", "bt", "xt", "cb", "y", "y_state", "ds0", "ds1"]
            names_v = ["diff_t", "masked_t", "xdt", "xdd", "cbt", "cs", "spread", "y_skip", "y", "s_decayed", "s0", "s1"]
            names_a = names_a + ["y_state"]
        p, v, a = Steps(m, tag + "_pe", names_p), Steps(m, tag + "_dve", names_v), Steps(m, tag + "_act", names_a)
        q = Steps(m, tag + "_pool", SSD_POOL)
        gb_loaded, state_loaded, state_out = m.sem(tag + "_gb"), m.sem(tag + "_state"), m.sem(tag + "_out")
        const_loaded = m.sem(tag + "_const")

        def sb(name, shape):
            return m.sb(f"{tag}_{name}", shape)

        bst, xst, rst = sb("bst", [P, GB, L]), sb("xst", [P, 4, L]), sb("rst", [P, 3, L])
        gb, eb, cs = sb("gb", [P, HB, L]), sb("eb", [P, HB, L]), sb("cs", [P, HB, L])
        cols, ercol = sb("cols", [L, 3, 64]), sb("ercol", [L, NR])
        diff_t, cbt = sb("difft", [L, HB, L]), sb("cbt", [L, HB, L])
        bt, xdt, xdd = sb("bt", [L, GB, NB]), sb("xdt", [L, HB, PB]), sb("xdd", [L, HB, PB])
        skip = sb("skip", [P, 4])
        if sampled:
            S, S1 = sb("s", [P, NSEQ, HB, PB]), sb("s1", [P, NSEQ, HB, PB])
            spread, yst = sb("spread", [L, NSEQ, HB * PB]), sb("yst", [P, 4, L])
        else:
            S, S1 = sb("s", [P, HB, PB]), sb("s1", [P, HB, PB])
        bank = [m.ps(f"{tag}_ps{i}", [P, 512]) for i in range(8)]
        full, neg_t = masks[:, 0, :], masks[0:L, 4 if sampled else 1, 0:L]
        xt_ps = bank[2][0:L, :].rearrange("p (h t) -> p h t", t=PB)
        cb_ps = bank[3][0:L, 0:GB * L].rearrange("p (g t) -> p g t", g=GB)
        y_ps = bank[4][:, 0:4 * L].rearrange("p (n t) -> p n t", n=4)
        y_state_ps = bank[5][:, 0:4 * L].rearrange("p (n t) -> p n t", n=4)

        def tokens(ap, c):
            return ap[:, :, TP:T] if sampled else ap[:, :, bass.ds(c * CH, CH)]

        def run(eng, chunk):
            if sampled:
                chunk(0)
            else:
                with eng.Fori(0, NCH) as c:
                    chunk(c)

        block = stack.enter_context(nc.Block())

        @block.sync
        def _(sp):
            sp.dma_start(skip[:], io["d_skip"]).then_inc(const_loaded, 16)
            if sampled:
                sp.dma_start(S[:], io["state_ssd"]).then_inc(state_loaded, 16)
                sp.dma_start(gb[:], g_dram[HA:NR, TP:T].partition_broadcast(P)).then_inc(gb_loaded, 16)
                sp.wait_ge(v.sem, v.at(0, "s1"))
                sp.dma_start(io["new_ssd_s"], S[:]).then_inc(state_out, 16)
            else:
                with sp.Fori(0, NCH) as c:
                    sp.wait_ge(v.sem, v.at(c, "diff_t", 1))
                    sp.wait_ge(a.sem, a.at(c, "eb", 1))
                    sp.dma_start(gb[:], g_dram[HA:NR, bass.ds(c * CH, CH)].partition_broadcast(P)
                                 ).then_inc(gb_loaded, 16)
                sp.wait_ge(v.sem, v.at(NCH - 1, "s"))
                sp.dma_start(io["new_ssd_p"], S[:]).then_inc(state_out, 16)
            sp.wait_ge(state_out, 16)

        @block.gpsimd
        def _(pool):
            q.start(pool)

            def chunk(c):
                pool.wait_ge(p.sem, p.at(c, "cb", 1))
                pool.tensor_copy(bst[:], tokens(act_out[:, AT_B:AT_B + GB], c)).then_inc(q.sem, 1)
                pool.tensor_copy(xst[:], tokens(act_out[:, AT_X:AT_X + 4], c)).then_inc(q.sem, 1)

            run(pool, chunk)

        @block.scalar
        def _(act):
            a.start(act)

            def wait(steps, c, name, back=0):
                act.wait_ge(steps.sem, steps.at(c, name, back))

            def chunk(c):
                wait(p, c, "rows", 1)
                for i, row in enumerate(rows):
                    src = row[:, TP:T] if sampled else row[:, bass.ds(c * CH, CH)]
                    ins = act.copy(rst[:, i, :], src)
                ins.then_inc(a.sem, 1)
                wait(p, c, "rows")
                wait(v, c, "xdd", 1)
                act.copy(cols[:], bank[0][0:L, 0:3 * P].rearrange("p (r c) -> p r c", r=3)[:, :, 0:64]).then_inc(a.sem, 1)
                wait(a, c, "cols")
                act.activation(ercol[:], cols[:, 1, ROW_G:ROW_G + NR], ACT.Exp).then_inc(a.sem, 1)
                wait(p, c, "bt")
                act.copy(bt[:], bank[1][0:L, 0:GB * NB].rearrange("p (g s) -> p g s", g=GB)).then_inc(a.sem, 1)
                act.wait_ge(gb_loaded, c * 16 + 16)
                if not sampled:
                    wait(v, c, "s_decayed", 1)
                act.activation(eb[:], gb[:], ACT.Exp).then_inc(a.sem, 1)
                wait(v, c, "masked_t")
                act.activation(diff_t[:], diff_t[:], ACT.Exp).then_inc(a.sem, 1)
                if sampled:
                    wait(p, c, "y_state")
                    act.copy(yst[:], y_state_ps).then_inc(a.sem, 1)

            run(act, chunk)

        @block.vector
        def _(dve):
            v.start(dve)

            def wait(steps, c, name, back=0):
                dve.wait_ge(steps.sem, steps.at(c, name, back))

            def tt_(dst, x, z, op):
                dve.tensor_tensor(dst, x, z, op).then_inc(v.sem, 1)

            def chunk(c):
                dve.wait_ge(gb_loaded, c * 16 + 16)
                wait(a, c, "cols")
                wait(v, c, "cbt", 1)
                tt_(diff_t[:], gb[0:L], bc(cols[:, 0, ROW_G + HA:ROW_G + NR], L), ALU.subtract)
                wait(v, c, "diff_t")
                tt_(diff_t[:], diff_t[:], neg_t.unsqueeze(1).to_broadcast([L, HB, L]), ALU.add)
                wait(p, c, "xt")
                tt_(xdt[:], xt_ps, bc(cols[:, 2, ROW_G + HA:ROW_G + NR], PB), ALU.mult)
                wait(v, c, "xdt")
                wait(a, c, "ercol")
                tt_(xdd[:], xdt[:], bc(ercol[:, HA:NR], PB), ALU.mult)
                wait(p, c, "cb")
                wait(a, c, "dec_t")
                for g in range(GB):
                    ins = dve.tensor_tensor(cbt[:, g * HPG:(g + 1) * HPG, :],
                                            cb_ps[:, g:g + 1, :].to_broadcast([L, HPG, L]),
                                            diff_t[:, g * HPG:(g + 1) * HPG, :], ALU.mult)
                ins.then_inc(v.sem, 1)
                wait(a, c, "eb")
                for g in range(GB):
                    cg = tokens(act_out[:, AT_C + g:AT_C + g + 1], c)
                    ins = dve.tensor_tensor(cs[:, g * HPG:(g + 1) * HPG, :], cg.to_broadcast([P, HPG, L]),
                                            eb[:, g * HPG:(g + 1) * HPG, :], ALU.mult)
                ins.then_inc(v.sem, 1)
                if sampled:
                    wait(v, c, "xdd")
                    seq = masks[0:TS, 6, 0:NSEQ].unsqueeze(2).to_broadcast([TS, NSEQ, HB * PB])
                    flat = xdd[:].rearrange("p h t -> p (h t)").unsqueeze(1).to_broadcast([TS, NSEQ, HB * PB])
                    tt_(spread[:], flat, seq, ALU.mult)
                wait(p, c, "y")
                for n in range(4):
                    x = tokens(act_out[:, AT_X + n:AT_X + n + 1], c)
                    ins = dve.scalar_tensor_tensor(x, x, skip[:, n:n + 1], y_ps[:, n:n + 1, :], ALU.mult, ALU.add)
                ins.then_inc(v.sem, 1)
                if sampled:
                    wait(a, c, "y_state")
                    wait(v, c, "y_skip")
                    x = act_out[:, AT_X:AT_X + 4, TP:T]
                    tt_(x, x, yst[:], ALU.add)
                    last = eb[:].rearrange("p h (b t) -> p b h t", t=LSEQ)[:, :, :, LSEQ - 1:LSEQ]
                    tt_(S1[:], S[:], last.to_broadcast([P, NSEQ, HB, PB]), ALU.mult)
                    wait(v, c, "s_decayed")
                    for g in range(GB):
                        wait(p, c, f"ds{g}")
                        for j in range(4):
                            b = (4 * g + j) % 8
                            ins = dve.tensor_tensor(
                                S[:, 2 * j:2 * j + 2, g * HPG:(g + 1) * HPG, :],
                                bank[b][:].rearrange("p (b h t) -> p b h t", b=2, t=PB),
                                S1[:, 2 * j:2 * j + 2, g * HPG:(g + 1) * HPG, :], ALU.add)
                        ins.then_inc(v.sem, 1)
                else:
                    tt_(S1[:], S[:], eb[:, :, L - 1:L].to_broadcast([P, HB, PB]), ALU.mult)
                    wait(v, c, "s_decayed")
                    wait(p, c, "ds")
                    tt_(S[:], bank[5][:].rearrange("p (h t) -> p h t", t=PB), S1[:], ALU.add)

            dve.wait_ge(const_loaded, 16)
            if not sampled:
                dve.memset(S[:], 0.0).then_inc(state_loaded, 16)
            dve.wait_ge(state_loaded, 16)
            run(dve, chunk)

        @block.tensor
        def _(pe):
            p.start(pe)

            def wait(steps, c, name, back=0):
                pe.wait_ge(steps.sem, steps.at(c, name, back))

            def chunk(c):
                wait(a, c, "rows_st")
                wait(a, c, "cols", 1)
                for i in range(3):
                    mm = pe.transpose(bank[0][0:L, i * P:(i + 1) * P], rst[:, i, :], full)
                mm.then_inc(p.sem, 1)
                wait(q, c, "b_st")
                wait(a, c, "bt", 1)
                for g in range(GB):
                    mm = pe.transpose(bank[1][0:L, g * NB:(g + 1) * NB], bst[:, g, :], full)
                mm.then_inc(p.sem, 1)
                wait(q, c, "x_st")
                wait(v, c, "cbt", 1)
                for n in range(4):
                    mm = pe.transpose(bank[2][0:L, n * P:(n + 1) * P], xst[:, n, :], full)
                mm.then_inc(p.sem, 1)
                for g in range(GB):
                    cg = act_out[:, AT_C + g, TP:T] if sampled else act_out[:, AT_C + g, bass.ds(c * CH, CH)]
                    mm = pe.matmul(cb_ps[:, g, :], bst[:, g, :], cg, start=True, stop=True)
                mm.then_inc(p.sem, 1)
                wait(v, c, "cs")
                wait(v, c, "s" if not sampled else "s1", 1)
                for h in range(HB):
                    half = slice((h % 2) * PB, (h % 2 + 1) * PB)
                    mm = pe.matmul(y_ps[half, h // 2, :], xdt[:, h, :], cbt[:, h, :], start=True, stop=sampled)
                    if not sampled:
                        mm = pe.matmul(y_ps[half, h // 2, :], S[:, h, :], cs[:, h, :], start=False, stop=True)
                mm.then_inc(p.sem, 1)
                wait(a, c, "bt")
                if not sampled:
                    for g in range(GB):
                        mm = pe.matmul(bank[5][:, g * W:(g + 1) * W], bt[:, g, :],
                                       xdd[:, g * HPG:(g + 1) * HPG, :].rearrange("p h t -> p (h t)"),
                                       start=True, stop=True)
                    mm.then_inc(p.sem, 1)
                else:
                    for h in range(HB):
                        half = slice((h % 2) * PB, (h % 2 + 1) * PB)
                        for b in range(NSEQ):
                            cut = slice(b * LSEQ, (b + 1) * LSEQ)
                            mm = pe.matmul(y_state_ps[half, h // 2, cut], S[:, b, h, :], cs[:, h, cut],
                                           start=True, stop=True)
                    mm.then_inc(p.sem, 1)
                    wait(v, c, "spread")
                    wait(v, c, "y")
                    for g in range(GB):
                        for j in range(4):
                            mm = pe.matmul(bank[4 * g + j][:], bt[:, g, :],
                                           spread[:, 2 * j:2 * j + 2, g * W:(g + 1) * W], start=True, stop=True)
                        mm.then_inc(p.sem, 1)

            pe.wait_ge(state_loaded, 16)
            run(pe, chunk)


def gate_phase(nc, io, act_out, ones, z_dram, yc_dram):
    AT_ZA, AT_YC, AT_ZB = HA, 2 * HA, AT_B
    with ExitStack() as stack:
        m = Memory(nc, stack)
        ow, yw = m.sb("m_ow", [P, 1]), m.sb("m_yw", [P, 4])
        sq = m.sb("m_sq", [P, 2, T])
        r = m.sb("m_r", [P, T])
        ps = m.ps("m_ps", [P, NT, 512])
        loaded = m.sem("m_loaded")
        a, p = Steps(m, "m_act", ["square", "root"]), Steps(m, "m_pe", ["sum"])
        v = Steps(m, "m_dve", ["gated", "mean", "inverse", "weighted", "scaled"])
        block = stack.enter_context(nc.Block())
        tiled = r[:].rearrange("p (n t) -> p n t", n=NT)

        @block.sync
        def _(sp):
            sp.dma_start(ow[:], io["onorm_a"]).then_inc(loaded, 16)
            sp.dma_start(yw[:], io["onorm_b"]).then_inc(loaded, 16)
            sp.dma_start(act_out[:, AT_ZA:AT_ZA + 4, :], z_dram[0:4].rearrange("a p t -> p a t")).then_inc(loaded, 16)
            sp.dma_start(act_out[:, AT_ZB:AT_ZB + 4, :], z_dram[4:8].rearrange("a p t -> p a t")).then_inc(loaded, 16)
            sp.dma_start(act_out[:, AT_YC:AT_YC + 4, :], yc_dram.rearrange("a p t -> p a t")).then_inc(loaded, 16)
            sp.wait_ge(loaded, 80)

        def members(c):
            return [c] if c < HA else [AT_X + 2 * (c - HA), AT_X + 2 * (c - HA) + 1]

        @block.scalar
        def _(act):
            a.start(act)
            act.wait_ge(loaded, 80)
            for c in range(HA + GB):
                act.wait_ge(p.sem, p.at(c, "sum", 1))
                if c >= HA:
                    act.wait_ge(v.sem, v.at(c, "gated"))
                for j, b in enumerate(members(c)):
                    ins = act.activation(sq[:, j, :], act_out[:, b, :], ACT.Square)
                ins.then_inc(a.sem, 1)
                act.wait_ge(v.sem, v.at(c, "mean"))
                act.activation(r[:], r[:], ACT.Sqrt).then_inc(a.sem, 1)

        @block.tensor
        def _(pe):
            p.start(pe)
            for c in range(HA + GB):
                pe.wait_ge(a.sem, a.at(c, "square"))
                pe.wait_ge(v.sem, v.at(c, "mean", 1))
                n_in = len(members(c))
                for n in range(NT):
                    for j in range(n_in):
                        mm = pe.matmul(ps[:, n, 0:TW], ones[:], sq[:, j, n * TW:(n + 1) * TW],
                                       start=(j == 0), stop=(j == n_in - 1))
                mm.then_inc(p.sem, 1)

        @block.vector
        def _(dve):
            v.start(dve)
            dve.wait_ge(loaded, 80)
            for c in range(HA + GB):
                ms = members(c)
                if c >= HA:
                    for j, b in enumerate(ms):
                        ins = dve.tensor_tensor(act_out[:, b, :], act_out[:, b, :],
                                                act_out[:, AT_ZB + b - AT_X, :], ALU.mult)
                    ins.then_inc(v.sem, 1)
                else:
                    z = act_out[:, AT_ZA + c, :]
                    dve.tensor_scalar(z, z, ow[:, 0:1], None, ALU.mult).then_inc(v.sem, 1)
                dve.wait_ge(p.sem, p.at(c, "sum"))
                dve.wait_ge(v.sem, v.at(c, "scaled", 1))
                dve.tensor_scalar(tiled, ps[:, :, 0:TW], 1.0 / (P * len(ms)), EPS, ALU.mult, ALU.add).then_inc(v.sem, 1)
                dve.wait_ge(a.sem, a.at(c, "root"))
                dve.reciprocal(r[:], r[:]).then_inc(v.sem, 1)
                for j, b in enumerate(ms):
                    w = act_out[:, AT_ZA + c, :] if c < HA else yw[:, b - AT_X:b - AT_X + 1].to_broadcast([P, T])
                    ins = dve.tensor_tensor(act_out[:, b, :], act_out[:, b, :], w, ALU.mult)
                ins.then_inc(v.sem, 1)
                dve.wait_ge(v.sem, v.at(c, "weighted"))
                for b in ms:
                    ins = dve.tensor_tensor(act_out[:, b, :], act_out[:, b, :], r[:], ALU.mult)
                ins.then_inc(v.sem, 1)
        return list(range(HA)) + list(range(AT_X, AT_X + 4)) + list(range(AT_YC, AT_YC + 4))


def out_projection_phase(nc, io, act_out, mixed, x2):
    with ExitStack() as stack:
        m = Memory(nc, stack)
        w = m.sb("o_w", [P, 2, NMIX, P])
        ps = m.ps("o_ps", [P, 2, NT, 512])
        x_loaded = m.sem("o_x")
        w_loaded = [m.sem(f"o_w{h}") for h in range(2)]
        done = [m.sem(f"o_pe{h}") for h in range(2)]
        added = [m.sem(f"o_dve{h}") for h in range(2)]
        block = stack.enter_context(nc.Block())

        @block.sync
        def _(sp):
            sp.dma_start(w[:, 0], io["w_out"][0]).then_inc(w_loaded[0], 16)
            sp.dma_start(w[:, 1], io["w_out"][1]).then_inc(w_loaded[1], 16)
            sp.dma_start(x2[:], io["xT"]).then_inc(x_loaded, 16)
            with sp.Fori(0, KD // 2 - 1) as i:
                for h in range(2):
                    sp.wait_ge(done[h], i + 1)
                    sp.dma_start(w[:, h], io["w_out"][bass.ds(i * 2 + (2 + h), 1)].rearrange(
                        "a p k c -> (a p) k c")).then_inc(w_loaded[h], 16)

        @block.tensor
        def _(pe):
            with pe.Fori(0, KD // 2) as i:
                for h in range(2):
                    pe.wait_ge(w_loaded[h], i * 16 + 16)
                    pe.wait_ge(added[h], i + 1)
                    for n in range(NT):
                        for k in range(NMIX):
                            mm = pe.matmul(ps[:, h, n, 0:TW], w[:, h, k, :], act_out[:, mixed[k], n * TW:(n + 1) * TW],
                                           start=(k == 0), stop=(k == NMIX - 1))
                    mm.then_inc(done[h], 1)

        @block.vector
        def _(dve):
            for h in range(2):
                dve.sem_inc(added[h], 1)
            dve.wait_ge(x_loaded, 16)
            with dve.Fori(0, KD // 2) as i:
                for h in range(2):
                    dve.wait_ge(done[h], i + 1)
                    x = one(x2, i * 2 + h).rearrange("p (n t) -> p n t", n=NT)
                    dve.tensor_tensor(x, x, ps[:, h, :, 0:TW], ALU.add).then_inc(added[h], 1)


def norm_phase(nc, tag, src, weight, dst, ones, y_dram=None):
    with ExitStack() as stack:
        m = Memory(nc, stack)
        w1 = m.sb(tag + "_w", [P, KD])
        sq = m.sb(tag + "_sq", [P, 2, T])
        rb = m.sb(tag + "_rb", [P, T])
        ss = m.ps(tag + "_ss", [P, NT, 512])
        loaded, out = m.sem(tag + "_loaded"), m.sem(tag + "_out")
        squared, summed = m.sem(tag + "_squared"), m.sem(tag + "_summed")
        mean_ready, scaled = m.sem(tag + "_mean"), m.sem(tag + "_scaled")
        block = stack.enter_context(nc.Block())

        @block.sync
        def _(sp):
            sp.dma_start(w1[:], weight).then_inc(loaded, 16)
            if y_dram is not None:
                for k in range(KD):
                    sp.wait_ge(scaled, k + 1)
                    sp.dma_start(y_dram[:, k, :], dst[:, k, :]).then_inc(out, 16)
                sp.wait_ge(out, 16 * KD)

        @block.scalar
        def _(act):
            for k in range(KD):
                if k >= 2:
                    act.wait_ge(summed, k - 1)
                act.activation(sq[:, k % 2, :], src[:, k, :], ACT.Square).then_inc(squared, 1)
            act.wait_ge(mean_ready, 1)
            act.activation(rb[:], rb[:], ACT.Sqrt).then_inc(mean_ready, 1)

        @block.tensor
        def _(pe):
            for k in range(KD):
                pe.wait_ge(squared, k + 1)
                for n in range(NT):
                    mm = pe.matmul(ss[:, n, 0:TW], ones[:], sq[:, k % 2, n * TW:(n + 1) * TW],
                                   start=(k == 0), stop=(k == KD - 1))
                mm.then_inc(summed, 1)

        @block.vector
        def _(dve):
            dve.wait_ge(loaded, 16)
            dve.wait_ge(summed, KD)
            dve.tensor_scalar(rb[:].rearrange("p (n t) -> p n t", n=NT), ss[:, :, 0:TW], 1.0 / D, EPS,
                              ALU.mult, ALU.add).then_inc(mean_ready, 1)
            dve.wait_ge(mean_ready, 2)
            dve.reciprocal(rb[:], rb[:]).then_inc(mean_ready, 1)
            dve.wait_ge(mean_ready, 3)
            for k in range(KD):
                dve.scalar_tensor_tensor(dst[:, k, :], src[:, k, :], w1[:, k:k + 1], rb[:],
                                         ALU.mult, ALU.mult).then_inc(scaled, 1)


RT, RL = 12, T // 12


def router_phase(nc, io, h2, masks, comb_dram):
    with ExitStack() as stack:
        m = Memory(nc, stack)
        NL = NG + NE
        wr = m.sb("r_w", [P, KD, NL])
        lt = m.sb("r_lt", [NL, T])
        lg = m.sb("r_lg", [RL, RT, NL])

        def sb(name, *shape):
            return m.sb("r_" + name, [RL, RT, *shape])

        mx, e, s, pt, eq, hot, left = (sb("mx", 1), sb("e", NG), sb("s", 1), sb("pt", 1), sb("eq", NG),
                                       sb("hot", NG), sb("left", 1))
        prod, ls = sb("prod", NG, EPG), sb("ls", EPG)
        hot1, hot2, v1, v2, c4, comb = sb("h1", EPG), sb("h2", EPG), sb("v1", 1), sb("v2", 1), sb("c4", EPG), sb("c", NG, EPG)
        rows = m.sb("r_rows", [NE, T])
        ps = m.ps("r_ps", [P, NT, 512])
        ps2, ps3 = m.ps("r_ps2", [P, 512]), m.ps("r_ps3", [P, NT, 512])
        loaded, pe_s, act_s, dve_s, out = m.sem("r_l"), m.sem("r_pe"), m.sem("r_act"), m.sem("r_dve"), m.sem("r_out")
        ready, back = m.sem("r_ready"), m.sem("r_back")
        block = stack.enter_context(nc.Block())

        @block.sync
        def _(sp):
            sp.dma_start(wr[:], io["w_router"]).then_inc(loaded, 16)
            sp.wait_ge(act_s, 3)
            sp.dma_start(comb_dram, rows[:]).then_inc(out, 16)
            sp.wait_ge(out, 16)

        @block.tensor
        def _(pe):
            pe.wait_ge(loaded, 16)
            for n in range(NT):
                for k in range(KD):
                    mm = pe.matmul(ps[0:NL, n, 0:TW], wr[:, k, :], h2[:, k, n * TW:(n + 1) * TW],
                                   start=(k == 0), stop=(k == KD - 1))
            mm.then_inc(pe_s, 1)
            pe.wait_ge(act_s, 1)
            for t in range(RT):
                mm = pe.transpose(ps2[0:RL, t * NL:(t + 1) * NL], lt[:, t * RL:(t + 1) * RL], masks[0:NL, 0, 0:NL])
            mm.then_inc(pe_s, 1)
            pe.wait_ge(ready, 3)
            per = RT // NT
            for t in range(RT):
                mm = pe.transpose(ps3[0:NE, t // per, (t % per) * RL:(t % per + 1) * RL],
                                  comb[:, t].rearrange("p g e -> p (g e)"), masks[0:RL, 0, 0:RL])
            mm.then_inc(pe_s, 1)

        @block.scalar
        def _(act):
            act.wait_ge(pe_s, 1)
            act.copy(lt[:].rearrange("p (n t) -> p n t", n=NT), ps[0:NL, :, 0:TW]).then_inc(act_s, 1)
            act.wait_ge(ready, 1)
            act.activation(e[:], e[:], ACT.Exp).then_inc(back, 1)
            act.wait_ge(ready, 2)
            act.activation(ls[:], ls[:], ACT.Exp).then_inc(back, 1)
            act.wait_ge(pe_s, 3)
            act.copy(rows[:].rearrange("p (n t) -> p n t", n=NT), ps3[0:NE, :, 0:TW]).then_inc(act_s, 2)

        @block.vector
        def _(dve):
            count = [0]

            def link(ins):
                count[0] += 1
                ins.then_inc(dve_s, 1)
                dve.wait_ge(dve_s, count[0])

            def wide(ap, n):
                return ap.to_broadcast([RL, RT, n])

            def first_max(hot_, val, n):
                link(dve.tensor_reduce(mx[:], val[:], AX.X, ALU.max))
                link(dve.tensor_tensor(eq[:], val[:], wide(mx[:], n), ALU.is_ge))
                link(dve.memset(left[:], 1.0))
                for i in range(n):
                    link(dve.tensor_tensor(hot_[:, :, i:i + 1], eq[:, :, i:i + 1], left[:], ALU.mult))
                    link(dve.tensor_tensor(left[:], left[:], hot_[:, :, i:i + 1], ALU.subtract))

            dve.wait_ge(pe_s, 2)
            link(dve.tensor_copy(lg[:].rearrange("p t l -> p (t l)"), ps2[0:RL, 0:RT * NL]))
            link(dve.tensor_reduce(mx[:], lg[:, :, 0:NG], AX.X, ALU.max))
            dve.tensor_tensor(e[:], lg[:, :, 0:NG], wide(mx[:], NG), ALU.subtract).then_inc(ready, 1)
            dve.wait_ge(back, 1)
            link(dve.tensor_reduce(s[:], e[:], AX.X, ALU.add))
            first_max(hot, e, NG)
            link(dve.reciprocal(pt[:], s[:]))
            link(dve.tensor_tensor(pt[:], pt[:], mx[:], ALU.mult))
            link(dve.tensor_tensor(prod[:], lg[:, :, NG:].rearrange("p t (g e) -> p t g e", g=NG),
                                   hot[:].unsqueeze(3).to_broadcast([RL, RT, NG, EPG]), ALU.mult))
            link(dve.tensor_reduce(ls[:].unsqueeze(3), prod[:].rearrange("p t g e -> p t e g"), AX.X, ALU.add))
            link(dve.tensor_reduce(mx[:], ls[:], AX.X, ALU.max))
            dve.tensor_tensor(ls[:], ls[:], wide(mx[:], EPG), ALU.subtract).then_inc(ready, 1)
            dve.wait_ge(back, 2)
            link(dve.tensor_reduce(s[:], ls[:], AX.X, ALU.add))
            link(dve.reciprocal(s[:], s[:]))
            link(dve.tensor_tensor(ls[:], ls[:], wide(s[:], EPG), ALU.mult))
            first_max(hot1, ls, EPG)
            link(dve.tensor_copy(v1[:], mx[:]))
            link(dve.scalar_tensor_tensor(ls[:], hot1[:], -4.0, ls[:], ALU.mult, ALU.add))
            first_max(hot2, ls, EPG)
            link(dve.tensor_copy(v2[:], mx[:]))
            link(dve.tensor_tensor(s[:], v1[:], v2[:], ALU.add))
            link(dve.reciprocal(s[:], s[:]))
            link(dve.tensor_tensor(s[:], s[:], pt[:], ALU.mult))
            link(dve.tensor_tensor(hot1[:], hot1[:], wide(v1[:], EPG), ALU.mult))
            link(dve.tensor_tensor(hot2[:], hot2[:], wide(v2[:], EPG), ALU.mult))
            link(dve.tensor_tensor(c4[:], hot1[:], hot2[:], ALU.add))
            link(dve.tensor_tensor(c4[:], c4[:], wide(s[:], EPG), ALU.mult))
            dve.tensor_tensor(comb[:], hot[:].unsqueeze(3).to_broadcast([RL, RT, NG, EPG]),
                              c4[:].unsqueeze(2).to_broadcast([RL, RT, NG, EPG]), ALU.mult).then_inc(ready, 1)


MOE_PE = [f"{x}{f}" for f in range(2) for x in ("gate", "up")] + [f"down{d}" for d in range(KD)]
MOE_ACT = ["silu0", "silu1"]
MOE_DVE = ["gated0", "act0", "gated1", "act1"] + [f"add{d}" for d in range(KD)]


def moe_phase(nc, io, x2, h2, comb_dram):
    with ExitStack() as stack:
        m = Memory(nc, stack)
        wg, wu = m.sb("e_wg", [P, 2, KD, P]), m.sb("e_wu", [P, 2, KD, P])
        wd = m.sb("e_wd", [P, KD, 2, P])
        cb = m.sb("e_cb", [P, T])
        s = m.sb("e_s", [P, T])
        g = m.sb("e_g", [P, T])
        hid = m.sb("e_hid", [P, 2, T])
        ps = m.ps("e_ps", [P, 2, NT, 512])
        in_loaded, down_loaded, c_loaded = m.sem("e_in"), m.sem("e_down"), m.sem("e_c")
        p, a, v = Steps(m, "e_pe", MOE_PE), Steps(m, "e_act", MOE_ACT), Steps(m, "e_dve", MOE_DVE)
        block = stack.enter_context(nc.Block())

        def tiled(ap):
            return ap.rearrange("p (n t) -> p n t", n=NT)

        @block.sync
        def _(sp):
            with sp.Fori(0, NE) as e:
                sp.wait_ge(p.sem, p.at(e, "up1", 1))
                for src, dst in (("w_gate", wg), ("w_up", wu)):
                    sp.dma_start(dst[:], io[src][bass.ds(e, 1)].rearrange("a p f k c -> (a p) f k c")).then_inc(in_loaded, 16)
                sp.wait_ge(v.sem, v.at(e, "act1", 1))
                sp.dma_start(cb[:], comb_dram[bass.ds(e, 1), :].rearrange("a t -> (a t)").partition_broadcast(P)
                             ).then_inc(c_loaded, 16)
                sp.wait_ge(p.sem, p.at(e, f"down{KD - 1}", 1))
                sp.dma_start(wd[:], io["w_down"][bass.ds(e, 1)].rearrange("a p d f c -> (a p) d f c")).then_inc(down_loaded, 16)

        @block.tensor
        def _(pe):
            p.start(pe)
            with pe.Fori(0, NE) as e:
                def mm_tiles(half, lhs, rhs, n_in):
                    for n in range(NT):
                        for k in range(n_in):
                            mm = pe.matmul(ps[:, half, n, 0:TW], lhs(k), rhs(k)[:, n * TW:(n + 1) * TW],
                                           start=(k == 0), stop=(k == n_in - 1))
                    mm.then_inc(p.sem, 1)

                pe.wait_ge(in_loaded, e * 32 + 32)
                for f in range(2):
                    if f == 0:
                        pe.wait_ge(v.sem, v.at(e, f"add{KD - 2}", 1))
                    else:
                        pe.wait_ge(a.sem, a.at(e, "silu0"))
                    mm_tiles(0, lambda k: wg[:, f, k, :], lambda k: h2[:, k, :], KD)
                    if f == 0:
                        pe.wait_ge(v.sem, v.at(e, f"add{KD - 1}", 1))
                    else:
                        pe.wait_ge(v.sem, v.at(e, "act0"))
                    mm_tiles(1, lambda k: wu[:, f, k, :], lambda k: h2[:, k, :], KD)
                pe.wait_ge(down_loaded, e * 16 + 16)
                pe.wait_ge(v.sem, v.at(e, "act1"))
                for d in range(KD):
                    if d >= 2:
                        pe.wait_ge(v.sem, v.at(e, f"add{d - 2}"))
                    mm_tiles(d % 2, lambda k: wd[:, d, k, :], lambda k: hid[:, k, :], 2)

        @block.scalar
        def _(act):
            a.start(act)
            with act.Fori(0, NE) as e:
                for f in range(2):
                    act.wait_ge(p.sem, p.at(e, f"gate{f}"))
                    act.wait_ge(v.sem, v.at(e, "gated1", 1) if f == 0 else v.at(e, "gated0"))
                    act.activation(tiled(s[:]), ps[:, 0, :, 0:TW], ACT.Silu).then_inc(a.sem, 1)

        @block.vector
        def _(dve):
            v.start(dve)
            with dve.Fori(0, NE) as e:
                dve.wait_ge(c_loaded, e * 16 + 16)
                for f in range(2):
                    dve.wait_ge(a.sem, a.at(e, f"silu{f}"))
                    dve.wait_ge(v.sem, v.at(e, "act1", 1) if f == 0 else v.at(e, "act0"))
                    dve.tensor_tensor(g[:], s[:], cb[:], ALU.mult).then_inc(v.sem, 1)
                    dve.wait_ge(v.sem, v.at(e, f"gated{f}"))
                    dve.wait_ge(p.sem, p.at(e, f"up{f}"))
                    dve.wait_ge(p.sem, p.at(e, f"down{KD - 1}", 1))
                    dve.tensor_tensor(tiled(hid[:, f, :]), tiled(g[:]), ps[:, 1, :, 0:TW], ALU.mult).then_inc(v.sem, 1)
                for d in range(KD):
                    dve.wait_ge(p.sem, p.at(e, f"down{d}"))
                    dve.wait_ge(v.sem, v.at(e, f"add{d}", 1))
                    x = tiled(x2[:, d, :])
                    dve.tensor_tensor(x, x, ps[:, d % 2, :, 0:TW], ALU.add).then_inc(v.sem, 1)


def program(nc, io):
    z_dram = nc.dram_tensor("z_rows", (NZ, P, T), F32, kind="Internal").ap()
    yc_dram = nc.dram_tensor("yc_rows", (NC, P, T), F32, kind="Internal").ap()
    g_dram = nc.dram_tensor("g_rows", (NR, T), F32, kind="Internal").ap()
    comb_dram = nc.dram_tensor("comb_rows", (NE, T), F32, kind="Internal").ap()
    with ExitStack() as stack:
        m = Memory(nc, stack)
        ones = m.sb("ones", [P, P])
        masks = m.sb("masks", [P, 7, P])
        with ExitStack() as mix:
            mm = Memory(nc, mix)
            act_out = mm.sb("act_out", [P, NCONV, T])
            rows = [mm.sb(f"rows_{x}", [P, T]) for x in "abc"]
            with ExitStack() as first:
                hn = Memory(nc, first).sb("hn", [P, KD, T])
                norm1_phase(nc, io, hn, ones, masks)
                gates_phase(nc, io, hn, *rows, g_dram)
                projection_phase(nc, io, hn, act_out, z_dram, yc_dram)
            qk_norm_phase(nc, act_out, ones)
            gdn_phase(nc, io, act_out, rows, g_dram, masks, False)
            gdn_phase(nc, io, act_out, rows, g_dram, masks, True)
            ssd_phase(nc, io, act_out, rows, g_dram, masks, False)
            ssd_phase(nc, io, act_out, rows, g_dram, masks, True)
            mixed = gate_phase(nc, io, act_out, ones, z_dram, yc_dram)
            x2_out = mm.sb("x2_first", [P, KD, T])
            out_projection_phase(nc, io, act_out, mixed, x2_out)
            x2 = x2_out
            h2 = act_out[:, 0:KD, :]
            norm_phase(nc, "n2", x2, io["norm2_w"], h2, ones)
            router_phase(nc, io, h2, masks, comb_dram)
            moe_phase(nc, io, x2, h2, comb_dram)
            norm_phase(nc, "nf", x2, io["final_w"], x2, ones, io["yT"])


def gdn_states(a):
    return np.ascontiguousarray(a[0].transpose(2, 0, 1, 3))


def channel_blocks(a):
    b, r, c = a.shape[1:]
    return a[0].reshape(b, r, c // P, P).transpose(3, 2, 0, 1)


def from_channel_blocks(a):
    p, n, b, r = a.shape
    return np.ascontiguousarray(a.transpose(2, 3, 1, 0).reshape(1, b, r, n * p))


def mask_constants():
    i = np.arange(P)
    later = i[None, :] >= i[:, None]
    below = i[:, None] > i[None, :]
    seq = i[:, None] // LSEQ == i[None, :] // LSEQ
    none = np.float32(NEG)
    zero = np.float32(0)
    out = np.stack([
        np.eye(P, dtype=np.float32),
        np.where(later, zero, none), np.where(below, zero, none),
        (i[:, None] // 16 == i[None, :] // 16).astype(np.float32),
        np.where(later & seq, zero, none), np.where(below & seq, zero, none),
        (i[:, None] // LSEQ == i[None, :]).astype(np.float32)], axis=1)
    return np.ascontiguousarray(out.astype(np.float32))


def lay_out(x):
    f = lambda n: np.asarray(x[n], dtype=np.float32)
    tokens = np.concatenate([f("meta_tokens"), f("x_prompt")[0], f("x_sample").reshape(TS, D)])
    w = f("w_in")[0]
    at = {}
    start = 0
    for name, n in (("qkv", 1536), ("z_a", 512), ("b", HA), ("a", HA), ("xbc", 1024), ("z_b", 512), ("dt", HB),
                    ("h", 512), ("c", 512), ("bb", 512)):
        at[name] = w[:, start:start + n]
        start += n
    short = [at[n][:, c * P:(c + 1) * P] for c in range(NC) for n in ("h", "c", "bb")]
    blocks = np.concatenate([at["qkv"], at["xbc"], at["z_a"], at["z_b"], *short], axis=1)
    gates = np.zeros((D, 64), np.float32)
    gates[:, 0:HA], gates[:, ROW_G:ROW_G + HA], gates[:, ROW_G + HA:ROW_G + NR] = at["b"], at["a"], at["dt"]
    bias, alog = np.zeros((64, 1), np.float32), np.zeros((64, 1), np.float32)
    bias[ROW_G:ROW_G + HA, 0], bias[ROW_G + HA:ROW_G + NR, 0] = f("dt_bias_a")[0], f("dt_bias_b")[0]
    alog[ROW_G:ROW_G + HA, 0], alog[ROW_G + HA:ROW_G + NR, 0] = f("a_log_a")[0], f("a_log_b")[0]

    def columns(v):
        return v.reshape(-1, P).T

    def stationary(v, n):
        return v.reshape(-1, P, n, v.shape[1] // n).transpose(2, 1, 0, 3)

    taps = np.zeros((P, NCONV, W_A + 1), np.float32)
    taps[:, :12, :W_A] = f("conv_a_w")[0].reshape(W_A, 12, P).transpose(2, 1, 0)
    taps[:, 12:, :W_A] = f("conv_b_w")[0].reshape(W_A, 8, P).transpose(2, 1, 0)
    taps[:, 12:, W_A] = columns(f("conv_b_b")[0])
    io = {
        "xT": tokens.T.reshape(KD, P, T).transpose(1, 0, 2),
        "masks": mask_constants(),
        "norm1_w": columns(f("norm1_w")[0]), "norm2_w": columns(f("norm2_w")[0]), "final_w": columns(f("final_norm_w")),
        "w_gates": gates.reshape(KD, P, 64).transpose(1, 0, 2), "gate_bias": bias, "gate_alog": alog,
        "w_in": stationary(blocks, NCONV + NZ + 3 * NC),
        "taps": taps, "taps_c": f("conv_c_w")[0].reshape(W_C, NC, P).transpose(2, 1, 0),
        "hist_ab": np.concatenate([channel_blocks(f("state_gdn_conv")), channel_blocks(f("state_ssd_conv"))], axis=1),
        "hist_c": channel_blocks(f("state_sconv")),
        "state_gdn": f("state_gdn")[0].transpose(2, 0, 1, 3),
        "state_ssd": f("state_ssd")[0].transpose(3, 0, 1, 2),
        "d_skip": columns(np.repeat(f("d_skip_b")[0], PB)),
        "onorm_a": columns(f("onorm_a_w")[0]), "onorm_b": columns(f("onorm_b_w")[0]),
        "w_out": stationary(f("w_out")[0], KD),
        "w_router": np.concatenate([f("w_router_g")[0], f("w_router_e")[0]], axis=1).reshape(KD, P, -1).transpose(1, 0, 2),
        "w_gate": f("w_gate")[0].reshape(NE, KD, P, 2, P).transpose(0, 2, 3, 1, 4),
        "w_up": f("w_up")[0].reshape(NE, KD, P, 2, P).transpose(0, 2, 3, 1, 4),
        "w_down": f("w_down")[0].reshape(NE, 2, P, KD, P).transpose(0, 2, 3, 1, 4),
    }
    return {k: np.ascontiguousarray(v) for k, v in io.items()}


OUTPUTS = {
    "yT": (P, KD, T), "new_hist_ab": (P, NCONV, 1 + NSEQ, HIST), "new_hist_c": (P, NC, 1 + NSEQ, HISTC),
    "new_gdn_p": (P, HA, DK), "new_gdn_s": (P, NSEQ, HA, DK), "new_ssd_p": (P, HB, PB), "new_ssd_s": (P, NSEQ, HB, PB),
}


def kernel(**inputs):
    import concourse.bacc as bacc
    from concourse.bass_utils import run_bass_kernel_spmd

    nc = bacc.Bacc("TRN2", target_bir_lowering=False, num_devices=1)
    arrays = lay_out(inputs)
    io = {n: nc.dram_tensor("in_" + n, a.shape, F32, kind="ExternalInput").ap() for n, a in arrays.items()}
    io |= {n: nc.dram_tensor(n, s, F32, kind="ExternalOutput").ap() for n, s in OUTPUTS.items()}
    program(nc, io)
    got = run_bass_kernel_spmd(nc, [{"in_" + n: a for n, a in arrays.items()}], core_ids=[0]).results[0]

    y = got["yT"].transpose(2, 1, 0).reshape(T, D)
    hist = got["new_hist_ab"]
    na = 3 * HA
    out = (
        y[N_META:TP][None], y[TP:].reshape(NSEQ, LSEQ, D),
        got["new_gdn_p"].transpose(1, 0, 2)[None, None],
        from_channel_blocks(hist[:, :na, :1]), got["new_ssd_p"].transpose(1, 2, 0)[None, None],
        from_channel_blocks(hist[:, na:, :1]), from_channel_blocks(got["new_hist_c"][:, :, :1]),
        got["new_gdn_s"].transpose(1, 2, 0, 3)[None],
        from_channel_blocks(hist[:, :na, 1:]), got["new_ssd_s"].transpose(1, 2, 3, 0)[None],
        from_channel_blocks(hist[:, na:, 1:]), from_channel_blocks(got["new_hist_c"][:, :, 1:]),
    )
    return tuple(np.ascontiguousarray(a) for a in out)
```

```python
from contextlib import ExitStack

import numpy as np

import concourse.bass as bass
from concourse import mybir

F32 = mybir.dt.float32
F32R = mybir.dt.float32r
ALU = mybir.AluOpType
ACT = mybir.ActivationFunctionType
AX = mybir.AxisListType

P = 128
D = 1024
KD = D // P
N_META, SEQ = 16, 1024
TP = N_META + SEQ
NSEQ, LSEQ = 8, 8
TS = NSEQ * LSEQ
T = TP + TS
NT, TW = 3, T // 3
HA, DK = 4, 128
HB, PB, GB, NB = 8, 64, 2, 128
CH = 104
NCH = TP // CH
W_A, W_C = 4, 3
NCONV, NZ, NC = 20, 8, 4
HIST = W_A - 1
RAW = HIST + TP + NSEQ * (HIST + LSEQ)
CONVW = RAW - HIST
HISTC = W_C - 1
RAWC = HISTC + TP + NSEQ * (HISTC + LSEQ)
CONVWC = RAWC - HISTC
NPAIR = 2
NE, NG, EPG, FF, TOPK = 16, 4, 4, 256, 2
NMIX = 12
EPS = 1e-6
NEG = -1e30
ROW_G = 32
NR = 12
TAIL = TP - 2 * TW


def samples(ap, base, stride, lo, hi):
    return ap[:, base:base + NSEQ * stride].rearrange("p (b s) -> p b s", s=stride)[:, :, lo:hi]


def one(ap, b):
    names = "xyz"[:len(ap.shape) - 2]
    return ap[:, bass.ds(b, 1)].rearrange(f"p a {' '.join(names)} -> p (a {names[0]}) {' '.join(names[1:])}")


class Memory:

    def __init__(self, nc, stack):
        self.nc, self.stack = nc, stack

    def sb(self, name, shape, dt=F32):
        return self.stack.enter_context(self.nc.sbuf_tensor(name, shape, dt))

    def ps(self, name, shape, dt=F32):
        return self.stack.enter_context(self.nc.psum_tensor(name, shape, dt))

    def sem(self, name):
        return self.stack.enter_context(self.nc.semaphore(name))


def norm1_phase(nc, io, hn, ones, masks):
    with ExitStack() as stack:
        m = Memory(nc, stack)
        w1 = m.sb("n1_w", [P, KD])
        sq = m.sb("n1_sq", [P, 2, T])
        rb = m.sb("n1_rb", [P, T])
        ss = m.ps("n1_ss", [P, NT, 512])
        loaded, ones_set = m.sem("n1_loaded"), m.sem("n1_ones")
        squared, summed = m.sem("n1_squared"), m.sem("n1_summed")
        mean_ready, scaled = m.sem("n1_mean"), m.sem("n1_scaled")
        block = stack.enter_context(nc.Block())

        @block.sync
        def _(sp):
            sp.dma_start(w1[:], io["norm1_w"]).then_inc(loaded, 16)
            sp.dma_start(masks[:], io["masks"]).then_inc(loaded, 16)
            for k in range(KD):
                sp.dma_start(hn[:, k, :], io["xT"][:, k, :]).then_inc(loaded, 16)

        @block.scalar
        def _(act):
            act.wait_ge(loaded, 16 * (KD + 2))
            for k in range(KD):
                if k >= 2:
                    act.wait_ge(summed, k - 1)
                act.activation(sq[:, k % 2, :], hn[:, k, :], ACT.Square).then_inc(squared, 1)
            act.wait_ge(mean_ready, 1)
            act.activation(rb[:], rb[:], ACT.Sqrt).then_inc(mean_ready, 1)

        @block.tensor
        def _(pe):
            pe.wait_ge(ones_set, 1)
            for k in range(KD):
                pe.wait_ge(squared, k + 1)
                for n in range(NT):
                    mm = pe.matmul(ss[:, n, 0:TW], ones[:], sq[:, k % 2, n * TW:(n + 1) * TW],
                                   start=(k == 0), stop=(k == KD - 1))
                mm.then_inc(summed, 1)

        @block.vector
        def _(dve):
            dve.memset(ones[:], 1.0).then_inc(ones_set, 1)
            dve.wait_ge(summed, KD)
            dve.tensor_scalar(rb[:].rearrange("p (n t) -> p n t", n=NT), ss[:, :, 0:TW], 1.0 / D, EPS,
                              ALU.mult, ALU.add).then_inc(mean_ready, 1)
            dve.wait_ge(mean_ready, 2)
            dve.reciprocal(rb[:], rb[:]).then_inc(mean_ready, 1)
            dve.wait_ge(mean_ready, 3)
            for k in range(KD):
                dve.scalar_tensor_tensor(hn[:, k, :], hn[:, k, :], w1[:, k:k + 1], rb[:],
                                         ALU.mult, ALU.mult).then_inc(scaled, 1)


def gates_phase(nc, io, hn, rows_a, rows_b, rows_c, g_dram):
    with ExitStack() as stack:
        m = Memory(nc, stack)
        wg = m.sb("g_w", [P, KD, 64])
        bias = m.sb("g_bias", [64, 1])
        a_log = m.sb("g_alog", [64, 1])
        neg_a = m.sb("g_nega", [64, 1])
        mask = m.sb("g_mask", [64, T])
        y = m.sb("g_y", [64, T])
        u = m.sb("g_u", [64, T])
        d = m.sb("g_d", [64, T])
        ps = m.ps("g_ps", [P, NT, 512])
        loaded, set_, proj = m.sem("g_loaded"), m.sem("g_set"), m.sem("g_proj")
        act_step, dve_step, out = m.sem("g_act"), m.sem("g_dve"), m.sem("g_out")
        block = stack.enter_context(nc.Block())
        gr = slice(ROW_G, ROW_G + NR)

        def tiles(ap):
            return ap.rearrange("p (n t) -> p n t", n=NT)

        @block.sync
        def _(sp):
            sp.dma_start(wg[:], io["w_gates"]).then_inc(loaded, 16)
            sp.dma_start(bias[:], io["gate_bias"]).then_inc(loaded, 16)
            sp.dma_start(a_log[:], io["gate_alog"]).then_inc(loaded, 16)
            sp.wait_ge(dve_step, 13)
            sp.dma_start(g_dram, rows_a[gr, :]).then_inc(out, 16)
            sp.wait_ge(out, 16)

        @block.tensor
        def _(pe):
            pe.wait_ge(loaded, 48)
            for n in range(NT):
                for k in range(KD):
                    mm = pe.matmul(ps[0:64, n, 0:TW], wg[:, k, :], hn[:, k, n * TW:(n + 1) * TW],
                                   start=(k == 0), stop=(k == KD - 1))
            mm.then_inc(proj, 1)

        @block.scalar
        def _(act):
            act.wait_ge(proj, 1)
            act.wait_ge(set_, 4)
            act.activation(tiles(rows_a[0:HA, :]), ps[0:HA, :, 0:TW], ACT.Exp, scale=-1.0).then_inc(act_step, 1)
            act.activation(neg_a[gr, :], a_log[gr, :], ACT.Exp).then_inc(act_step, 1)
            act.wait_ge(dve_step, 3)
            act.activation(y[gr, :], u[gr, :], ACT.Exp).then_inc(act_step, 1)
            act.wait_ge(dve_step, 5)
            act.activation(d[gr, :], u[gr, :], ACT.Ln).then_inc(act_step, 1)

        @block.vector
        def _(dve):
            dve.memset(rows_a[:], 0.0).then_inc(set_, 1)
            dve.memset(rows_b[:], 0.0).then_inc(set_, 1)
            dve.memset(rows_c[:], 0.0).then_inc(set_, 1)
            dve.memset(mask[:], 1.0).then_inc(set_, 1)
            dve.wait_ge(set_, 4)
            dve.memset(mask[:, 0:TP].rearrange("p (c t) -> p c t", t=CH)[:, :, 0:1], 0.0).then_inc(set_, 1)
            dve.memset(samples(mask, TP, LSEQ, 0, 1), 0.0).then_inc(set_, 1)
            dve.wait_ge(proj, 1)
            dve.wait_ge(loaded, 48)
            dve.tensor_scalar(tiles(rows_c[gr, :]), ps[gr, :, 0:TW], bias[gr, :], None,
                              ALU.add).then_inc(dve_step, 1)
            dve.wait_ge(dve_step, 1)
            dve.tensor_scalar(d[gr, :], rows_c[gr, :], -1.0, None, ALU.mult).then_inc(dve_step, 1)
            dve.wait_ge(dve_step, 2)
            dve.tensor_tensor(u[gr, :], rows_c[gr, :], d[gr, :], ALU.min).then_inc(dve_step, 1)
            dve.wait_ge(act_step, 1)
            dve.tensor_scalar(rows_a[0:HA, :], rows_a[0:HA, :], 1.0, None, ALU.add).then_inc(dve_step, 1)
            dve.wait_ge(act_step, 3)
            dve.tensor_scalar(u[gr, :], y[gr, :], 1.0, None, ALU.add).then_inc(dve_step, 1)
            dve.wait_ge(dve_step, 5)
            dve.scalar_tensor_tensor(y[gr, :], u[gr, :], -1.0, y[gr, :], ALU.add, ALU.subtract,
                                     ).then_inc(dve_step, 1)
            dve.reciprocal(rows_a[0:HA, :], rows_a[0:HA, :]).then_inc(dve_step, 1)
            dve.wait_ge(act_step, 4)
            dve.reciprocal(u[gr, :], u[gr, :]).then_inc(dve_step, 1)
            dve.wait_ge(dve_step, 8)
            dve.tensor_tensor(y[gr, :], y[gr, :], u[gr, :], ALU.mult).then_inc(dve_step, 1)
            dve.wait_ge(dve_step, 9)
            dve.tensor_tensor(d[gr, :], d[gr, :], y[gr, :], ALU.subtract).then_inc(dve_step, 1)
            dve.wait_ge(dve_step, 10)
            dve.scalar_tensor_tensor(rows_c[gr, :], rows_c[gr, :], 0.0, d[gr, :], ALU.max,
                                     ALU.add).then_inc(dve_step, 1)
            dve.wait_ge(dve_step, 11)
            dve.tensor_scalar(y[gr, :], rows_c[gr, :], neg_a[gr, :], -1.0, ALU.mult,
                              ALU.mult).then_inc(dve_step, 1)
            dve.wait_ge(dve_step, 12)
            dve.wait_ge(set_, 6)
            dve.tensor_tensor_scan(rows_a[gr, :], mask[gr, :], y[gr, :], 0.0, ALU.mult,
                                   ALU.add).then_inc(dve_step, 1)
            dve.wait_ge(dve_step, 13)
            for start, length in ((0, CH), (TP, LSEQ)):
                end = TP if start == 0 else T
                g = rows_a[gr, start:end].rearrange("p (c t) -> p c t", t=length)
                o = rows_b[gr, start:end].rearrange("p (c t) -> p c t", t=length)
                dve.tensor_tensor(o, g[:, :, length - 1:length].to_broadcast(list(g.shape)), g,
                                  ALU.subtract).then_inc(dve_step, 1)


def put_raw(op, dst, src, hist_n):
    op(dst[:, hist_n:hist_n + TW], src[:, 0, 0:TW], (0, TW))
    op(dst[:, hist_n + TW:hist_n + 2 * TW], src[:, 1, 0:TW], (TW, 2 * TW))
    op(dst[:, hist_n + 2 * TW:hist_n + TP], src[:, 2, 0:TAIL], (2 * TW, TP))
    return op(samples(dst, hist_n + TP, hist_n + LSEQ, hist_n, hist_n + LSEQ),
              src[:, 2, TAIL:TW].rearrange("p (b t) -> p b t", t=LSEQ), (TP, T))


def keep_tail(eng, tails, b, raw, hist_n):
    tail = one(tails, b)
    eng.tensor_copy(tail[:, 0, :], raw[:, TP:TP + hist_n])
    return eng.tensor_copy(tail[:, 1:, :], samples(raw, hist_n + TP, hist_n + LSEQ, LSEQ, hist_n + LSEQ))


def projection_phase(nc, io, hn, act_out, z_dram, yc_dram):
    with ExitStack() as stack:
        m = Memory(nc, stack)
        w = m.sb("c_w", [P, 2, KD, P])
        raw = m.sb("c_raw", [P, 2, RAW])
        y = m.sb("c_y", [P, 2, RAW])
        out = m.sb("c_out", [P, 2, T])
        taps = m.sb("c_taps", [P, NCONV, W_A + 1])
        hist = m.sb("c_hist", [P, NCONV, NSEQ, HIST])
        tails = m.sb("c_tails", [P, NCONV, 1 + NSEQ, HIST])
        taps_c = m.sb("c_tapsc", [P, NC, W_C])
        hist_c = m.sb("c_histc", [P, NC, NSEQ, HISTC])
        tails_c = m.sb("c_tailsc", [P, NC, 1 + NSEQ, HISTC])
        ps = m.ps("c_ps", [P, 2, NT, 512])

        def pair(name):
            return [m.sem(f"c_{name}{h}") for h in range(2)]

        consts, kept = m.sem("c_consts"), m.sem("c_kept")
        w_loaded, proj_done = pair("wloaded"), pair("proj")
        ps_free, raw_done, hist_done, tail_done = pair("psfree"), pair("raw"), pair("hist"), pair("tail")
        tapped, conv_done, silu_done = pair("tapped"), pair("conv"), pair("silu")
        z_done, z_sent, yc_sent, out_free = pair("z"), pair("zsent"), pair("ycsent"), pair("outfree")
        h_done, craw_done, ctapped, yc_done = m.sem("c_h"), m.sem("c_craw"), m.sem("c_ctapped"), m.sem("c_yc")
        chist_done, ctail_done = m.sem("c_chist"), m.sem("c_ctail")
        NB_ALL = NCONV + NZ + 3 * NC

        with nc.Block() as block:
            @block.sync
            def _(sp):
                sp.dma_start(taps[:], io["taps"]).then_inc(consts, 16)
                sp.dma_start(hist[:], io["hist_ab"]).then_inc(consts, 16)
                sp.dma_start(taps_c[:], io["taps_c"]).then_inc(consts, 16)
                sp.dma_start(hist_c[:], io["hist_c"]).then_inc(consts, 16)
                for h in range(2):
                    sp.dma_start(w[:, h], io["w_in"][h]).then_inc(w_loaded[h], 16)
                with sp.Fori(0, NB_ALL // 2 - 1) as i:
                    for h in range(2):
                        sp.wait_ge(proj_done[h], i + 1)
                        sp.dma_start(w[:, h], io["w_in"][bass.ds(i * 2 + (2 + h), 1)].rearrange(
                            "a p k c -> (a p) k c")).then_inc(w_loaded[h], 16)
                for h in range(2):
                    sp.wait_ge(z_sent[h], 16 * (NZ // 2))
                    sp.wait_ge(yc_sent[h], 16 * NPAIR)
                sp.wait_ge(kept, 32)

            @block.tensor
            def _(pe):
                with pe.Fori(0, NB_ALL // 2) as i:
                    for h in range(2):
                        pe.wait_ge(w_loaded[h], i * 16 + 16)
                        pe.wait_ge(ps_free[h], i + 1)
                        for n in range(NT):
                            for k in range(KD):
                                mm = pe.matmul(ps[:, h, n, 0:TW], w[:, h, k, :], hn[:, k, n * TW:(n + 1) * TW],
                                               start=(k == 0), stop=(k == KD - 1))
                        mm.then_inc(proj_done[h], 1)

            @block.scalar
            def _(act):
                for h in range(2):
                    act.sem_inc(ps_free[h], 1)
                    act.sem_inc(raw_done[h], 1)
                    act.sem_inc(silu_done[h], 1)
                with act.Fori(0, NCONV // 2) as i:
                    for h in range(2):
                        act.wait_ge(proj_done[h], i + 1)
                        act.wait_ge(conv_done[h], i + 1)
                        act.wait_ge(tail_done[h], i + 1)
                        put_raw(lambda o, s, _: act.copy(o, s), raw[:, h, :], ps[:, h], HIST).then_inc(raw_done[h], 1)
                        act.wait_ge(raw_done[h], i + 2)
                        act.sem_inc(ps_free[h], 1)
                        act.wait_ge(conv_done[h], i + 2)
                        dst = one(act_out, i * 2 + h)
                        act.activation(dst[:, 0:TP], y[:, h, 0:TP], ACT.Silu)
                        act.activation(dst[:, TP:T].rearrange("p (b t) -> p b t", t=LSEQ),
                                       samples(y[:, h], TP, HIST + LSEQ, HIST, HIST + LSEQ),
                                       ACT.Silu).then_inc(silu_done[h], 1)
                with act.Fori(0, NZ // 2) as i:
                    for h in range(2):
                        act.wait_ge(proj_done[h], i + (NCONV // 2 + 1))
                        act.wait_ge(out_free[h], i + 1)
                        act.activation(out[:, h, :].rearrange("p (n t) -> p n t", n=NT), ps[:, h, :, 0:TW],
                                       ACT.Silu).then_inc(z_done[h], 1)
                        act.wait_ge(z_done[h], i + 1)
                        act.sem_inc(ps_free[h], 1)
                act.wait_ge(conv_done[0], NCONV // 2 + 1)
                act.wait_ge(tail_done[0], NCONV // 2 + 1)
                with act.Fori(0, NPAIR) as i:
                    for c in range(2):
                        act.wait_ge(proj_done[c], i * 3 + (NCONV + NZ) // 2 + 1 + c)
                        act.wait_ge(craw_done, i * 2 + (1 + c))
                        act.copy(raw[:, 0, 0:T].rearrange("p (n t) -> p n t", n=NT),
                                 ps[:, c, :, 0:TW]).then_inc(h_done, 1)
                        act.wait_ge(h_done, i * 2 + (1 + c))
                        act.sem_inc(ps_free[c], 1)

            @block.gpsimd
            def _(pool):
                for h in range(2):
                    pool.sem_inc(out_free[h], 1)
                    pool.sem_inc(tail_done[h], 1)
                    pool.memset(raw[:, h, 0:HIST], 0.0).then_inc(hist_done[h], 1)
                pool.wait_ge(consts, 64)
                with pool.Fori(0, NCONV // 2) as i:
                    for h in range(2):
                        pool.wait_ge(conv_done[h], i + 1)
                        pool.wait_ge(tail_done[h], i + 1)
                        pool.wait_ge(hist_done[h], i + 1)
                        pool.tensor_copy(samples(raw[:, h], HIST + TP, HIST + LSEQ, 0, HIST),
                                         one(hist, i * 2 + h)).then_inc(hist_done[h], 1)
                        pool.wait_ge(raw_done[h], i + 2)
                        keep_tail(pool, tails, i * 2 + h, raw[:, h], HIST).then_inc(tail_done[h], 1)
                for h in range(2):
                    pool.wait_ge(tail_done[h], NCONV // 2 + 1)
                pool.dma_start(io["new_hist_ab"], tails[:]).then_inc(kept, 16)
                with pool.Fori(0, NZ // 2) as i:
                    for h in range(2):
                        pool.wait_ge(z_done[h], i + 1)
                        pool.dma_start(z_dram[bass.ds(i * 2 + h, 1)].rearrange("a p t -> (a p) t"),
                                       out[:, h, :]).then_inc(z_sent[h], 16)
                        pool.wait_ge(z_sent[h], i * 16 + 16)
                        pool.sem_inc(out_free[h], 1)
                for h in range(2):
                    pool.wait_ge(conv_done[h], NCONV // 2 + 1)
                pool.memset(raw[:, 1, 0:HISTC], 0.0).then_inc(chist_done, 1)
                with pool.Fori(0, NPAIR) as i:
                    for c in range(2):
                        pool.wait_ge(yc_done, i * 2 + (1 + c))
                        pool.wait_ge(ctail_done, i * 2 + (1 + c))
                        pool.wait_ge(chist_done, i * 2 + (1 + c))
                        pool.tensor_copy(samples(raw[:, 1], HISTC + TP, HISTC + LSEQ, 0, HISTC),
                                         one(hist_c, i * 2 + c)).then_inc(chist_done, 1)
                        pool.wait_ge(craw_done, i * 2 + (2 + c))
                        keep_tail(pool, tails_c, i * 2 + c, raw[:, 1], HISTC).then_inc(ctail_done, 1)
                        pool.wait_ge(yc_done, i * 2 + (2 + c))
                        pool.dma_start(yc_dram[bass.ds(i * 2 + c, 1)].rearrange("a p t -> (a p) t"),
                                       out[:, c, :]).then_inc(yc_sent[c], 16)
                        pool.wait_ge(yc_sent[c], i * 16 + 16)
                        pool.sem_inc(out_free[c], 1)
                pool.wait_ge(ctail_done, NC + 1)
                pool.dma_start(io["new_hist_c"], tails_c[:]).then_inc(kept, 16)

            @block.vector
            def _(dve):
                dve.sem_inc(conv_done[0], 1)
                dve.sem_inc(conv_done[1], 1)
                dve.sem_inc(craw_done, 1)
                dve.sem_inc(yc_done, 1)
                dve.sem_inc(ctail_done, 1)
                dve.wait_ge(consts, 64)
                with dve.Fori(0, NCONV // 2) as i:
                    for h in range(2):
                        dve.wait_ge(raw_done[h], i + 2)
                        dve.wait_ge(hist_done[h], i + 2)
                        dve.wait_ge(silu_done[h], i + 1)
                        tap = taps[:, bass.ds(i * 2 + h, 1), :].rearrange("p a t -> p (a t)")
                        dve.tensor_scalar(y[:, h, 0:CONVW], raw[:, h, 0:CONVW], tap[:, 0:1],
                                          tap[:, W_A:W_A + 1], ALU.mult, ALU.add).then_inc(tapped[h], 1)
                        for j in range(1, W_A):
                            dve.wait_ge(tapped[h], i * (W_A - 1) + j)
                            op = dve.scalar_tensor_tensor(y[:, h, 0:CONVW], raw[:, h, j:j + CONVW], tap[:, j:j + 1],
                                                          y[:, h, 0:CONVW], ALU.mult, ALU.add)
                            op.then_inc(tapped[h] if j < W_A - 1 else conv_done[h], 1)
                dve.wait_ge(silu_done[0], NCONV // 2 + 1)
                dve.wait_ge(tail_done[1], NCONV // 2 + 1)
                with dve.Fori(0, NPAIR) as i:
                    for c in range(2):
                        at_c, at_b = (1 + 3 * c) // 2, (2 + 3 * c) // 2
                        half_c, half_b = (1 + 3 * c) % 2, (2 + 3 * c) % 2
                        dve.wait_ge(proj_done[half_c], i * 3 + ((NCONV + NZ) // 2 + 1 + at_c))
                        dve.wait_ge(h_done, i * 2 + (1 + c))
                        dve.wait_ge(ctail_done, i * 2 + (1 + c))
                        put_raw(lambda o, s, t: dve.tensor_tensor(o, raw[:, 0, t[0]:t[1]] if t[1] <= TP else
                                                                  raw[:, 0, TP:T].rearrange("p (b t) -> p b t", t=LSEQ),
                                                                  s, ALU.mult),
                                raw[:, 1], ps[:, half_c], HISTC).then_inc(craw_done, 1)
                        dve.wait_ge(craw_done, i * 2 + (2 + c))
                        dve.sem_inc(ps_free[half_c], 1)
                        dve.wait_ge(chist_done, i * 2 + (2 + c))
                        tap = taps_c[:, bass.ds(i * 2 + c, 1), :].rearrange("p a t -> p (a t)")
                        dve.tensor_scalar(y[:, 0, 0:CONVWC], raw[:, 1, 0:CONVWC], tap[:, 0:1], None,
                                          ALU.mult).then_inc(ctapped, 1)
                        for j in range(1, W_C):
                            dve.wait_ge(ctapped, i * (2 * W_C) + (c * W_C + j))
                            dve.scalar_tensor_tensor(y[:, 0, 0:CONVWC], raw[:, 1, j:j + CONVWC], tap[:, j:j + 1],
                                                     y[:, 0, 0:CONVWC], ALU.mult, ALU.add).then_inc(ctapped, 1)
                        dve.wait_ge(ctapped, i * (2 * W_C) + (c * W_C + W_C))
                        dve.wait_ge(proj_done[half_b], i * 3 + ((NCONV + NZ) // 2 + 1 + at_b))
                        dve.wait_ge(out_free[c], i + (NZ // 2 + 1))
                        dve.tensor_tensor(out[:, c, 0:2 * TW].rearrange("p (n t) -> p n t", n=2),
                                          y[:, 0, 0:2 * TW].rearrange("p (n t) -> p n t", n=2),
                                          ps[:, half_b, 0:2, 0:TW], ALU.mult)
                        dve.tensor_tensor(out[:, c, 2 * TW:TP], y[:, 0, 2 * TW:TP], ps[:, half_b, 2, 0:TAIL], ALU.mult)
                        dve.tensor_tensor(out[:, c, TP:T].rearrange("p (b t) -> p b t", t=LSEQ),
                                          samples(y[:, 0], TP, HISTC + LSEQ, HISTC, HISTC + LSEQ),
                                          ps[:, half_b, 2, TAIL:TW].rearrange("p (b t) -> p b t", t=LSEQ),
                                          ALU.mult).then_inc(yc_done, 1)
                        dve.wait_ge(yc_done, i * 2 + (2 + c))
                        dve.sem_inc(ps_free[half_b], 1)


class Steps:

    def __init__(self, m, name, names, ahead=1):
        self.sem, self.names, self.n, self.ahead = m.sem(name), names, len(names), ahead

    def start(self, eng):
        eng.sem_inc(self.sem, self.n * self.ahead)

    def at(self, r, name, back=0):
        return r * self.n + (self.n * (self.ahead - back) + self.names.index(name) + 1)


def bc(col, n):
    return col.unsqueeze(2).to_broadcast([col.shape[0], col.shape[1], n])


def qk_norm_phase(nc, act_out, ones):
    with ExitStack() as stack:
        m = Memory(nc, stack)
        sq = m.sb("n_sq", [P, T])
        r = m.sb("n_r", [P, T])
        ps = m.ps("n_ps", [P, NT, 512])
        a = Steps(m, "n_act", ["square", "root"])
        p = Steps(m, "n_pe", ["sum"])
        v = Steps(m, "n_dve", ["sum", "inverse", "scaled"])
        block = stack.enter_context(nc.Block())

        @block.scalar
        def _(act):
            a.start(act)
            with act.Fori(0, 2 * HA) as b:
                act.wait_ge(p.sem, p.at(b, "sum", 1))
                act.activation(sq[:], one(act_out, b), ACT.Square).then_inc(a.sem, 1)
                act.wait_ge(v.sem, v.at(b, "sum"))
                act.activation(r[:], r[:], ACT.Sqrt).then_inc(a.sem, 1)

        @block.tensor
        def _(pe):
            p.start(pe)
            with pe.Fori(0, 2 * HA) as b:
                pe.wait_ge(a.sem, a.at(b, "square"))
                pe.wait_ge(v.sem, v.at(b, "sum", 1))
                for n in range(NT):
                    mm = pe.matmul(ps[:, n, 0:TW], ones[:], sq[:, n * TW:(n + 1) * TW], start=True, stop=True)
                mm.then_inc(p.sem, 1)

        @block.vector
        def _(dve):
            v.start(dve)
            for part, scale in ((0, DK ** -0.5), (1, 1.0)):
                with dve.Fori(part * HA, (part + 1) * HA) as b:
                    dve.wait_ge(p.sem, p.at(b, "sum"))
                    dve.wait_ge(v.sem, v.at(b, "scaled", 1))
                    dve.tensor_scalar(r[:].rearrange("p (n t) -> p n t", n=NT), ps[:, :, 0:TW], EPS, None,
                                      ALU.add).then_inc(v.sem, 1)
                    dve.wait_ge(a.sem, a.at(b, "root"))
                    dve.reciprocal(r[:], r[:]).then_inc(v.sem, 1)
                    dve.wait_ge(v.sem, v.at(b, "inverse"))
                    x = one(act_out, b)
                    dve.scalar_tensor_tensor(x, x, scale, r[:], ALU.mult, ALU.mult).then_inc(v.sem, 1)


GDN_PE = ["rows", "k", "v", "kk", "qk", "mt", "m2", "m2t", "m4", "m4t", "r1", "m8", "r2", "r3",
          "td", "y", "yt", "y2", "y2t", "y4", "z1", "z2", "tt", "u", "wk", "w", "o", "ds"]
GDN_DVE = ["diff_t", "masked_t", "diff", "masked", "kb", "kbg", "kd", "vb", "qkt", "qg",
           "mk", "m", "m16", "lm", "r0", "m2t", "m4t", "r1", "r2", "r3", "yt", "vv", "y2t", "z1", "z2", "u", "w",
           "s_decayed", "s"]
GDN_ACT = ["rows_st", "cols", "ecol", "ercol", "eb", "dec_t", "dec", "mt", "m2", "m4", "m8", "td", "y", "y2", "y4", "tt",
           "wk", "o"]
GDN_POOL = ["k_st", "v_st"]
SAMPLE_ONLY_OUT = {"m8", "r3", "td", "y", "yt", "y2", "y2t", "y4", "z1", "z2", "tt", "vv", "lm", "m4t", "m16"}


def gdn_phase(nc, io, act_out, rows, g_dram, masks, sampled, slots_dram=None):
    L = TS if sampled else CH
    rounds = 1 if sampled else NCH
    tag = "ds" if sampled else "dp"
    with ExitStack() as stack:
        m = Memory(nc, stack)
        out = SAMPLE_ONLY_OUT if sampled else set()
        names_p = [x for x in GDN_PE if x not in out]
        names_v = [x for x in GDN_DVE if x not in out]
        names_a = [x for x in GDN_ACT if x not in out]
        if sampled:
            names_p = names_p[:names_p.index("w")] + ["w_state", "w_turned", "o", "o_state"] + [
                f"ds{h}" for h in range(HA)]
            names_v = names_v[:names_v.index("w")] + ["w", "o"] + [
                f"{x}{h}" for h in range(HA) for x in ("spread", "decayed", "s")]
            names_a = names_a[:-1] + ["w_state", "o_state"]
        p, v, a = Steps(m, tag + "_pe", names_p), Steps(m, tag + "_dve", names_v), Steps(m, tag + "_act", names_a)
        q = Steps(m, tag + "_pool", GDN_POOL)
        gb_loaded, state_loaded, state_out = m.sem(tag + "_gb"), m.sem(tag + "_state"), m.sem(tag + "_out")

        def sb(name, shape):
            return m.sb(f"{tag}_{name}", shape)

        heads = [L, HA, L]
        kst, vst = sb("kst", [P, HA, L]), sb("vst", [P, HA, L])
        rst = sb("rst", [P, 3, L])
        gb, eb = sb("gb", [P, HA, L]), sb("eb", [P, HA, L])
        cols, ecol, ercol, kb = sb("cols", [L, 3, 64]), sb("ecol", [L, NR]), sb("ercol", [L, NR]), sb("kb", [L, HA])
        diff_t, diff = sb("difft", heads), sb("diff", heads)
        kbg, kd, vb = sb("kbg", [L, HA, DK]), sb("kd", [L, HA, DK]), sb("vb", [L, HA, DK])
        qkt, qg = sb("qkt", heads), sb("qg", [P, HA, L])
        M = sb("m", heads)
        M16 = M if sampled else sb("m16", heads)
        mt, r0, r1, r2 = sb("mt", heads), sb("r0", heads), sb("r1", heads), sb("r2", heads)
        m2, m2t, m4 = sb("m2", heads), sb("m2t", heads), sb("m4", heads)
        if not sampled:
            lm, m4t, m8, r3, td = sb("lm", heads), sb("m4t", heads), sb("m8", heads), sb("r3", heads), sb("td", heads)
            y, yt, vv, y2, y2t = sb("y", heads), sb("yt", heads), sb("vv", heads), sb("y2", heads), sb("y2t", heads)
            y4, z1, z2, tt = sb("y4", heads), sb("z1", heads), sb("z2", heads), sb("tt", heads)
            S = sb("s", [P, HA, DK])
            S1 = sb("s1", [P, HA, DK])
            zeros = sb("zeros", [P, D])
            zeros_set, zeros_sent = m.sem(tag + "_zeroset"), m.sem(tag + "_zerosent")
            zero_tiles = slots_dram.rearrange("(c n p) d -> c p n d", p=P, c=NCH)
        else:
            tt = r2
            S = sb("s", [P, NSEQ, HA, DK])
            S1 = sb("s1", [P, 2, NSEQ, DK])
            wst, ost = sb("wst", [P, HA, L]), sb("ost", [P, HA, L])
            spread = sb("spread", [L, 2, NSEQ, DK])
        U, wk, w = sb("u", [L, HA, DK]), sb("wk", [P, HA, L]), sb("w", [L, HA, DK])
        bank = [m.ps(f"{tag}_ps{i}", [P, 512]) for i in range(8)]

        def sq_(i):
            return bank[i][0:L, 0:HA * L].rearrange("p (h t) -> p h t", h=HA)

        def wide(i):
            return bank[i][0:L, :].rearrange("p (h t) -> p h t", h=HA)

        def tall(i):
            return bank[i][:, 0:HA * L].rearrange("p (h t) -> p h t", h=HA)

        ident = masks[0:L, 0, 0:L]
        neg_t, neg = (masks[0:L, 4, 0:L], masks[0:L, 5, 0:L]) if sampled else (masks[0:L, 1, 0:L], masks[0:L, 2, 0:L])
        same16 = masks[0:L, 3, 0:L]
        col_g, col_b = cols[:, 0, ROW_G:ROW_G + HA], cols[:, 0, 0:HA]

        def over_heads(mask):
            return mask.unsqueeze(1).to_broadcast(heads)

        def tokens(ap, c):
            return ap[:, :, TP:T] if sampled else ap[:, :, bass.ds(c * CH, CH)]

        def loop(eng):
            return eng.Fori(0, NCH)

        block = stack.enter_context(nc.Block())

        @block.sync
        def _(sp):
            if sampled:
                sp.dma_start(S[:], io["state_gdn"]).then_inc(state_loaded, 16)
                sp.dma_start(gb[:], g_dram[0:HA, TP:T].partition_broadcast(P)).then_inc(gb_loaded, 16)
                sp.wait_ge(v.sem, v.at(0, f"s{HA - 1}"))
                sp.dma_start(io["new_gdn_s"], S[:]).then_inc(state_out, 16)
            else:
                sp.wait_ge(zeros_set, 1)
                with loop(sp) as c:
                    sp.wait_ge(v.sem, v.at(c, "diff", 1))
                    sp.wait_ge(a.sem, a.at(c, "eb", 1))
                    sp.dma_start(gb[:], g_dram[0:HA, bass.ds(c * CH, CH)].partition_broadcast(P)
                                 ).then_inc(gb_loaded, 16)
                    sp.dma_start(zero_tiles[bass.ds(c, 1)].rearrange("c p n d -> (c p) n d"),
                                 zeros[:].unsqueeze(1).to_broadcast([P, zero_tiles.shape[2], D])
                                 ).then_inc(zeros_sent, 16)
                sp.wait_ge(zeros_sent, 16 * NCH)
                sp.wait_ge(v.sem, v.at(NCH - 1, "s"))
                sp.dma_start(io["new_gdn_p"], S[:]).then_inc(state_out, 16)
            sp.wait_ge(state_out, 16)

        @block.gpsimd
        def _(pool):
            q.start(pool)

            def chunk(c):
                pool.wait_ge(p.sem, p.at(c, "qk", 1))
                pool.tensor_copy(kst[:], tokens(act_out[:, HA:2 * HA], c)).then_inc(q.sem, 1)
                pool.tensor_copy(vst[:], tokens(act_out[:, 2 * HA:3 * HA], c)).then_inc(q.sem, 1)

            if sampled:
                chunk(0)
            else:
                with loop(pool) as c:
                    chunk(c)

        @block.scalar
        def _(act):
            a.start(act)

            def wait(steps, c, name, back=0):
                act.wait_ge(steps.sem, steps.at(c, name, back))

            def copy(dst, src):
                act.copy(dst, src).then_inc(a.sem, 1)

            def exp(dst, src):
                act.activation(dst, src, ACT.Exp).then_inc(a.sem, 1)

            def chunk(c):
                wait(p, c, "rows", 1)
                for i, row in enumerate(rows):
                    src = row[:, TP:T] if sampled else row[:, bass.ds(c * CH, CH)]
                    ins = act.copy(rst[:, i, :], src)
                ins.then_inc(a.sem, 1)
                wait(p, c, "rows")
                wait(v, c, "m", 1)
                copy(cols[:], bank[0][0:L, 0:3 * P].rearrange("p (r c) -> p r c", r=3)[:, :, 0:64])
                wait(a, c, "cols")
                exp(ecol[:], cols[:, 0, ROW_G:ROW_G + NR])
                exp(ercol[:], cols[:, 1, ROW_G:ROW_G + NR])
                act.wait_ge(gb_loaded, c * 16 + 16)
                if not sampled:
                    wait(v, c, "s_decayed", 1)
                exp(eb[:], gb[:])
                wait(v, c, "masked_t")
                exp(diff_t[:], diff_t[:])
                wait(v, c, "masked")
                exp(diff[:], diff[:])
                wait(p, c, "mt")
                copy(mt[:], sq_(5))
                wait(p, c, "m2")
                copy(m2[:], sq_(6))
                wait(p, c, "m4")
                copy(m4[:], sq_(6))
                if not sampled:
                    wait(p, c, "m8")
                    copy(m8[:], sq_(6))
                    wait(p, c, "td")
                    copy(td[:], sq_(6))
                    wait(p, c, "y")
                    copy(y[:], sq_(7))
                    wait(p, c, "y2")
                    copy(y2[:], sq_(6))
                    wait(p, c, "y4")
                    copy(y4[:], sq_(6))
                    wait(p, c, "tt")
                    copy(tt[:], sq_(6))
                wait(p, c, "wk")
                act.mul(wk[:], tall(7), -1.0).then_inc(a.sem, 1)
                if not sampled:
                    wait(p, c, "o")
                    copy(tokens(act_out[:, 0:HA], c), tall(1))
                else:
                    wait(p, c, "w_state")
                    copy(wst[:], tall(0))
                    wait(p, c, "o_state")
                    copy(ost[:], tall(4))

            if sampled:
                chunk(0)
            else:
                with loop(act) as c:
                    chunk(c)

        @block.vector
        def _(dve):
            v.start(dve)
            if not sampled:
                dve.memset(S[:], 0.0).then_inc(state_loaded, 16)
                dve.memset(zeros[:], 0.0).then_inc(zeros_set, 1)

            def wait(steps, c, name, back=0):
                dve.wait_ge(steps.sem, steps.at(c, name, back))

            def tt_(dst, x, z, op):
                dve.tensor_tensor(dst, x, z, op).then_inc(v.sem, 1)

            def chunk(c):
                dve.wait_ge(gb_loaded, c * 16 + 16)
                wait(a, c, "cols")
                wait(v, c, "qkt", 1)
                g = bc(col_g, L)
                tt_(diff_t[:], gb[0:L], g, ALU.subtract)
                wait(v, c, "diff_t")
                tt_(diff_t[:], diff_t[:], over_heads(neg_t), ALU.add)
                tt_(diff[:], g, gb[0:L], ALU.subtract)
                wait(v, c, "diff")
                tt_(diff[:], diff[:], over_heads(neg), ALU.add)
                wait(a, c, "ecol")
                tt_(kb[:], col_b, ecol[:, 0:HA], ALU.mult)
                wait(v, c, "kb")
                wait(p, c, "k")
                tt_(kbg[:], wide(1), bc(kb[:], DK), ALU.mult)
                wait(a, c, "ercol")
                tt_(kd[:], wide(1), bc(ercol[:, 0:HA], DK), ALU.mult)
                wait(p, c, "v")
                tt_(vb[:], wide(2), bc(col_b, DK), ALU.mult)
                wait(a, c, "dec_t")
                wait(p, c, "qk")
                tt_(qkt[:], sq_(4), diff_t[:], ALU.mult)
                wait(a, c, "eb")
                tt_(qg[:], tokens(act_out[:, 0:HA], c), eb[:], ALU.mult)
                wait(a, c, "dec")
                wait(p, c, "kk")
                dve.scalar_tensor_tensor(M[:], sq_(3), -1.0, diff[:], ALU.mult, ALU.mult).then_inc(v.sem, 1)
                wait(v, c, "mk")
                tt_(M[:], M[:], bc(col_b, L), ALU.mult)
                wait(v, c, "m")
                if not sampled:
                    tt_(M16[:], M[:], over_heads(same16), ALU.mult)
                    wait(v, c, "m16")
                    tt_(lm[:], M[:], M16[:], ALU.subtract)
                wait(a, c, "mt")
                tt_(r0[:], mt[:], over_heads(ident), ALU.add)
                wait(p, c, "m2t")
                dve.tensor_copy(m2t[:], sq_(7)).then_inc(v.sem, 1)
                if not sampled:
                    wait(p, c, "m4t")
                    dve.tensor_copy(m4t[:], sq_(7)).then_inc(v.sem, 1)
                wait(p, c, "r1")
                tt_(r1[:], sq_(5), r0[:], ALU.add)
                wait(v, c, "r1")
                wait(p, c, "r2")
                tt_(r2[:], sq_(7), r1[:], ALU.add)
                if not sampled:
                    wait(v, c, "r2")
                    wait(p, c, "r3")
                    tt_(r3[:], sq_(5), r2[:], ALU.add)
                    wait(p, c, "yt")
                    dve.tensor_copy(yt[:], sq_(5)).then_inc(v.sem, 1)
                    tt_(vv[:], sq_(5), over_heads(ident), ALU.add)
                    wait(p, c, "y2t")
                    dve.tensor_copy(y2t[:], sq_(7)).then_inc(v.sem, 1)
                    wait(p, c, "z1")
                    tt_(z1[:], sq_(5), vv[:], ALU.add)
                    wait(v, c, "z1")
                    wait(p, c, "z2")
                    tt_(z2[:], sq_(7), z1[:], ALU.add)
                wait(p, c, "u")
                dve.tensor_copy(U[:], wide(5)).then_inc(v.sem, 1)
                wait(v, c, "u")
                if not sampled:
                    wait(p, c, "w")
                    tt_(w[:], wide(0), U[:], ALU.add)
                    wait(p, c, "o")
                    tt_(S1[:], S[:], eb[:, :, L - 1:L].to_broadcast([P, HA, DK]), ALU.mult)
                    wait(v, c, "s_decayed")
                    wait(p, c, "ds")
                    tt_(S[:], bank[3][:].rearrange("p (h t) -> p h t", h=HA), S1[:], ALU.add)
                else:
                    wait(p, c, "w_turned")
                    tt_(w[:], wide(1), U[:], ALU.add)
                    wait(a, c, "o_state")
                    wait(p, c, "o")
                    tt_(act_out[:, 0:HA, TP:T], tall(2), ost[:], ALU.add)
                    wait(v, c, "w")
                    for h in range(HA):
                        seq = masks[0:TS, 6, 0:NSEQ].unsqueeze(2).to_broadcast([TS, NSEQ, DK])
                        if h >= 2:
                            wait(p, c, f"ds{h - 2}")
                        tt_(spread[:, h % 2], w[:, h, :].unsqueeze(1).to_broadcast([TS, NSEQ, DK]), seq, ALU.mult)
                        if h >= 2:
                            wait(v, c, f"s{h - 2}")
                        last = eb[:, h, :].rearrange("p (b t) -> p b t", t=LSEQ)[:, :, LSEQ - 1:LSEQ]
                        tt_(S1[:, h % 2], S[:, :, h, :], last.to_broadcast([P, NSEQ, DK]), ALU.mult)
                        wait(v, c, f"decayed{h}")
                        wait(p, c, f"ds{h}")
                        for half in range(2):
                            ins = dve.tensor_tensor(
                                S[:, 4 * half:4 * half + 4, h, :],
                                bank[(h % 2) * 2 + 4 + half][:].rearrange("p (b t) -> p b t", t=DK),
                                S1[:, h % 2, 4 * half:4 * half + 4], ALU.add)
                        ins.then_inc(v.sem, 1)

            if sampled:
                dve.wait_ge(state_loaded, 16)
                chunk(0)
            else:
                dve.wait_ge(state_loaded, 16)
                with loop(dve) as c:
                    chunk(c)

        @block.tensor
        def _(pe):
            p.start(pe)

            def wait(steps, c, name, back=0):
                pe.wait_ge(steps.sem, steps.at(c, name, back))

            def each(dst, lhs, rhs):
                for h in range(HA):
                    mm = pe.matmul(dst[:, h, :], lhs(h), rhs(h), start=True, stop=True)
                mm.then_inc(p.sem, 1)

            def prod(dst, lhs, rhs):
                each(dst, lambda h: lhs[:, h, :], lambda h: rhs[:, h, :])

            def turn(dst, src, ident_):
                for h in range(HA):
                    mm = pe.transpose(dst[:, h, :], src[:, h, :], ident_)
                mm.then_inc(p.sem, 1)

            def chunk(c):
                full = masks[:, 0, :]
                wait(a, c, "rows_st")
                for i in range(3):
                    mm = pe.transpose(bank[0][0:L, i * P:(i + 1) * P], rst[:, i, :], full)
                mm.then_inc(p.sem, 1)
                wait(q, c, "k_st")
                wait(v, c, "kd", 1)
                wait(a, c, "o" if not sampled else "o_state", 1)
                turn(wide(1), kst, full)
                wait(q, c, "v_st")
                turn(wide(2), vst, full)
                wait(v, c, "s" if not sampled else f"s{HA - 1}", 1)
                prod(sq_(3), kst, kst)
                each(sq_(4), lambda h: kst[:, h, :],
                     lambda h: act_out[:, h, TP:T] if sampled else act_out[:, h, bass.ds(c * CH, CH)])
                wait(v, c, "m" if sampled else "m16")
                turn(sq_(5), M16, ident)
                wait(a, c, "mt")
                prod(sq_(6), mt, M16)
                prod(sq_(7), M16, mt)
                wait(a, c, "m2")
                wait(v, c, "m2t")
                prod(sq_(6), m2t, m2)
                if not sampled:
                    prod(sq_(7), m2, m2t)
                wait(v, c, "r0")
                prod(sq_(5), m2, r0)
                wait(a, c, "m4")
                if not sampled:
                    wait(v, c, "m4t")
                    prod(sq_(6), m4t, m4)
                wait(v, c, "r1")
                prod(sq_(7), m4, r1)
                if not sampled:
                    wait(a, c, "m8")
                    wait(v, c, "r2")
                    prod(sq_(5), m8, r2)
                    wait(v, c, "r3")
                    turn(sq_(6), r3, ident)
                    wait(v, c, "lm")
                    prod(sq_(7), r3, lm)
                    prod(sq_(5), lm, r3)
                    wait(a, c, "y")
                    wait(v, c, "vv")
                    wait(a, c, "td")
                    prod(sq_(6), yt, y)
                    prod(sq_(7), y, yt)
                    wait(a, c, "y2")
                    wait(v, c, "y2t")
                    prod(sq_(6), y2t, y2)
                    prod(sq_(5), y2, vv)
                    wait(a, c, "y4")
                    wait(v, c, "z1")
                    prod(sq_(7), y4, z1)
                    wait(v, c, "z2")
                    prod(sq_(6), td, z2)
                    wait(a, c, "tt")
                else:
                    wait(v, c, "r2")
                wait(v, c, "vb")
                prod(wide(5), tt, vb)
                wait(v, c, "kbg")
                prod(tall(7), kbg, tt)
                if not sampled:
                    pe.wait_ge(state_loaded, 16)
                    wait(a, c, "wk")
                    wait(v, c, "s", 1)
                    prod(wide(0), wk, S)
                    wait(v, c, "w")
                    wait(v, c, "qg")
                    for h in range(HA):
                        pe.matmul(tall(1)[:, h, :], S[:, h, :], qg[:, h, :], start=True, stop=False)
                        mm = pe.matmul(tall(1)[:, h, :], w[:, h, :], qkt[:, h, :], start=False, stop=True)
                    mm.then_inc(p.sem, 1)
                    prod(bank[3][:].rearrange("p (h t) -> p h t", h=HA), kd, w)
                else:
                    wait(a, c, "wk")
                    for dst, src in ((0, wk), (4, qg)):
                        if dst == 4:
                            wait(a, c, "w_state")
                            turn(wide(1), wst, full)
                            wait(v, c, "w")
                            prod(tall(2), w, qkt)
                        for h in range(HA):
                            for b in range(NSEQ):
                                cut = slice(b * LSEQ, (b + 1) * LSEQ)
                                mm = pe.matmul(tall(dst)[:, h, cut], S[:, b, h, :], src[:, h, cut],
                                               start=True, stop=True)
                        mm.then_inc(p.sem, 1)
                    wait(a, c, "o_state")
                    for h in range(HA):
                        wait(v, c, f"spread{h}")
                        if h >= 2:
                            wait(v, c, f"s{h - 2}")
                        for half in range(2):
                            mm = pe.matmul(bank[(h % 2) * 2 + 4 + half][:], kd[:, h, :],
                                           spread[:, h % 2, 4 * half:4 * half + 4, :].rearrange("p b t -> p (b t)"),
                                           start=True, stop=True)
                        mm.then_inc(p.sem, 1)

            if sampled:
                pe.wait_ge(state_loaded, 16)
                chunk(0)
            else:
                with loop(pe) as c:
                    chunk(c)


SSD_PE = ["rows", "bt", "xt", "cb", "y", "ds"]
SSD_DVE = ["diff_t", "masked_t", "xdt", "xdd", "cbt", "cs", "y", "s_decayed", "s"]
SSD_ACT = ["rows_st", "cols", "ercol", "bt", "eb", "dec_t"]
SSD_POOL = ["b_st", "x_st"]
AT_X, AT_B, AT_C = 3 * HA, 3 * HA + 4, 3 * HA + 6


def ssd_phase(nc, io, act_out, rows, g_dram, masks, sampled):
    L = TS if sampled else CH
    tag = "ss" if sampled else "sp"
    HPG = HB // GB
    W = HPG * PB
    with ExitStack() as stack:
        m = Memory(nc, stack)
        names_p, names_v, names_a = list(SSD_PE), list(SSD_DVE), list(SSD_ACT)
        if sampled:
            names_p = ["rows", "bt", "xt", "cb", "y", "y_state", "ds0", "ds1"]
            names_v = ["diff_t", "masked_t", "xdt", "xdd", "cbt", "cs", "spread", "y_skip", "y", "s_decayed", "s0", "s1"]
            names_a = names_a + ["y_state"]
        p, v, a = Steps(m, tag + "_pe", names_p), Steps(m, tag + "_dve", names_v), Steps(m, tag + "_act", names_a)
        q = Steps(m, tag + "_pool", SSD_POOL)
        gb_loaded, state_loaded, state_out = m.sem(tag + "_gb"), m.sem(tag + "_state"), m.sem(tag + "_out")
        const_loaded = m.sem(tag + "_const")

        def sb(name, shape):
            return m.sb(f"{tag}_{name}", shape)

        bst, xst, rst = sb("bst", [P, GB, L]), sb("xst", [P, 4, L]), sb("rst", [P, 3, L])
        gb, eb, cs = sb("gb", [P, HB, L]), sb("eb", [P, HB, L]), sb("cs", [P, HB, L])
        cols, ercol = sb("cols", [L, 3, 64]), sb("ercol", [L, NR])
        diff_t, cbt = sb("difft", [L, HB, L]), sb("cbt", [L, HB, L])
        bt, xdt, xdd = sb("bt", [L, GB, NB]), sb("xdt", [L, HB, PB]), sb("xdd", [L, HB, PB])
        skip = sb("skip", [P, 4])
        if sampled:
            S, S1 = sb("s", [P, NSEQ, HB, PB]), sb("s1", [P, NSEQ, HB, PB])
            spread, yst = sb("spread", [L, NSEQ, HB * PB]), sb("yst", [P, 4, L])
        else:
            S, S1 = sb("s", [P, HB, PB]), sb("s1", [P, HB, PB])
        bank = [m.ps(f"{tag}_ps{i}", [P, 512]) for i in range(8)]
        full, neg_t = masks[:, 0, :], masks[0:L, 4 if sampled else 1, 0:L]
        xt_ps = bank[2][0:L, :].rearrange("p (h t) -> p h t", t=PB)
        cb_ps = bank[3][0:L, 0:GB * L].rearrange("p (g t) -> p g t", g=GB)
        y_ps = bank[4][:, 0:4 * L].rearrange("p (n t) -> p n t", n=4)
        y_state_ps = bank[5][:, 0:4 * L].rearrange("p (n t) -> p n t", n=4)

        def tokens(ap, c):
            return ap[:, :, TP:T] if sampled else ap[:, :, bass.ds(c * CH, CH)]

        def run(eng, chunk):
            if sampled:
                chunk(0)
            else:
                with eng.Fori(0, NCH) as c:
                    chunk(c)

        block = stack.enter_context(nc.Block())

        @block.sync
        def _(sp):
            sp.dma_start(skip[:], io["d_skip"]).then_inc(const_loaded, 16)
            if sampled:
                sp.dma_start(S[:], io["state_ssd"]).then_inc(state_loaded, 16)
                sp.dma_start(gb[:], g_dram[HA:NR, TP:T].partition_broadcast(P)).then_inc(gb_loaded, 16)
                sp.wait_ge(v.sem, v.at(0, "s1"))
                sp.dma_start(io["new_ssd_s"], S[:]).then_inc(state_out, 16)
            else:
                with sp.Fori(0, NCH) as c:
                    sp.wait_ge(v.sem, v.at(c, "diff_t", 1))
                    sp.wait_ge(a.sem, a.at(c, "eb", 1))
                    sp.dma_start(gb[:], g_dram[HA:NR, bass.ds(c * CH, CH)].partition_broadcast(P)
                                 ).then_inc(gb_loaded, 16)
                sp.wait_ge(v.sem, v.at(NCH - 1, "s"))
                sp.dma_start(io["new_ssd_p"], S[:]).then_inc(state_out, 16)
            sp.wait_ge(state_out, 16)

        @block.gpsimd
        def _(pool):
            q.start(pool)

            def chunk(c):
                pool.wait_ge(p.sem, p.at(c, "cb", 1))
                pool.tensor_copy(bst[:], tokens(act_out[:, AT_B:AT_B + GB], c)).then_inc(q.sem, 1)
                pool.tensor_copy(xst[:], tokens(act_out[:, AT_X:AT_X + 4], c)).then_inc(q.sem, 1)

            run(pool, chunk)

        @block.scalar
        def _(act):
            a.start(act)

            def wait(steps, c, name, back=0):
                act.wait_ge(steps.sem, steps.at(c, name, back))

            def chunk(c):
                wait(p, c, "rows", 1)
                for i, row in enumerate(rows):
                    src = row[:, TP:T] if sampled else row[:, bass.ds(c * CH, CH)]
                    ins = act.copy(rst[:, i, :], src)
                ins.then_inc(a.sem, 1)
                wait(p, c, "rows")
                wait(v, c, "xdd", 1)
                act.copy(cols[:], bank[0][0:L, 0:3 * P].rearrange("p (r c) -> p r c", r=3)[:, :, 0:64]).then_inc(a.sem, 1)
                wait(a, c, "cols")
                act.activation(ercol[:], cols[:, 1, ROW_G:ROW_G + NR], ACT.Exp).then_inc(a.sem, 1)
                wait(p, c, "bt")
                act.copy(bt[:], bank[1][0:L, 0:GB * NB].rearrange("p (g s) -> p g s", g=GB)).then_inc(a.sem, 1)
                act.wait_ge(gb_loaded, c * 16 + 16)
                if not sampled:
                    wait(v, c, "s_decayed", 1)
                act.activation(eb[:], gb[:], ACT.Exp).then_inc(a.sem, 1)
                wait(v, c, "masked_t")
                act.activation(diff_t[:], diff_t[:], ACT.Exp).then_inc(a.sem, 1)
                if sampled:
                    wait(p, c, "y_state")
                    act.copy(yst[:], y_state_ps).then_inc(a.sem, 1)

            run(act, chunk)

        @block.vector
        def _(dve):
            v.start(dve)

            def wait(steps, c, name, back=0):
                dve.wait_ge(steps.sem, steps.at(c, name, back))

            def tt_(dst, x, z, op):
                dve.tensor_tensor(dst, x, z, op).then_inc(v.sem, 1)

            def chunk(c):
                dve.wait_ge(gb_loaded, c * 16 + 16)
                wait(a, c, "cols")
                wait(v, c, "cbt", 1)
                tt_(diff_t[:], gb[0:L], bc(cols[:, 0, ROW_G + HA:ROW_G + NR], L), ALU.subtract)
                wait(v, c, "diff_t")
                tt_(diff_t[:], diff_t[:], neg_t.unsqueeze(1).to_broadcast([L, HB, L]), ALU.add)
                wait(p, c, "xt")
                tt_(xdt[:], xt_ps, bc(cols[:, 2, ROW_G + HA:ROW_G + NR], PB), ALU.mult)
                wait(v, c, "xdt")
                wait(a, c, "ercol")
                tt_(xdd[:], xdt[:], bc(ercol[:, HA:NR], PB), ALU.mult)
                wait(p, c, "cb")
                wait(a, c, "dec_t")
                for g in range(GB):
                    ins = dve.tensor_tensor(cbt[:, g * HPG:(g + 1) * HPG, :],
                                            cb_ps[:, g:g + 1, :].to_broadcast([L, HPG, L]),
                                            diff_t[:, g * HPG:(g + 1) * HPG, :], ALU.mult)
                ins.then_inc(v.sem, 1)
                wait(a, c, "eb")
                for g in range(GB):
                    cg = tokens(act_out[:, AT_C + g:AT_C + g + 1], c)
                    ins = dve.tensor_tensor(cs[:, g * HPG:(g + 1) * HPG, :], cg.to_broadcast([P, HPG, L]),
                                            eb[:, g * HPG:(g + 1) * HPG, :], ALU.mult)
                ins.then_inc(v.sem, 1)
                if sampled:
                    wait(v, c, "xdd")
                    seq = masks[0:TS, 6, 0:NSEQ].unsqueeze(2).to_broadcast([TS, NSEQ, HB * PB])
                    flat = xdd[:].rearrange("p h t -> p (h t)").unsqueeze(1).to_broadcast([TS, NSEQ, HB * PB])
                    tt_(spread[:], flat, seq, ALU.mult)
                wait(p, c, "y")
                for n in range(4):
                    x = tokens(act_out[:, AT_X + n:AT_X + n + 1], c)
                    ins = dve.scalar_tensor_tensor(x, x, skip[:, n:n + 1], y_ps[:, n:n + 1, :], ALU.mult, ALU.add)
                ins.then_inc(v.sem, 1)
                if sampled:
                    wait(a, c, "y_state")
                    wait(v, c, "y_skip")
                    x = act_out[:, AT_X:AT_X + 4, TP:T]
                    tt_(x, x, yst[:], ALU.add)
                    last = eb[:].rearrange("p h (b t) -> p b h t", t=LSEQ)[:, :, :, LSEQ - 1:LSEQ]
                    tt_(S1[:], S[:], last.to_broadcast([P, NSEQ, HB, PB]), ALU.mult)
                    wait(v, c, "s_decayed")
                    for g in range(GB):
                        wait(p, c, f"ds{g}")
                        for j in range(4):
                            b = (4 * g + j) % 8
                            ins = dve.tensor_tensor(
                                S[:, 2 * j:2 * j + 2, g * HPG:(g + 1) * HPG, :],
                                bank[b][:].rearrange("p (b h t) -> p b h t", b=2, t=PB),
                                S1[:, 2 * j:2 * j + 2, g * HPG:(g + 1) * HPG, :], ALU.add)
                        ins.then_inc(v.sem, 1)
                else:
                    tt_(S1[:], S[:], eb[:, :, L - 1:L].to_broadcast([P, HB, PB]), ALU.mult)
                    wait(v, c, "s_decayed")
                    wait(p, c, "ds")
                    tt_(S[:], bank[5][:].rearrange("p (h t) -> p h t", t=PB), S1[:], ALU.add)

            dve.wait_ge(const_loaded, 16)
            if not sampled:
                dve.memset(S[:], 0.0).then_inc(state_loaded, 16)
            dve.wait_ge(state_loaded, 16)
            run(dve, chunk)

        @block.tensor
        def _(pe):
            p.start(pe)

            def wait(steps, c, name, back=0):
                pe.wait_ge(steps.sem, steps.at(c, name, back))

            def chunk(c):
                wait(a, c, "rows_st")
                wait(a, c, "cols", 1)
                for i in range(3):
                    mm = pe.transpose(bank[0][0:L, i * P:(i + 1) * P], rst[:, i, :], full)
                mm.then_inc(p.sem, 1)
                wait(q, c, "b_st")
                wait(a, c, "bt", 1)
                for g in range(GB):
                    mm = pe.transpose(bank[1][0:L, g * NB:(g + 1) * NB], bst[:, g, :], full)
                mm.then_inc(p.sem, 1)
                wait(q, c, "x_st")
                wait(v, c, "cbt", 1)
                for n in range(4):
                    mm = pe.transpose(bank[2][0:L, n * P:(n + 1) * P], xst[:, n, :], full)
                mm.then_inc(p.sem, 1)
                for g in range(GB):
                    cg = act_out[:, AT_C + g, TP:T] if sampled else act_out[:, AT_C + g, bass.ds(c * CH, CH)]
                    mm = pe.matmul(cb_ps[:, g, :], bst[:, g, :], cg, start=True, stop=True)
                mm.then_inc(p.sem, 1)
                wait(v, c, "cs")
                wait(v, c, "s" if not sampled else "s1", 1)
                for h in range(HB):
                    half = slice((h % 2) * PB, (h % 2 + 1) * PB)
                    mm = pe.matmul(y_ps[half, h // 2, :], xdt[:, h, :], cbt[:, h, :], start=True, stop=sampled)
                    if not sampled:
                        mm = pe.matmul(y_ps[half, h // 2, :], S[:, h, :], cs[:, h, :], start=False, stop=True)
                mm.then_inc(p.sem, 1)
                wait(a, c, "bt")
                if not sampled:
                    for g in range(GB):
                        mm = pe.matmul(bank[5][:, g * W:(g + 1) * W], bt[:, g, :],
                                       xdd[:, g * HPG:(g + 1) * HPG, :].rearrange("p h t -> p (h t)"),
                                       start=True, stop=True)
                    mm.then_inc(p.sem, 1)
                else:
                    for h in range(HB):
                        half = slice((h % 2) * PB, (h % 2 + 1) * PB)
                        for b in range(NSEQ):
                            cut = slice(b * LSEQ, (b + 1) * LSEQ)
                            mm = pe.matmul(y_state_ps[half, h // 2, cut], S[:, b, h, :], cs[:, h, cut],
                                           start=True, stop=True)
                    mm.then_inc(p.sem, 1)
                    wait(v, c, "spread")
                    wait(v, c, "y")
                    for g in range(GB):
                        for j in range(4):
                            mm = pe.matmul(bank[4 * g + j][:], bt[:, g, :],
                                           spread[:, 2 * j:2 * j + 2, g * W:(g + 1) * W], start=True, stop=True)
                        mm.then_inc(p.sem, 1)

            pe.wait_ge(state_loaded, 16)
            run(pe, chunk)


def gate_phase(nc, io, act_out, ones, z_dram, yc_dram):
    AT_ZA, AT_YC, AT_ZB = HA, 2 * HA, AT_B
    with ExitStack() as stack:
        m = Memory(nc, stack)
        ow, yw = m.sb("m_ow", [P, 1]), m.sb("m_yw", [P, 4])
        sq = m.sb("m_sq", [P, 2, T])
        r = m.sb("m_r", [P, T])
        ps = m.ps("m_ps", [P, NT, 512])
        loaded = m.sem("m_loaded")
        a, p = Steps(m, "m_act", ["square", "root"]), Steps(m, "m_pe", ["sum"])
        v = Steps(m, "m_dve", ["gated", "mean", "inverse", "weighted", "scaled"])
        block = stack.enter_context(nc.Block())
        tiled = r[:].rearrange("p (n t) -> p n t", n=NT)

        @block.sync
        def _(sp):
            sp.dma_start(ow[:], io["onorm_a"]).then_inc(loaded, 16)
            sp.dma_start(yw[:], io["onorm_b"]).then_inc(loaded, 16)
            sp.dma_start(act_out[:, AT_ZA:AT_ZA + 4, :], z_dram[0:4].rearrange("a p t -> p a t")).then_inc(loaded, 16)
            sp.dma_start(act_out[:, AT_ZB:AT_ZB + 4, :], z_dram[4:8].rearrange("a p t -> p a t")).then_inc(loaded, 16)
            sp.dma_start(act_out[:, AT_YC:AT_YC + 4, :], yc_dram.rearrange("a p t -> p a t")).then_inc(loaded, 16)
            sp.wait_ge(loaded, 80)

        def members(c):
            return [c] if c < HA else [AT_X + 2 * (c - HA), AT_X + 2 * (c - HA) + 1]

        @block.scalar
        def _(act):
            a.start(act)
            act.wait_ge(loaded, 80)
            for c in range(HA + GB):
                act.wait_ge(p.sem, p.at(c, "sum", 1))
                if c >= HA:
                    act.wait_ge(v.sem, v.at(c, "gated"))
                for j, b in enumerate(members(c)):
                    ins = act.activation(sq[:, j, :], act_out[:, b, :], ACT.Square)
                ins.then_inc(a.sem, 1)
                act.wait_ge(v.sem, v.at(c, "mean"))
                act.activation(r[:], r[:], ACT.Sqrt).then_inc(a.sem, 1)

        @block.tensor
        def _(pe):
            p.start(pe)
            for c in range(HA + GB):
                pe.wait_ge(a.sem, a.at(c, "square"))
                pe.wait_ge(v.sem, v.at(c, "mean", 1))
                n_in = len(members(c))
                for n in range(NT):
                    for j in range(n_in):
                        mm = pe.matmul(ps[:, n, 0:TW], ones[:], sq[:, j, n * TW:(n + 1) * TW],
                                       start=(j == 0), stop=(j == n_in - 1))
                mm.then_inc(p.sem, 1)

        @block.vector
        def _(dve):
            v.start(dve)
            dve.wait_ge(loaded, 80)
            for c in range(HA + GB):
                ms = members(c)
                if c >= HA:
                    for j, b in enumerate(ms):
                        ins = dve.tensor_tensor(act_out[:, b, :], act_out[:, b, :],
                                                act_out[:, AT_ZB + b - AT_X, :], ALU.mult)
                    ins.then_inc(v.sem, 1)
                else:
                    z = act_out[:, AT_ZA + c, :]
                    dve.tensor_scalar(z, z, ow[:, 0:1], None, ALU.mult).then_inc(v.sem, 1)
                dve.wait_ge(p.sem, p.at(c, "sum"))
                dve.wait_ge(v.sem, v.at(c, "scaled", 1))
                dve.tensor_scalar(tiled, ps[:, :, 0:TW], 1.0 / (P * len(ms)), EPS, ALU.mult, ALU.add).then_inc(v.sem, 1)
                dve.wait_ge(a.sem, a.at(c, "root"))
                dve.reciprocal(r[:], r[:]).then_inc(v.sem, 1)
                for j, b in enumerate(ms):
                    w = act_out[:, AT_ZA + c, :] if c < HA else yw[:, b - AT_X:b - AT_X + 1].to_broadcast([P, T])
                    ins = dve.tensor_tensor(act_out[:, b, :], act_out[:, b, :], w, ALU.mult)
                ins.then_inc(v.sem, 1)
                dve.wait_ge(v.sem, v.at(c, "weighted"))
                for b in ms:
                    ins = dve.tensor_tensor(act_out[:, b, :], act_out[:, b, :], r[:], ALU.mult)
                ins.then_inc(v.sem, 1)
        return list(range(HA)) + list(range(AT_X, AT_X + 4)) + list(range(AT_YC, AT_YC + 4))


def out_projection_phase(nc, io, act_out, mixed, x2):
    with ExitStack() as stack:
        m = Memory(nc, stack)
        w = m.sb("o_w", [P, 2, NMIX, P])
        ps = m.ps("o_ps", [P, 2, NT, 512])
        x_loaded = m.sem("o_x")
        w_loaded = [m.sem(f"o_w{h}") for h in range(2)]
        done = [m.sem(f"o_pe{h}") for h in range(2)]
        added = [m.sem(f"o_dve{h}") for h in range(2)]
        block = stack.enter_context(nc.Block())

        @block.sync
        def _(sp):
            sp.dma_start(w[:, 0], io["w_out"][0]).then_inc(w_loaded[0], 16)
            sp.dma_start(w[:, 1], io["w_out"][1]).then_inc(w_loaded[1], 16)
            sp.dma_start(x2[:], io["xT"]).then_inc(x_loaded, 16)
            with sp.Fori(0, KD // 2 - 1) as i:
                for h in range(2):
                    sp.wait_ge(done[h], i + 1)
                    sp.dma_start(w[:, h], io["w_out"][bass.ds(i * 2 + (2 + h), 1)].rearrange(
                        "a p k c -> (a p) k c")).then_inc(w_loaded[h], 16)

        @block.tensor
        def _(pe):
            with pe.Fori(0, KD // 2) as i:
                for h in range(2):
                    pe.wait_ge(w_loaded[h], i * 16 + 16)
                    pe.wait_ge(added[h], i + 1)
                    for n in range(NT):
                        for k in range(NMIX):
                            mm = pe.matmul(ps[:, h, n, 0:TW], w[:, h, k, :], act_out[:, mixed[k], n * TW:(n + 1) * TW],
                                           start=(k == 0), stop=(k == NMIX - 1))
                    mm.then_inc(done[h], 1)

        @block.vector
        def _(dve):
            for h in range(2):
                dve.sem_inc(added[h], 1)
            dve.wait_ge(x_loaded, 16)
            with dve.Fori(0, KD // 2) as i:
                for h in range(2):
                    dve.wait_ge(done[h], i + 1)
                    x = one(x2, i * 2 + h).rearrange("p (n t) -> p n t", n=NT)
                    dve.tensor_tensor(x, x, ps[:, h, :, 0:TW], ALU.add).then_inc(added[h], 1)


RT, RL = 12, T // 12
BLK = 256
NBLK = (TOPK * T - NE) // BLK + NE
SLOTS = NBLK * BLK


def transpose_x_phase(nc, x2t, x2, masks):
    with ExitStack() as stack:
        m = Memory(nc, stack)
        ps = m.ps("t_ps", [P, 4, 512])
        turned, copied = m.sem("t_turned"), m.sem("t_copied")
        block = stack.enter_context(nc.Block())

        @block.tensor
        def _(pe):
            for t in range(RT):
                for half in range(2):
                    r = 2 * t + half
                    if r >= 4:
                        pe.wait_ge(copied, r - 3)
                    for k in range(4):
                        mm = pe.transpose(ps[0:RL, r % 4, k * P:(k + 1) * P],
                                          x2t[:, half * 4 + k, t * RL:(t + 1) * RL], masks[:, 0, :])
                    mm.then_inc(turned, 1)

        @block.vector
        def _(dve):
            for t in range(RT):
                for half in range(2):
                    r = 2 * t + half
                    dve.wait_ge(turned, r + 1)
                    if r % 2:
                        dve.wait_ge(copied, r)
                        dve.tensor_copy(x2[:, t, half * 512:(half + 1) * 512], ps[0:RL, r % 4, :]).then_inc(copied, 1)

        @block.scalar
        def _(act):
            for t in range(RT):
                r = 2 * t
                act.wait_ge(turned, r + 1)
                if r:
                    act.wait_ge(copied, r)
                act.copy(x2[:, t, 0:512], ps[0:RL, r % 4, :]).then_inc(copied, 1)


def routing_phase(nc, io, x2t, x2, wts, idx, expert_of, masks, ones, slots_dram, x2_dram):
    with ExitStack() as stack:
        m = Memory(nc, stack)
        NL = NG + NE
        w2c, w2r = m.sb("r_w2c", [P, KD]), m.sb("r_w2r", [P, D])
        wr, consts = m.sb("r_w", [P, KD, NL]), m.sb("r_consts", [NE, io["route_consts"].shape[1]])
        xw = m.sb("r_xw", [P, 2, T])
        lt = m.sb("r_lt", [NL, T])
        lg = m.sb("r_lg", [RL, RT, NL])
        h2 = m.sb("r_h2", [RL, 4, D])
        junk = m.sb("r_junk", [RL, D])
        rs = m.sb("r_rs", [RL, RT, 1])

        def sb(name, *shape):
            return m.sb("r_" + name, [RL, RT, *shape])

        mx, e, s, pt, eq, hot, left = (sb("mx", 1), sb("e", NG), sb("s", 1), sb("pt", 1), sb("eq", NG),
                                       sb("hot", NG), sb("left", 1))
        prod, ls = sb("prod", NG, EPG), sb("ls", EPG)
        hots = [sb("hot1", EPG), sb("hot2", EPG)]
        vals = [sb("v1", 1), sb("v2", 1)]
        both = [sb("both1", NG, EPG), sb("both2", NG, EPG)]
        sel, slot_t, slot_f = sb("sel", NE), sb("slott", NE), sb("slotf", TOPK)
        sel_rows, pos = m.sb("r_selrows", [NE, T]), m.sb("r_pos", [NE, T])
        one_rows = m.sb("r_onerows", [NE, T])
        gt, n_blocks, base = m.sb("r_gt", [NE, 8]), m.sb("r_nblocks", [NE, 1]), m.sb("r_base", [NE, 1])
        ended, owner = m.sb("r_ended", [NE, NBLK + 1]), m.sb("r_owner", [1, NBLK + 1])
        ps = m.ps("r_ps", [P, NT, 512])
        ps2, ps3 = m.ps("r_ps2", [P, 512]), m.ps("r_ps3", [P, NT, 512])
        loaded, xw_s, summed, pe_s, dve_s = m.sem("r_l"), m.sem("r_xw"), m.sem("r_summed"), m.sem("r_pe"), m.sem("r_dve")
        ready, back, squares = m.sem("r_ready"), m.sem("r_back"), m.sem("r_squares")
        x2_sent = m.sem("r_x2sent")
        h2_ready, sent = m.sem("r_h2s"), [m.sem(f"r_sent{i}") for i in range(4)]
        block = stack.enter_context(nc.Block())
        thresholds, block_ids, upto = consts[:, 0:8], consts[:, 8:9 + NBLK], consts[:, 9 + NBLK:9 + NBLK + NE]
        per = RT // NT

        @block.sync
        def _(sp):
            sp.dma_start(x2_dram.rearrange("(t p) d -> p t d", p=RL), x2).then_inc(x2_sent, 16)
            sp.dma_start(w2c[:], io["norm2_w"]).then_inc(loaded, 16)
            sp.dma_start(w2r[:], io["norm2_row"].partition_broadcast(P)).then_inc(loaded, 16)
            sp.dma_start(wr[:], io["w_router"]).then_inc(loaded, 16)
            sp.dma_start(consts[:], io["route_consts"]).then_inc(loaded, 16)
            sp.wait_ge(x2_sent, 16)

        @block.tensor
        def _(pe):
            pe.wait_ge(loaded, 64)
            for k in range(KD):
                pe.wait_ge(xw_s, k + 1)
                for n in range(NT):
                    mm = pe.matmul(ps[0:NL, n, 0:TW], wr[:, k, :], xw[:, k % 2, n * TW:(n + 1) * TW],
                                   start=(k == 0), stop=(k == KD - 1))
                mm.then_inc(summed, 1)
            pe.wait_ge(back, 1)
            for t in range(RT):
                mm = pe.transpose(ps2[0:RL, t * NL:(t + 1) * NL], lt[:, t * RL:(t + 1) * RL], masks[0:NL, 0, 0:NL])
            mm.then_inc(pe_s, 1)
            pe.wait_ge(ready, 3)
            for t in range(RT):
                mm = pe.transpose(ps3[0:NE, t // per, (t % per) * RL:(t % per + 1) * RL],
                                  sel[:, t, :], masks[0:RL, 0, 0:RL])
            mm.then_inc(pe_s, 1)
            pe.wait_ge(ready, 4)
            pe.matmul(ps[0:NE, 0, 0:1], upto, n_blocks[:], start=True, stop=True).then_inc(pe_s, 1)
            pe.wait_ge(ready, 5)
            pe.matmul(ps[0:1, 1, 0:NBLK + 1], ones[0:NE, 0:1], ended[:], start=True, stop=True).then_inc(pe_s, 1)
            pe.wait_ge(ready, 6)
            for t in range(RT):
                mm = pe.transpose(ps2[0:RL, t * NE:(t + 1) * NE], pos[:, t * RL:(t + 1) * RL], masks[0:NE, 0, 0:NE])
            mm.then_inc(pe_s, 1)

        @block.scalar
        def _(act):
            for t in range(RT):
                if t:
                    act.wait_ge(squares, t)
                act.activation(junk[:], x2[:, t, :], ACT.Square, accum_out=rs[:, t, :]).then_inc(squares, 1)
            act.wait_ge(squares, RT + 1)
            act.activation(rs[:], rs[:], ACT.Sqrt).then_inc(squares, 1)
            act.wait_ge(summed, KD)
            act.copy(lt[:].rearrange("p (n t) -> p n t", n=NT), ps[0:NL, :, 0:TW]).then_inc(back, 1)
            act.wait_ge(ready, 1)
            act.activation(e[:], e[:], ACT.Exp).then_inc(back, 1)
            act.wait_ge(ready, 2)
            act.activation(ls[:], ls[:], ACT.Exp).then_inc(back, 1)
            act.wait_ge(pe_s, 2)
            act.copy(sel_rows[:].rearrange("p (n t) -> p n t", n=NT), ps3[0:NE, :, 0:TW]).then_inc(back, 1)

        @block.gpsimd
        def _(pool):
            pool.wait_ge(ready, 7)
            for t in range(RT):
                pool.wait_ge(h2_ready, t + 1)
                for k in range(TOPK):
                    pool.indirect_dma_start(slots_dram, bass.IndirectOffsetOnAxis(ap=idx[:, t, k:k + 1], axis=0),
                                            h2[:, t % 4, :], None).then_inc(sent[t % 4], 16)
            for q in sent:
                pool.wait_ge(q, 16 * TOPK * RT // 4)

        @block.vector
        def _(dve):
            count = [0]

            def link(ins):
                count[0] += 1
                ins.then_inc(dve_s, 1)
                dve.wait_ge(dve_s, count[0])

            def wide(ap, n):
                return ap.to_broadcast([RL, RT, n])

            def first_max(hot_, val, n):
                link(dve.tensor_reduce(mx[:], val[:], AX.X, ALU.max))
                dve.memset(left[:], 1.0)
                link(dve.tensor_tensor(eq[:], val[:], wide(mx[:], n), ALU.is_ge))
                for i in range(n):
                    link(dve.tensor_tensor(hot_[:, :, i:i + 1], eq[:, :, i:i + 1], left[:], ALU.mult))
                    link(dve.tensor_tensor(left[:], left[:], hot_[:, :, i:i + 1], ALU.subtract))

            dve.wait_ge(loaded, 64)
            for k in range(KD):
                if k >= 2:
                    dve.wait_ge(summed, k - 1)
                dve.tensor_scalar(xw[:, k % 2, :], x2t[:, k, :], w2c[:, k:k + 1], None, ALU.mult).then_inc(xw_s, 1)
            dve.wait_ge(squares, RT)
            dve.tensor_scalar(rs[:], rs[:], 1.0 / D, EPS, ALU.mult, ALU.add).then_inc(squares, 1)
            dve.memset(one_rows[:], 1.0)
            dve.wait_ge(squares, RT + 2)
            link(dve.reciprocal(rs[:], rs[:]))
            dve.wait_ge(pe_s, 1)
            link(dve.tensor_tensor(lg[:], ps2[0:RL, 0:RT * NL].rearrange("p (t l) -> p t l", l=NL),
                                   wide(rs[:], NL), ALU.mult))
            link(dve.tensor_reduce(mx[:], lg[:, :, 0:NG], AX.X, ALU.max))
            dve.tensor_tensor(e[:], lg[:, :, 0:NG], wide(mx[:], NG), ALU.subtract).then_inc(ready, 1)
            dve.wait_ge(back, 2)
            link(dve.tensor_reduce(s[:], e[:], AX.X, ALU.add))
            first_max(hot, e, NG)
            link(dve.reciprocal(pt[:], s[:]))
            link(dve.tensor_tensor(pt[:], pt[:], mx[:], ALU.mult))
            link(dve.tensor_tensor(prod[:], lg[:, :, NG:].rearrange("p t (g e) -> p t g e", g=NG),
                                   hot[:].unsqueeze(3).to_broadcast([RL, RT, NG, EPG]), ALU.mult))
            link(dve.tensor_reduce(ls[:].unsqueeze(3), prod[:].rearrange("p t g e -> p t e g"), AX.X, ALU.add))
            link(dve.tensor_reduce(mx[:], ls[:], AX.X, ALU.max))
            dve.tensor_tensor(ls[:], ls[:], wide(mx[:], EPG), ALU.subtract).then_inc(ready, 1)
            dve.wait_ge(back, 3)
            link(dve.tensor_reduce(s[:], ls[:], AX.X, ALU.add))
            link(dve.reciprocal(s[:], s[:]))
            link(dve.tensor_tensor(ls[:], ls[:], wide(s[:], EPG), ALU.mult))
            for k in range(TOPK):
                first_max(hots[k], ls, EPG)
                dve.tensor_copy(vals[k][:], mx[:])
                link(dve.tensor_tensor(both[k][:], hot[:].unsqueeze(3).to_broadcast([RL, RT, NG, EPG]),
                                       hots[k][:].unsqueeze(2).to_broadcast([RL, RT, NG, EPG]), ALU.mult))
                if k == 0:
                    link(dve.scalar_tensor_tensor(ls[:], hots[0][:], -4.0, ls[:], ALU.mult, ALU.add))
            flat = [b[:].rearrange("p t g e -> p t (g e)") for b in both]
            dve.tensor_tensor(sel[:], flat[0], flat[1], ALU.add).then_inc(ready, 1)
            link(dve.tensor_tensor(s[:], vals[0][:], vals[1][:], ALU.add))
            link(dve.reciprocal(s[:], s[:]))
            link(dve.tensor_tensor(s[:], s[:], pt[:], ALU.mult))
            for k in range(TOPK):
                link(dve.tensor_tensor(wts[:, :, k:k + 1], vals[k][:], s[:], ALU.mult))
            dve.wait_ge(back, 4)
            link(dve.tensor_tensor_scan(pos[:], one_rows[:], sel_rows[:], 0.0, ALU.mult, ALU.add))
            link(dve.tensor_tensor(gt[:], pos[:, T - 1:T].to_broadcast([NE, 8]), thresholds, ALU.is_gt))
            dve.tensor_reduce(n_blocks[:], gt[:], AX.X, ALU.add).then_inc(ready, 1)
            dve.wait_ge(pe_s, 3)
            link(dve.tensor_copy(base[:], ps[0:NE, 0, 0:1]))
            dve.tensor_tensor(ended[:], block_ids, base[:].to_broadcast([NE, NBLK + 1]), ALU.is_ge).then_inc(ready, 1)
            dve.wait_ge(ready, 5)
            link(dve.tensor_tensor(base[:], base[:], n_blocks[:], ALU.subtract))
            link(dve.tensor_scalar(base[:], base[:], float(BLK), -1.0, ALU.mult, ALU.add))
            dve.tensor_scalar(pos[:], pos[:], base[:], None, ALU.add).then_inc(ready, 1)
            dve.wait_ge(pe_s, 4)
            link(dve.tensor_scalar(owner[:], ps[0:1, 1, 0:NBLK + 1], float(NE - 1), None, ALU.min))
            link(dve.tensor_copy(expert_of[:], owner[:]))
            dve.wait_ge(pe_s, 5)
            link(dve.tensor_copy(slot_t[:], ps2[0:RL, 0:RT * NE].rearrange("p (t l) -> p t l", l=NE)))
            for k in range(TOPK):
                link(dve.tensor_tensor(sel[:], slot_t[:], flat[k], ALU.mult))
                link(dve.tensor_reduce(slot_f[:, :, k:k + 1], sel[:], AX.X, ALU.add))
            dve.tensor_copy(idx[:], slot_f[:]).then_inc(ready, 1)
            for t in range(RT):
                if t >= 4:
                    dve.wait_ge(sent[t % 4], 16 * TOPK * (t // 4))
                dve.scalar_tensor_tensor(h2[:, t % 4, :], x2[:, t, :], rs[:, t, :], w2r[0:RL, :], ALU.mult,
                                         ALU.mult).then_inc(h2_ready, 1)


def expert_phase(nc, io, expert_of, masks, slots_dram, y_dram):
    with ExitStack() as stack:
        m = Memory(nc, stack)
        win, wdn = m.sb("e_win", [P, KD, 512]), m.sb("e_wdn", [P, 2, D])
        win_r = [m.sb(f"e_win{x}", [P, 2, KD, 512], F32R) for x in ("hi", "lo")]
        wdn_r = [m.sb(f"e_wdn{x}", [P, 2, 2, D], F32R) for x in ("hi", "lo")]
        xs = m.sb("e_xs", [P, 2, D])
        ht = [m.sb(f"e_ht{x}", [P, 2, KD, BLK], F32R) for x in ("hi", "lo")]
        s, gated = m.sb("e_s", [P, 2, FF]), m.sb("e_gated", [P, 2, FF])
        at = [m.sb(f"e_at{x}", [P, 2, 2, P], F32R) for x in ("hi", "lo")]
        ys = m.sb("e_ys", [P, 2, 2, D])
        ps_t, ps_g, ps_a, ps_d = (m.ps("e_pst", [P, 2, 512]), m.ps("e_psg", [P, 2, 512]), m.ps("e_psa", [P, 2, 512]),
                                  m.ps("e_psd", [P, 2, 512]))
        turned = ps_a[:, :, 0:FF].rearrange("p t (f s) -> p t f s", f=2)
        PARTS = ((0, 1), (1, 0), (0, 0))
        pp = Steps(m, "e_ppe", ["t0", "t1", "t2", "t3"])
        pa = Steps(m, "e_pact", ["in0", "in1", "t0", "t1", "t2", "t3", "dn"])
        pv = Steps(m, "e_pdve", ["in0", "in1", "t0", "t1", "t2", "t3", "dn"])
        p = Steps(m, "e_pe", ["g0", "g1", "a0", "a1", "d0", "d1", "d2", "d3"], ahead=2)
        a = Steps(m, "e_act", ["s0", "s1", "a0", "a1", "y0", "y2"])
        v = Steps(m, "e_dve", ["h0", "h1", "a0", "a1", "y1", "y3"])
        in_loaded, dn_loaded, x_loaded = m.sem("e_inl"), m.sem("e_dnl"), m.sem("e_xl")
        y_sent, y_free = [m.sem(f"e_ysent{h}") for h in range(2)], [m.sem(f"e_yfree{h}") for h in range(2)]
        rows_of = slots_dram.rearrange("(n t p) d -> n p t d", t=2, p=P)
        y_of = y_dram.rearrange("(n t p) d -> n p t d", t=2, p=P)
        block = stack.enter_context(nc.Block())

        this_round = [None]

        def rounds_before():
            return this_round[0]

        def waiter(eng):
            return lambda steps, r, name, back=0: eng.wait_ge(steps.sem, steps.at(r, name, back))

        def loop(eng, main, prepare):
            prepare(0, 0, [0, 1, 2])
            with eng.Fori(0, NBLK // 2) as i:
                for h in range(2):
                    this_round[0] = i + 1
                    main(i * 2 + h, h, lambda part, i=i, h=h: prepare(i * 2 + (h + 1), 1 - h, [part]))

        @block.sync
        def _(sp):
            wait = waiter(sp)
            with sp.Fori(0, NBLK + 1) as r:
                e = sp.value_load(expert_of[0:1, bass.ds(r, 1)], min_val=0, max_val=NE - 1)
                wait(pv, r, "in1", 1)
                sp.dma_start(win[:], io["w_gate_up"][bass.ds(e, 1)].rearrange("a p k f -> (a p) k f")
                             ).then_inc(in_loaded, 16)
                wait(pp, r, "t3", 1)
                sp.dma_start(xs[:], rows_of[bass.ds(r, 1)].rearrange("a p t d -> (a p) t d")).then_inc(x_loaded, 16)
                wait(pv, r, "dn", 1)
                sp.dma_start(wdn[:], io["w_down"][bass.ds(e, 1)].rearrange("a p k d -> (a p) k d")
                             ).then_inc(dn_loaded, 16)

        @block.gpsimd
        def _(pool):
            wait = waiter(pool)
            for h in range(2):
                pool.sem_inc(y_free[h], 1)
            with pool.Fori(0, NBLK // 2) as i:
                for h in range(2):
                    wait(a, i * 2 + h, "y2")
                    wait(v, i * 2 + h, "y3")
                    pool.dma_start(y_of[bass.ds(i * 2 + h, 1)].rearrange("a p t d -> (a p) t d"), ys[:, h]
                                   ).then_inc(y_sent[h], 16)
                    pool.wait_ge(y_sent[h], i * 16 + 16)
                    pool.sem_inc(y_free[h], 1)

        @block.tensor
        def _(pe):
            wait = waiter(pe)
            pp.start(pe)
            p.start(pe)

            def prepare(r, q, parts):
                for part in parts:
                    if part == 0:
                        pe.wait_ge(x_loaded, r * 16 + 16)
                    for g in range(4):
                        if g // 2 != part:
                            continue
                        bank = g % 2
                        wait(pa, r, f"t{g - 2}" if g >= 2 else f"t{g + 2}", 0 if g >= 2 else 1)
                        wait(pv, r, f"t{g - 2}" if g >= 2 else f"t{g + 2}", 0 if g >= 2 else 1)
                        for k in range(4):
                            at_ = ((g % 2) * 4 + k) * P
                            mm = pe.transpose(ps_t[:, bank, k * P:(k + 1) * P], xs[:, g // 2, at_:at_ + P],
                                              masks[:, 0, :])
                        mm.then_inc(pp.sem, 1)

            def passes(dst, lhs, rhs, ks):
                for n, (x, z) in enumerate(PARTS):
                    for k in range(ks):
                        mm = pe.matmul(dst, lhs(x, k), rhs(z, k), start=(n == 0 and k == 0),
                                       stop=(n == 2 and k == ks - 1))
                mm.then_inc(p.sem, 1)

            def main(j, q, prepare_next):
                wait(pv, j, "in1")
                wait(pv, j, "t3")
                wait(pa, j, "t3")
                for t in range(2):
                    wait(v, j, f"h{t}", 1)
                    passes(ps_g[:, t, :], lambda x, k: ht[x][:, q, k, t * P:(t + 1) * P],
                           lambda z, k: win_r[z][:, q, k, :], KD)
                prepare_next(0)
                for t in range(2):
                    wait(v, j, f"h{t}")
                    wait(a, j, f"a{t}", 1)
                    wait(v, j, f"a{t}", 1)
                    for f in range(2):
                        mm = pe.transpose(turned[:, t, f, :], gated[:, t, f * P:(f + 1) * P], masks[:, 0, :])
                    mm.then_inc(p.sem, 1)
                prepare_next(1)
                wait(pv, j, "dn")
                for d in range(4):
                    t = d // 2
                    wait(v, j, f"a{t}")
                    wait((a, v)[d % 2], j, f"y{(d + 2) % 4}", 0 if d >= 2 else 1)
                    passes(ps_d[:, d % 2, :], lambda x, k: at[x][:, t, k, :],
                           lambda z, k: wdn_r[z][:, q, k, (d % 2) * 512:(d % 2 + 1) * 512], 2)

            loop(pe, main, prepare)

        def group_dst(part, q, g):
            k0 = (g % 2) * 4
            return ht[part][:, q, k0:k0 + 4, (g // 2) * P:(g // 2 + 1) * P]

        def group_src(g):
            return ps_t[:, g % 2, :].rearrange("p (k s) -> p k s", k=4)

        @block.scalar
        def _(act):
            wait = waiter(act)
            pa.start(act)
            a.start(act)

            def prepare(r, q, parts):
                if 0 in parts:
                    act.wait_ge(in_loaded, r * 16 + 16)
                    wait(p, r, "g1", 2)
                    for h in range(2):
                        act.copy(win_r[0][:, q, h * 4:h * 4 + 4, :], win[:, h * 4:h * 4 + 4, :]).then_inc(pa.sem, 1)
                for part in (1, 2):
                    if part in parts:
                        for g in (2 * part - 2, 2 * part - 1):
                            wait(pp, r, f"t{g}")
                            act.copy(group_dst(0, q, g), group_src(g)).then_inc(pa.sem, 1)
                if 2 in parts:
                    act.wait_ge(dn_loaded, r * 16 + 16)
                    wait(p, r, "d3", 2)
                    act.copy(wdn_r[0][:, q], wdn[:]).then_inc(pa.sem, 1)

            def main(j, q, prepare_next):
                prepare_next(0)
                for t in range(2):
                    wait(p, j, f"g{t}")
                    act.activation(s[:, t, :], ps_g[:, t, 0:FF], ACT.Silu).then_inc(a.sem, 1)
                prepare_next(1)
                for t in range(2):
                    wait(p, j, f"a{t}")
                    act.copy(at[0][:, t], turned[:, t]).then_inc(a.sem, 1)
                prepare_next(2)
                act.wait_ge(y_free[q], rounds_before())
                for d in (0, 2):
                    wait(p, j, f"d{d}")
                    act.copy(ys[:, q, d // 2, 0:512], ps_d[:, d % 2, :]).then_inc(a.sem, 1)

            loop(act, main, prepare)

        @block.vector
        def _(dve):
            wait = waiter(dve)
            pv.start(dve)
            v.start(dve)

            def prepare(r, q, parts):
                if 0 in parts:
                    for h in range(2):
                        wait(pa, r, f"in{h}")
                        ks = slice(h * 4, h * 4 + 4)
                        dve.tensor_tensor(win_r[1][:, q, ks, :], win[:, ks, :], win_r[0][:, q, ks, :].bitcast(F32),
                                          ALU.subtract).then_inc(pv.sem, 1)
                for part in (1, 2):
                    if part in parts:
                        for g in (2 * part - 2, 2 * part - 1):
                            wait(pa, r, f"t{g}")
                            dve.tensor_tensor(group_dst(1, q, g), group_src(g), group_dst(0, q, g).bitcast(F32),
                                              ALU.subtract).then_inc(pv.sem, 1)
                if 2 in parts:
                    wait(pa, r, "dn")
                    dve.tensor_tensor(wdn_r[1][:, q], wdn[:], wdn_r[0][:, q].bitcast(F32),
                                      ALU.subtract).then_inc(pv.sem, 1)

            def main(j, q, prepare_next):
                prepare_next(0)
                for t in range(2):
                    wait(a, j, f"s{t}")
                    dve.tensor_tensor(gated[:, t, :], s[:, t, :], ps_g[:, t, FF:], ALU.mult).then_inc(v.sem, 1)
                prepare_next(1)
                for t in range(2):
                    wait(a, j, f"a{t}")
                    dve.tensor_tensor(at[1][:, t], turned[:, t], at[0][:, t].bitcast(F32), ALU.subtract).then_inc(v.sem, 1)
                prepare_next(2)
                dve.wait_ge(y_free[q], rounds_before())
                for d in (1, 3):
                    wait(p, j, f"d{d}")
                    dve.tensor_copy(ys[:, q, d // 2, 512:], ps_d[:, d % 2, :]).then_inc(v.sem, 1)

            loop(dve, main, prepare)


def combine_phase(nc, io, wts, idx, x2_dram, y_dram):
    BUFS = 4
    with ExitStack() as stack:
        m = Memory(nc, stack)
        wf = m.sb("f_w", [P, D])
        x, r1, r2 = m.sb("f_x", [RL, BUFS, D]), m.sb("f_r1", [RL, BUFS, D]), m.sb("f_r2", [RL, BUFS, D])
        junk, q = m.sb("f_junk", [RL, D]), m.sb("f_q", [RL, RT, 1])
        w_loaded = m.sem("f_wl")
        loaded, gathered = [m.sem(f"f_l{i}") for i in range(BUFS)], [m.sem(f"f_g{i}") for i in range(BUFS)]
        sent = [m.sem(f"f_sent{i}") for i in range(BUFS)]
        a, v = Steps(m, "f_act", ["square", "root"]), Steps(m, "f_dve", ["one", "two", "mean", "inverse", "out"])
        block = stack.enter_context(nc.Block())

        @block.sync
        def _(sp):
            sp.dma_start(wf[:], io["final_row"].partition_broadcast(P)).then_inc(w_loaded, 16)
            for t in range(RT + 2):
                if t < RT:
                    if t >= BUFS:
                        sp.wait_ge(sent[t % BUFS], 16 * (t // BUFS))
                    sp.dma_start(x[:, t % BUFS, :], x2_dram[t * RL:(t + 1) * RL, :]).then_inc(loaded[t % BUFS], 16)
                if t >= 2:
                    o = t - 2
                    sp.wait_ge(v.sem, v.at(o, "out"))
                    sp.dma_start(io["y"][o * RL:(o + 1) * RL, :], x[:, o % BUFS, :]).then_inc(sent[o % BUFS], 16)
            for b in range(BUFS):
                sp.wait_ge(sent[b], 16 * (RT // BUFS))

        @block.gpsimd
        def _(pool):
            for t in range(RT):
                if t >= BUFS:
                    pool.wait_ge(v.sem, v.at(t - BUFS, "two"))
                for k, r in enumerate((r1, r2)):
                    pool.indirect_dma_start(r[:, t % BUFS, :], None, y_dram,
                                            bass.IndirectOffsetOnAxis(ap=idx[:, t, k:k + 1], axis=0)
                                            ).then_inc(gathered[t % BUFS], 16)

        @block.scalar
        def _(act):
            a.start(act)
            for t in range(RT):
                act.wait_ge(v.sem, v.at(t, "two"))
                act.wait_ge(a.sem, a.at(t, "square", 1))
                act.activation(junk[:], x[:, t % BUFS, :], ACT.Square, accum_out=q[:, t, :]).then_inc(a.sem, 1)
                act.wait_ge(v.sem, v.at(t, "mean"))
                act.activation(q[:, t, :], q[:, t, :], ACT.Sqrt).then_inc(a.sem, 1)

        @block.vector
        def _(dve):
            v.start(dve)
            dve.wait_ge(w_loaded, 16)
            for t in range(RT):
                b = t % BUFS
                xt = x[:, b, :]
                dve.wait_ge(loaded[b], 16 * (t // BUFS + 1))
                dve.wait_ge(gathered[b], 32 * (t // BUFS + 1))
                dve.scalar_tensor_tensor(xt, r1[:, b, :], wts[:, t, 0:1], xt, ALU.mult, ALU.add).then_inc(v.sem, 1)
                dve.wait_ge(v.sem, v.at(t, "one"))
                dve.scalar_tensor_tensor(xt, r2[:, b, :], wts[:, t, 1:2], xt, ALU.mult, ALU.add).then_inc(v.sem, 1)
                dve.wait_ge(a.sem, a.at(t, "square"))
                dve.tensor_scalar(q[:, t, :], q[:, t, :], 1.0 / D, EPS, ALU.mult, ALU.add).then_inc(v.sem, 1)
                dve.wait_ge(a.sem, a.at(t, "root"))
                dve.reciprocal(q[:, t, :], q[:, t, :]).then_inc(v.sem, 1)
                dve.wait_ge(v.sem, v.at(t, "inverse"))
                dve.scalar_tensor_tensor(xt, xt, q[:, t, :], wf[0:RL, :], ALU.mult, ALU.mult).then_inc(v.sem, 1)


def program(nc, io):
    def dram(name, *shape):
        return nc.dram_tensor(name, shape, F32, kind="Internal").ap()

    z_dram, yc_dram, g_dram = dram("z_rows", NZ, P, T), dram("yc_rows", NC, P, T), dram("g_rows", NR, T)
    x2_dram = dram("x2_rows", T, D)
    slots_dram, y_dram = dram("slot_rows", SLOTS + BLK, D), dram("expert_rows", SLOTS, D)
    with ExitStack() as stack:
        m = Memory(nc, stack)
        ones = m.sb("ones", [P, P])
        masks = m.sb("masks", [P, 7, P])
        wts, idx = m.sb("wts", [RL, RT, TOPK]), m.sb("idx", [RL, RT, TOPK], mybir.dt.uint32)
        expert_of = m.sb("expert_of", [1, NBLK + 1], mybir.dt.int32)
        with ExitStack() as residual:
            with ExitStack() as mix:
                mm = Memory(nc, mix)
                act_out = mm.sb("act_out", [P, NCONV, T])
                rows = [mm.sb(f"rows_{x}", [P, T]) for x in "abc"]
                with ExitStack() as first:
                    hn = Memory(nc, first).sb("hn", [P, KD, T])
                    norm1_phase(nc, io, hn, ones, masks)
                    gates_phase(nc, io, hn, *rows, g_dram)
                    projection_phase(nc, io, hn, act_out, z_dram, yc_dram)
                qk_norm_phase(nc, act_out, ones)
                gdn_phase(nc, io, act_out, rows, g_dram, masks, False, slots_dram)
                gdn_phase(nc, io, act_out, rows, g_dram, masks, True)
                ssd_phase(nc, io, act_out, rows, g_dram, masks, False)
                ssd_phase(nc, io, act_out, rows, g_dram, masks, True)
                mixed = gate_phase(nc, io, act_out, ones, z_dram, yc_dram)
                x2t = mm.sb("x2t", [P, KD, T])
                out_projection_phase(nc, io, act_out, mixed, x2t)
                x2 = act_out[0:RL].rearrange("p n t -> p (n t)")[:, 0:RT * D].rearrange("p (n d) -> p n d", d=D)
                transpose_x_phase(nc, x2t, x2, masks)
                routing_phase(nc, io, x2t, x2, wts, idx, expert_of, masks, ones, slots_dram, x2_dram)
        expert_phase(nc, io, expert_of, masks, slots_dram, y_dram)
        combine_phase(nc, io, wts, idx, x2_dram, y_dram)


def gdn_states(a):
    return np.ascontiguousarray(a[0].transpose(2, 0, 1, 3))


def channel_blocks(a):
    b, r, c = a.shape[1:]
    return a[0].reshape(b, r, c // P, P).transpose(3, 2, 0, 1)


def from_channel_blocks(a):
    p, n, b, r = a.shape
    return np.ascontiguousarray(a.transpose(2, 3, 1, 0).reshape(1, b, r, n * p))


def mask_constants():
    i = np.arange(P)
    later = i[None, :] >= i[:, None]
    below = i[:, None] > i[None, :]
    seq = i[:, None] // LSEQ == i[None, :] // LSEQ
    none = np.float32(NEG)
    zero = np.float32(0)
    out = np.stack([
        np.eye(P, dtype=np.float32),
        np.where(later, zero, none), np.where(below, zero, none),
        (i[:, None] // 16 == i[None, :] // 16).astype(np.float32),
        np.where(later & seq, zero, none), np.where(below & seq, zero, none),
        (i[:, None] // LSEQ == i[None, :]).astype(np.float32)], axis=1)
    return np.ascontiguousarray(out.astype(np.float32))


def route_constants():
    out = np.zeros((NE, 9 + NBLK + NE), np.float32)
    out[:, 0:8] = np.arange(8) * BLK
    out[:, 8:9 + NBLK] = np.arange(NBLK + 1)
    out[:, 9 + NBLK:] = np.arange(NE)[:, None] <= np.arange(NE)[None, :]
    return out


def lay_out(x):
    f = lambda n: np.asarray(x[n], dtype=np.float32)
    tokens = np.concatenate([f("meta_tokens"), f("x_prompt")[0], f("x_sample").reshape(TS, D)])
    w = f("w_in")[0]
    at = {}
    start = 0
    for name, n in (("qkv", 1536), ("z_a", 512), ("b", HA), ("a", HA), ("xbc", 1024), ("z_b", 512), ("dt", HB),
                    ("h", 512), ("c", 512), ("bb", 512)):
        at[name] = w[:, start:start + n]
        start += n
    short = [at[n][:, c * P:(c + 1) * P] for c in range(NC) for n in ("h", "c", "bb")]
    blocks = np.concatenate([at["qkv"], at["xbc"], at["z_a"], at["z_b"], *short], axis=1)
    gates = np.zeros((D, 64), np.float32)
    gates[:, 0:HA], gates[:, ROW_G:ROW_G + HA], gates[:, ROW_G + HA:ROW_G + NR] = at["b"], at["a"], at["dt"]
    bias, alog = np.zeros((64, 1), np.float32), np.zeros((64, 1), np.float32)
    bias[ROW_G:ROW_G + HA, 0], bias[ROW_G + HA:ROW_G + NR, 0] = f("dt_bias_a")[0], f("dt_bias_b")[0]
    alog[ROW_G:ROW_G + HA, 0], alog[ROW_G + HA:ROW_G + NR, 0] = f("a_log_a")[0], f("a_log_b")[0]

    def columns(v):
        return v.reshape(-1, P).T

    def stationary(v, n):
        return v.reshape(-1, P, n, v.shape[1] // n).transpose(2, 1, 0, 3)

    taps = np.zeros((P, NCONV, W_A + 1), np.float32)
    taps[:, :12, :W_A] = f("conv_a_w")[0].reshape(W_A, 12, P).transpose(2, 1, 0)
    taps[:, 12:, :W_A] = f("conv_b_w")[0].reshape(W_A, 8, P).transpose(2, 1, 0)
    taps[:, 12:, W_A] = columns(f("conv_b_b")[0])
    io = {
        "xT": tokens.T.reshape(KD, P, T).transpose(1, 0, 2),
        "masks": mask_constants(),
        "norm1_w": columns(f("norm1_w")[0]), "norm2_w": columns(f("norm2_w")[0]),
        "w_gates": gates.reshape(KD, P, 64).transpose(1, 0, 2), "gate_bias": bias, "gate_alog": alog,
        "w_in": stationary(blocks, NCONV + NZ + 3 * NC),
        "taps": taps, "taps_c": f("conv_c_w")[0].reshape(W_C, NC, P).transpose(2, 1, 0),
        "hist_ab": np.concatenate([channel_blocks(f("state_gdn_conv")), channel_blocks(f("state_ssd_conv"))], axis=1),
        "hist_c": channel_blocks(f("state_sconv")),
        "state_gdn": f("state_gdn")[0].transpose(2, 0, 1, 3),
        "state_ssd": f("state_ssd")[0].transpose(3, 0, 1, 2),
        "d_skip": columns(np.repeat(f("d_skip_b")[0], PB)),
        "onorm_a": columns(f("onorm_a_w")[0]), "onorm_b": columns(f("onorm_b_w")[0]),
        "w_out": stationary(f("w_out")[0], KD),
        "w_router": np.concatenate([f("w_router_g")[0], f("w_router_e")[0]], axis=1).reshape(KD, P, -1).transpose(1, 0, 2),
        "w_gate_up": np.concatenate([f("w_gate")[0], f("w_up")[0]], axis=2).reshape(NE, KD, P, 2 * FF).transpose(0, 2, 1, 3),
        "w_down": f("w_down")[0].reshape(NE, 2, P, D).transpose(0, 2, 1, 3),
        "norm2_row": f("norm2_w")[0], "final_row": f("final_norm_w"), "route_consts": route_constants(),
    }
    return {k: np.ascontiguousarray(v) for k, v in io.items()}


OUTPUTS = {
    "y": (T, D), "new_hist_ab": (P, NCONV, 1 + NSEQ, HIST), "new_hist_c": (P, NC, 1 + NSEQ, HISTC),
    "new_gdn_p": (P, HA, DK), "new_gdn_s": (P, NSEQ, HA, DK), "new_ssd_p": (P, HB, PB), "new_ssd_s": (P, NSEQ, HB, PB),
}


def kernel(**inputs):
    import concourse.bacc as bacc
    from concourse.bass_utils import run_bass_kernel_spmd

    nc = bacc.Bacc("TRN2", target_bir_lowering=False, num_devices=1)
    arrays = lay_out(inputs)
    io = {n: nc.dram_tensor("in_" + n, a.shape, F32, kind="ExternalInput").ap() for n, a in arrays.items()}
    io |= {n: nc.dram_tensor(n, s, F32, kind="ExternalOutput").ap() for n, s in OUTPUTS.items()}
    program(nc, io)
    got = run_bass_kernel_spmd(nc, [{"in_" + n: a for n, a in arrays.items()}], core_ids=[0]).results[0]

    y = got["y"]
    hist = got["new_hist_ab"]
    na = 3 * HA
    out = (
        y[N_META:TP][None], y[TP:].reshape(NSEQ, LSEQ, D),
        got["new_gdn_p"].transpose(1, 0, 2)[None, None],
        from_channel_blocks(hist[:, :na, :1]), got["new_ssd_p"].transpose(1, 2, 0)[None, None],
        from_channel_blocks(hist[:, na:, :1]), from_channel_blocks(got["new_hist_c"][:, :, :1]),
        got["new_gdn_s"].transpose(1, 2, 0, 3)[None],
        from_channel_blocks(hist[:, :na, 1:]), got["new_ssd_s"].transpose(1, 2, 3, 0)[None],
        from_channel_blocks(hist[:, na:, 1:]), from_channel_blocks(got["new_hist_c"][:, :, 1:]),
    )
    return tuple(np.ascontiguousarray(a) for a in out)
```

```python
from contextlib import ExitStack

import numpy as np

import concourse.bass as bass
from concourse import mybir

F32 = mybir.dt.float32
F32R = mybir.dt.float32r
ALU = mybir.AluOpType
ACT = mybir.ActivationFunctionType
AX = mybir.AxisListType

P = 128
D = 1024
KD = D // P
N_META, SEQ = 16, 1024
TP = N_META + SEQ
NSEQ, LSEQ = 8, 8
TS = NSEQ * LSEQ
T = TP + TS
NT, TW = 3, T // 3
HA, DK = 4, 128
HB, PB, GB, NB = 8, 64, 2, 128
CH = 104
NCH = TP // CH
W_A, W_C = 4, 3
NCONV, NZ, NC = 20, 8, 4
HIST = W_A - 1
RAW = HIST + TP + NSEQ * (HIST + LSEQ)
CONVW = RAW - HIST
HISTC = W_C - 1
RAWC = HISTC + TP + NSEQ * (HISTC + LSEQ)
CONVWC = RAWC - HISTC
NE, NG, EPG, FF, TOPK = 16, 4, 4, 256, 2
NMIX = 12
NQKV = 3 * HA
AT_X, AT_B, AT_C = 0, 4, 6
EPS = 1e-6
NEG = -1e30
ROW_G = 32
NR = 12
TAIL = TP - 2 * TW


def samples(ap, base, stride, lo, hi):
    return ap[:, base:base + NSEQ * stride].rearrange("p (b s) -> p b s", s=stride)[:, :, lo:hi]


def one(ap, b):
    names = "xyz"[:len(ap.shape) - 2]
    return ap[:, bass.ds(b, 1)].rearrange(f"p a {' '.join(names)} -> p (a {names[0]}) {' '.join(names[1:])}")


class Memory:

    def __init__(self, nc, stack):
        self.nc, self.stack = nc, stack

    def sb(self, name, shape, dt=F32):
        return self.stack.enter_context(self.nc.sbuf_tensor(name, shape, dt))

    def ps(self, name, shape, dt=F32):
        return self.stack.enter_context(self.nc.psum_tensor(name, shape, dt))

    def sem(self, name):
        return self.stack.enter_context(self.nc.semaphore(name))


def copy_hi(eng, dst, src):
    return eng.copy(dst, src)


def take_lo(dve, dst, src, hi):
    return dve.tensor_tensor(dst, src, hi.bitcast(F32), ALU.subtract)


PARTS = ((0, 1), (1, 0), (0, 0))


def exact_product(pe, dst, left, right, ks):
    for n, (x, z) in enumerate(PARTS):
        for k in range(ks):
            mm = pe.matmul(dst, left(x, k), right(z, k), start=(n == 0 and k == 0), stop=(n == 2 and k == ks - 1))
    return mm


def norm1_phase(nc, io, hn, gates, ones, masks):
    with ExitStack() as stack:
        m = Memory(nc, stack)
        w1 = m.sb("n1_w", [P, KD])
        x = m.sb("n1_x", [P, KD, T])
        sq = m.sb("n1_sq", [P, 2, T])
        rb = m.sb("n1_rb", [P, T])
        ss = m.ps("n1_ss", [P, NT, 512])
        loaded, ones_set = m.sem("n1_loaded"), m.sem("n1_ones")
        x_loaded = [m.sem(f"n1_x{k}") for k in range(2)]
        squared, summed = m.sem("n1_squared"), m.sem("n1_summed")
        mean_ready, scaled, split = m.sem("n1_mean"), m.sem("n1_scaled"), m.sem("n1_split")
        block = stack.enter_context(nc.Block())

        @block.sync
        def _(sp):
            for h, ks in enumerate((slice(0, KD // 2), slice(KD // 2, KD))):
                sp.dma_start(x[:, ks, :], io["xT"][:, ks, :]).then_inc(x_loaded[h], 16)
            sp.dma_start(w1[:], io["norm1_w"]).then_inc(loaded, 16)
            sp.dma_start(masks[:], io["masks"]).then_inc(loaded, 16)
            gates.load(sp)

        @block.scalar
        def _(act):
            for k in range(KD):
                act.wait_ge(x_loaded[k // (KD // 2)], 16)
                if k >= 2:
                    act.wait_ge(summed, k - 1)
                act.activation(sq[:, k % 2, :], x[:, k, :], ACT.Square).then_inc(squared, 1)
            act.wait_ge(mean_ready, 1)
            act.activation(rb[:], rb[:], ACT.Sqrt).then_inc(mean_ready, 1)
            gates.hi(act)
            for k in range(KD):
                act.wait_ge(scaled, k + 1)
                copy_hi(act, hn[0][:, k, :], x[:, k, :]).then_inc(split, 1)

        @block.tensor
        def _(pe):
            pe.wait_ge(ones_set, 1)
            for k in range(KD):
                pe.wait_ge(squared, k + 1)
                for n in range(NT):
                    mm = pe.matmul(ss[:, n, 0:TW], ones[:], sq[:, k % 2, n * TW:(n + 1) * TW],
                                   start=(k == 0), stop=(k == KD - 1))
                mm.then_inc(summed, 1)

        @block.vector
        def _(dve):
            dve.memset(ones[:], 1.0).then_inc(ones_set, 1)
            gates.clear(dve)
            dve.wait_ge(loaded, 32)
            dve.wait_ge(summed, KD)
            dve.tensor_scalar(rb[:].rearrange("p (n t) -> p n t", n=NT), ss[:, :, 0:TW], 1.0 / D, EPS,
                              ALU.mult, ALU.add).then_inc(mean_ready, 1)
            dve.wait_ge(mean_ready, 2)
            dve.reciprocal(rb[:], rb[:]).then_inc(mean_ready, 1)
            gates.lo(dve)
            dve.wait_ge(mean_ready, 3)
            for k in range(KD + 1):
                if k < KD:
                    dve.scalar_tensor_tensor(x[:, k, :], x[:, k, :], w1[:, k:k + 1], rb[:],
                                             ALU.mult, ALU.mult).then_inc(scaled, 1)
                if k:
                    dve.wait_ge(split, k)
                    take_lo(dve, hn[1][:, k - 1, :], x[:, k - 1, :], hn[0][:, k - 1, :])


class Gates:

    def __init__(self, io, m, hn, rows, g_dram):
        self.io, self.hn, self.g_dram = io, hn, g_dram
        self.rows_a, self.rows_b, self.rows_c = rows
        self.wg = m.sb("g_w", [P, KD, P])
        self.wg_r = [m.sb(f"g_w{x}", [P, KD, P], F32R) for x in ("hi", "lo")]
        self.bias, self.a_log, self.neg_a = (m.sb(x, [64, 1]) for x in ("g_bias", "g_alog", "g_nega"))
        self.loaded, self.split, self.set, self.proj = m.sem("g_loaded"), m.sem("g_split"), m.sem("g_set"), m.sem("g_proj")
        self.act_step, self.dve_step, self.out = m.sem("g_act"), m.sem("g_dve"), m.sem("g_out")
        self.gr = slice(ROW_G, ROW_G + NR)

    def borrow(self, ps, y, u, d, mask):
        self.ps, self.y, self.u, self.d, self.mask = ps, y, u, d, mask

    def load(self, sp):
        sp.dma_start(self.wg[:], self.io["w_gates"]).then_inc(self.loaded, 16)
        sp.dma_start(self.bias[:], self.io["gate_bias"]).then_inc(self.loaded, 16)
        sp.dma_start(self.a_log[:], self.io["gate_alog"]).then_inc(self.loaded, 16)

    def store(self, sp):
        sp.wait_ge(self.dve_step, 13)
        sp.dma_start(self.g_dram[:, 0:T], self.rows_a[self.gr, :]).then_inc(self.out, 16)
        sp.dma_start(self.g_dram[:, T:], self.rows_a[self.gr, 0:TP + CH - T]).then_inc(self.out, 16)
        sp.wait_ge(self.out, 32)

    def product(self, pe):
        pe.wait_ge(self.split, 2)
        for n in range(NT):
            mm = exact_product(pe, self.ps[:, n, 0:TW], lambda x, k: self.wg_r[x][:, k, :],
                               lambda z, k: self.hn[z][:, k, n * TW:(n + 1) * TW], KD)
        mm.then_inc(self.proj, 1)

    def hi(self, act):
        act.wait_ge(self.loaded, 48)
        copy_hi(act, self.wg_r[0][:], self.wg[:]).then_inc(self.split, 1)

    def lo(self, dve):
        dve.wait_ge(self.split, 1)
        take_lo(dve, self.wg_r[1][:], self.wg[:], self.wg_r[0][:]).then_inc(self.split, 1)

    def exponentials(self, act):
        gr, rows_a, step = self.gr, self.rows_a, self.act_step
        act.wait_ge(self.proj, 1)
        act.wait_ge(self.set, 4)
        act.activation(rows_a[0:HA, :].rearrange("p (n t) -> p n t", n=NT), self.ps[0:HA, :, 0:TW], ACT.Exp,
                       scale=-1.0).then_inc(step, 1)
        act.activation(self.neg_a[gr, :], self.a_log[gr, :], ACT.Exp).then_inc(step, 1)
        act.wait_ge(self.dve_step, 3)
        act.activation(self.y[gr, :], self.u[gr, :], ACT.Exp).then_inc(step, 1)
        act.wait_ge(self.dve_step, 5)
        act.activation(self.d[gr, :], self.u[gr, :], ACT.Ln).then_inc(step, 1)

    def clear(self, dve):
        dve.memset(self.rows_a[:], 0.0).then_inc(self.set, 1)
        dve.memset(self.rows_b[:], 0.0).then_inc(self.set, 1)
        dve.memset(self.rows_c[:], 0.0).then_inc(self.set, 1)

    def constants(self, dve):
        dve.memset(self.mask, 1.0).then_inc(self.set, 1)
        dve.wait_ge(self.set, 4)
        dve.memset(self.mask[:, 0:TP].rearrange("p (c t) -> p c t", t=CH)[:, :, 0:1], 0.0).then_inc(self.set, 1)
        dve.memset(samples(self.mask, TP, LSEQ, 0, 1), 0.0).then_inc(self.set, 1)

    def arithmetic(self, dve, ps_free):
        gr, y, u, d, mask = self.gr, self.y, self.u, self.d, self.mask
        rows_a, rows_b, rows_c, done = self.rows_a, self.rows_b, self.rows_c, self.dve_step
        dve.wait_ge(self.proj, 1)
        dve.tensor_scalar(rows_c[gr, :].rearrange("p (n t) -> p n t", n=NT), self.ps[gr, :, 0:TW], self.bias[gr, :],
                          None, ALU.add).then_inc(done, 1)
        dve.wait_ge(done, 1)
        dve.wait_ge(self.act_step, 1)
        dve.sem_inc(ps_free, 1)
        dve.tensor_scalar(d[gr, :], rows_c[gr, :], -1.0, None, ALU.mult).then_inc(done, 1)
        dve.wait_ge(done, 2)
        dve.tensor_tensor(u[gr, :], rows_c[gr, :], d[gr, :], ALU.min).then_inc(done, 1)
        dve.tensor_scalar(rows_a[0:HA, :], rows_a[0:HA, :], 1.0, None, ALU.add).then_inc(done, 1)
        dve.wait_ge(self.act_step, 3)
        dve.tensor_scalar(u[gr, :], y[gr, :], 1.0, None, ALU.add).then_inc(done, 1)
        dve.wait_ge(done, 5)
        dve.scalar_tensor_tensor(y[gr, :], u[gr, :], -1.0, y[gr, :], ALU.add, ALU.subtract).then_inc(done, 1)
        dve.reciprocal(rows_a[0:HA, :], rows_a[0:HA, :]).then_inc(done, 1)
        dve.wait_ge(self.act_step, 4)
        dve.reciprocal(u[gr, :], u[gr, :]).then_inc(done, 1)
        dve.wait_ge(done, 8)
        dve.tensor_tensor(y[gr, :], y[gr, :], u[gr, :], ALU.mult).then_inc(done, 1)
        dve.wait_ge(done, 9)
        dve.tensor_tensor(d[gr, :], d[gr, :], y[gr, :], ALU.subtract).then_inc(done, 1)
        dve.wait_ge(done, 10)
        dve.scalar_tensor_tensor(rows_c[gr, :], rows_c[gr, :], 0.0, d[gr, :], ALU.max, ALU.add).then_inc(done, 1)
        dve.wait_ge(done, 11)
        dve.tensor_scalar(y[gr, :], rows_c[gr, :], self.neg_a[gr, :], -1.0, ALU.mult, ALU.mult).then_inc(done, 1)
        dve.wait_ge(done, 12)
        dve.wait_ge(self.set, 6)
        dve.tensor_tensor_scan(rows_a[gr, :], mask[gr, :], y[gr, :], 0.0, ALU.mult, ALU.add).then_inc(done, 1)
        dve.wait_ge(done, 13)
        for start, length in ((0, CH), (TP, LSEQ)):
            end = TP if start == 0 else T
            g = rows_a[gr, start:end].rearrange("p (c t) -> p c t", t=length)
            o = rows_b[gr, start:end].rearrange("p (c t) -> p c t", t=length)
            dve.tensor_tensor(o, g[:, :, length - 1:length].to_broadcast(list(g.shape)), g,
                              ALU.subtract).then_inc(done, 1)


def put_raw(op, dst, src, hist_n):
    op(dst[:, hist_n:hist_n + TW], src[:, 0, 0:TW], (0, TW))
    op(dst[:, hist_n + TW:hist_n + 2 * TW], src[:, 1, 0:TW], (TW, 2 * TW))
    op(dst[:, hist_n + 2 * TW:hist_n + TP], src[:, 2, 0:TAIL], (2 * TW, TP))
    return op(samples(dst, hist_n + TP, hist_n + LSEQ, hist_n, hist_n + LSEQ),
              src[:, 2, TAIL:TW].rearrange("p (b t) -> p b t", t=LSEQ), (TP, T))


def keep_tail(eng, tails, b, raw, hist_n):
    tail = one(tails, b)
    eng.tensor_copy(tail[:, 0, :], raw[:, TP:TP + hist_n])
    return eng.tensor_copy(tail[:, 1:, :], samples(raw, hist_n + TP, hist_n + LSEQ, LSEQ, hist_n + LSEQ))


def projection_phase(nc, io, hn, gates, qkv, xbc_dram, z_dram, yc_dram):
    with ExitStack() as stack:
        m = Memory(nc, stack)
        w = m.sb("c_w", [P, 2, KD, P])
        w_r = [m.sb(f"c_w{x}", [P, 2, KD, P], F32R) for x in ("hi", "lo")]
        raw = m.sb("c_raw", [P, 2, RAW])
        y = m.sb("c_y", [P, 2, RAW])
        out = m.sb("c_out", [P, 2, T])
        taps = m.sb("c_taps", [P, NCONV, W_A + 1])
        hist = m.sb("c_hist", [P, NCONV, NSEQ, HIST])
        tails = m.sb("c_tails", [P, NCONV, 1 + NSEQ, HIST])
        taps_c = m.sb("c_tapsc", [P, NC, W_C])
        hist_c = m.sb("c_histc", [P, NC, NSEQ, HISTC])
        tails_c = m.sb("c_tailsc", [P, NC, 1 + NSEQ, HISTC])
        ps = m.ps("c_ps", [P, 2, NT, 512])

        def pair(name):
            return [m.sem(f"c_{name}{h}") for h in range(2)]

        consts, kept = m.sem("c_consts"), m.sem("c_kept")
        w_loaded, hi_done, lo_done, proj_done = pair("wloaded"), pair("hi"), pair("lo"), pair("proj")
        ps_free, raw_done, hist_done, tail_done = pair("psfree"), pair("raw"), pair("hist"), pair("tail")
        tapped, conv_done, silu_done = pair("tapped"), pair("conv"), pair("silu")
        z_done, out_sent, out_free = pair("z"), pair("sent"), pair("outfree")
        h_done, craw_done, ctapped, yc_done = m.sem("c_h"), m.sem("c_craw"), m.sem("c_ctapped"), m.sem("c_yc")
        chist_done, ctail_done = m.sem("c_chist"), m.sem("c_ctail")
        gates.borrow(ps[:, 1], out[0:64, 0], out[0:64, 1], y[0:64, 0, 0:T], y[0:64, 1, 0:T])
        NB_ALL = NCONV + NZ + 3 * NC
        I_X, I_Z, I_C = NQKV // 2, NCONV // 2, (NCONV + NZ) // 2
        FIRST_C = NCONV + NZ

        def split_hi(act, i, h):
            act.wait_ge(proj_done[h], i + 1)
            act.wait_ge(w_loaded[h], i * 16 + 32)
            copy_hi(act, w_r[0][:, h], w[:, h]).then_inc(hi_done[h], 1)

        def split_lo(dve, i, h):
            dve.wait_ge(hi_done[h], i + 2)
            take_lo(dve, w_r[1][:, h], w[:, h], w_r[0][:, h]).then_inc(lo_done[h], 1)

        with nc.Block() as block:
            @block.sync
            def _(sp):
                for h in range(2):
                    sp.dma_start(w[:, h], io["w_in"][h]).then_inc(w_loaded[h], 16)
                sp.dma_start(taps[:], io["taps"]).then_inc(consts, 16)
                sp.dma_start(hist[:], io["hist_ab"]).then_inc(consts, 16)
                sp.dma_start(taps_c[:], io["taps_c"]).then_inc(consts, 16)
                sp.dma_start(hist_c[:], io["hist_c"]).then_inc(consts, 16)
                with sp.Fori(0, NB_ALL // 2 - 1) as i:
                    for h in range(2):
                        sp.wait_ge(lo_done[h], i + 1)
                        sp.dma_start(w[:, h], io["w_in"][bass.ds(i * 2 + (2 + h), 1)].rearrange(
                            "a p k c -> (a p) k c")).then_inc(w_loaded[h], 16)
                gates.store(sp)
                for h in range(2):
                    sp.wait_ge(out_sent[h], 16 * (I_C - I_X + NC // 2))
                sp.wait_ge(kept, 32)

            @block.tensor
            def _(pe):
                gates.product(pe)
                with pe.Fori(0, NB_ALL // 2) as i:
                    for h in range(2):
                        pe.wait_ge(lo_done[h], i + 1)
                        pe.wait_ge(ps_free[h], i + 1)
                        for n in range(NT):
                            mm = exact_product(pe, ps[:, h, n, 0:TW], lambda x, k: w_r[x][:, h, k, :],
                                               lambda z, k: hn[z][:, k, n * TW:(n + 1) * TW], KD)
                        mm.then_inc(proj_done[h], 1)

            @block.scalar
            def _(act):
                act.sem_inc(ps_free[0], 1)
                for h in range(2):
                    act.sem_inc(raw_done[h], 1)
                    act.sem_inc(silu_done[h], 1)
                    act.wait_ge(w_loaded[h], 16)
                    copy_hi(act, w_r[0][:, h], w[:, h]).then_inc(hi_done[h], 1)
                gates.exponentials(act)
                for first, last in ((0, I_X), (I_X, I_Z)):
                    with act.Fori(first, last) as i:
                        for h in range(2):
                            split_hi(act, i, h)
                            act.wait_ge(conv_done[h], i + 1)
                            act.wait_ge(tail_done[h], i + 1)
                            put_raw(lambda o, s, _: act.copy(o, s), raw[:, h, :], ps[:, h], HIST
                                    ).then_inc(raw_done[h], 1)
                            act.wait_ge(raw_done[h], i + 2)
                            act.sem_inc(ps_free[h], 1)
                            act.wait_ge(conv_done[h], i + 2)
                            if first == I_X:
                                act.wait_ge(out_free[h], i + (1 - I_X))
                                dst = out[:, h, :]
                            else:
                                dst = one(qkv, i * 2 + h)
                            act.activation(dst[:, 0:TP], y[:, h, 0:TP], ACT.Silu)
                            act.activation(dst[:, TP:T].rearrange("p (b t) -> p b t", t=LSEQ),
                                           samples(y[:, h], TP, HIST + LSEQ, HIST, HIST + LSEQ),
                                           ACT.Silu).then_inc(silu_done[h], 1)
                with act.Fori(I_Z, I_C) as i:
                    for h in range(2):
                        split_hi(act, i, h)
                        act.wait_ge(out_free[h], i + (1 - I_X))
                        act.activation(out[:, h, :].rearrange("p (n t) -> p n t", n=NT), ps[:, h, :, 0:TW],
                                       ACT.Silu).then_inc(z_done[h], 1)
                        act.wait_ge(z_done[h], i + (1 - I_Z))
                        act.sem_inc(ps_free[h], 1)
                act.wait_ge(conv_done[0], I_Z + 1)
                act.wait_ge(tail_done[0], I_Z + 1)
                for b in range(3 * NC):
                    i, h = divmod(FIRST_C + b, 2)
                    if b < 3 * NC - 2:
                        split_hi(act, i, h)
                    if b % 3 == 0:
                        act.wait_ge(proj_done[h], i + 1)
                        act.wait_ge(craw_done, b // 3 + 1)
                        act.copy(raw[:, 0, 0:T].rearrange("p (n t) -> p n t", n=NT),
                                 ps[:, h, :, 0:TW]).then_inc(h_done, 1)
                        act.wait_ge(h_done, b // 3 + 1)
                        act.sem_inc(ps_free[h], 1)

            @block.gpsimd
            def _(pool):
                for h in range(2):
                    pool.sem_inc(out_free[h], 1)
                    pool.sem_inc(tail_done[h], 1)
                    pool.memset(raw[:, h, 0:HIST], 0.0).then_inc(hist_done[h], 1)
                pool.wait_ge(consts, 64)

                def send(dst, h, n):
                    pool.dma_start(dst.rearrange("a p t -> (a p) t"), out[:, h, :]).then_inc(out_sent[h], 16)
                    pool.wait_ge(out_sent[h], n)
                    pool.sem_inc(out_free[h], 1)

                for first, last in ((0, I_X), (I_X, I_Z)):
                    with pool.Fori(first, last) as i:
                        for h in range(2):
                            pool.wait_ge(conv_done[h], i + 1)
                            pool.wait_ge(tail_done[h], i + 1)
                            pool.wait_ge(hist_done[h], i + 1)
                            pool.tensor_copy(samples(raw[:, h], HIST + TP, HIST + LSEQ, 0, HIST),
                                             one(hist, i * 2 + h)).then_inc(hist_done[h], 1)
                            pool.wait_ge(raw_done[h], i + 2)
                            keep_tail(pool, tails, i * 2 + h, raw[:, h], HIST).then_inc(tail_done[h], 1)
                            if first == I_X:
                                pool.wait_ge(silu_done[h], i + 2)
                                send(xbc_dram[bass.ds(i * 2 + (h - NQKV), 1)], h, i * 16 + (1 - I_X) * 16)
                for h in range(2):
                    pool.wait_ge(tail_done[h], I_Z + 1)
                pool.dma_start(io["new_hist_ab"], tails[:]).then_inc(kept, 16)
                with pool.Fori(0, NZ // 2) as i:
                    for h in range(2):
                        pool.wait_ge(z_done[h], i + 1)
                        send(z_dram[bass.ds(i * 2 + h, 1)], h, i * 16 + 16 * (I_Z - I_X + 1))
                for h in range(2):
                    pool.wait_ge(conv_done[h], I_Z + 1)
                pool.memset(raw[:, 1, 0:HISTC], 0.0).then_inc(chist_done, 1)
                for b in range(NC):
                    pool.wait_ge(yc_done, b + 1)
                    pool.wait_ge(ctail_done, b + 1)
                    pool.wait_ge(chist_done, b + 1)
                    pool.tensor_copy(samples(raw[:, 1], HISTC + TP, HISTC + LSEQ, 0, HISTC),
                                     hist_c[:, b]).then_inc(chist_done, 1)
                    pool.wait_ge(craw_done, b + 2)
                    pool.tensor_copy(tails_c[:, b, 0, :], raw[:, 1, TP:TP + HISTC])
                    pool.tensor_copy(tails_c[:, b, 1:, :], samples(raw[:, 1], HISTC + TP, HISTC + LSEQ, LSEQ,
                                                                   HISTC + LSEQ)).then_inc(ctail_done, 1)
                    pool.wait_ge(yc_done, b + 2)
                    send(yc_dram[b:b + 1], b % 2, 16 * (I_C - I_X + b // 2 + 1))
                pool.wait_ge(ctail_done, NC + 1)
                pool.dma_start(io["new_hist_c"], tails_c[:]).then_inc(kept, 16)

            @block.vector
            def _(dve):
                gates.constants(dve)
                for h in range(2):
                    dve.sem_inc(conv_done[h], 1)
                    dve.wait_ge(hi_done[h], 1)
                    take_lo(dve, w_r[1][:, h], w[:, h], w_r[0][:, h]).then_inc(lo_done[h], 1)
                dve.sem_inc(craw_done, 1)
                dve.sem_inc(yc_done, 1)
                dve.sem_inc(ctail_done, 1)
                gates.arithmetic(dve, ps_free[1])
                dve.wait_ge(gates.dve_step, 15)
                dve.wait_ge(consts, 64)
                with dve.Fori(0, I_Z) as i:
                    for h in range(2):
                        split_lo(dve, i, h)
                        dve.wait_ge(raw_done[h], i + 2)
                        dve.wait_ge(hist_done[h], i + 2)
                        dve.wait_ge(silu_done[h], i + 1)
                        tap = taps[:, bass.ds(i * 2 + h, 1), :].rearrange("p a t -> p (a t)")
                        dve.tensor_scalar(y[:, h, 0:CONVW], raw[:, h, 0:CONVW], tap[:, 0:1],
                                          tap[:, W_A:W_A + 1], ALU.mult, ALU.add).then_inc(tapped[h], 1)
                        for j in range(1, W_A):
                            dve.wait_ge(tapped[h], i * (W_A - 1) + j)
                            op = dve.scalar_tensor_tensor(y[:, h, 0:CONVW], raw[:, h, j:j + CONVW], tap[:, j:j + 1],
                                                          y[:, h, 0:CONVW], ALU.mult, ALU.add)
                            op.then_inc(tapped[h] if j < W_A - 1 else conv_done[h], 1)
                with dve.Fori(I_Z, I_C) as i:
                    for h in range(2):
                        split_lo(dve, i, h)
                dve.wait_ge(silu_done[0], I_Z + 1)
                dve.wait_ge(tail_done[1], I_Z + 1)
                for b in range(3 * NC):
                    i, h = divmod(FIRST_C + b, 2)
                    c = b // 3
                    if b < 3 * NC - 2:
                        split_lo(dve, i, h)
                    if b % 3 == 1:
                        dve.wait_ge(proj_done[h], i + 1)
                        dve.wait_ge(h_done, c + 1)
                        dve.wait_ge(ctail_done, c + 1)
                        put_raw(lambda o, s, t: dve.tensor_tensor(o, raw[:, 0, t[0]:t[1]] if t[1] <= TP else
                                                                  raw[:, 0, TP:T].rearrange("p (b t) -> p b t", t=LSEQ),
                                                                  s, ALU.mult),
                                raw[:, 1], ps[:, h], HISTC).then_inc(craw_done, 1)
                        dve.wait_ge(craw_done, c + 2)
                        dve.sem_inc(ps_free[h], 1)
                        dve.wait_ge(chist_done, c + 2)
                        dve.tensor_scalar(y[:, 0, 0:CONVWC], raw[:, 1, 0:CONVWC], taps_c[:, c, 0:1], None,
                                          ALU.mult).then_inc(ctapped, 1)
                        for j in range(1, W_C):
                            dve.wait_ge(ctapped, c * W_C + j)
                            dve.scalar_tensor_tensor(y[:, 0, 0:CONVWC], raw[:, 1, j:j + CONVWC], taps_c[:, c, j:j + 1],
                                                     y[:, 0, 0:CONVWC], ALU.mult, ALU.add).then_inc(ctapped, 1)
                    if b % 3 == 2:
                        dve.wait_ge(ctapped, (c + 1) * W_C)
                        dve.wait_ge(proj_done[h], i + 1)
                        dve.wait_ge(out_free[c % 2], c // 2 + (I_C - I_X + 1))
                        o = out[:, c % 2]
                        dve.tensor_tensor(o[:, 0:2 * TW].rearrange("p (n t) -> p n t", n=2),
                                          y[:, 0, 0:2 * TW].rearrange("p (n t) -> p n t", n=2),
                                          ps[:, h, 0:2, 0:TW], ALU.mult)
                        dve.tensor_tensor(o[:, 2 * TW:TP], y[:, 0, 2 * TW:TP], ps[:, h, 2, 0:TAIL], ALU.mult)
                        dve.tensor_tensor(o[:, TP:T].rearrange("p (b t) -> p b t", t=LSEQ),
                                          samples(y[:, 0], TP, HISTC + LSEQ, HISTC, HISTC + LSEQ),
                                          ps[:, h, 2, TAIL:TW].rearrange("p (b t) -> p b t", t=LSEQ),
                                          ALU.mult).then_inc(yc_done, 1)
                        dve.wait_ge(yc_done, c + 2)
                        dve.sem_inc(ps_free[h], 1)


class Steps:

    def __init__(self, m, name, names, ahead=1):
        self.sem, self.names, self.n, self.ahead = m.sem(name), names, len(names), ahead

    def start(self, eng):
        eng.sem_inc(self.sem, self.n * self.ahead)

    def at(self, r, name, back=0):
        return r * self.n + (self.n * (self.ahead - back) + self.names.index(name) + 1)


def bc(col, n):
    return col.unsqueeze(2).to_broadcast([col.shape[0], col.shape[1], n])


class RowNorm:
    RING = 3

    def __init__(self, m, name, n_rows, group, weight, dram):
        self.n, self.group, self.weight, self.dram = n_rows, group, weight, dram
        self.pick = m.sb(name + "_pick", [P, n_rows, n_rows])
        self.rows = m.sb(name + "_rows", [n_rows, T])
        self.eps = m.sb(name + "_epscol", [n_rows, 1])
        self.wide = m.sb(name + "_wide", [P, self.RING, T])
        self.sums = m.ps(name + "_sums", [n_rows, NT, 512])
        self.set, self.sent = m.sem(name + "_set"), m.sem(name + "_sent")
        self.loaded = [m.sem(f"{name}_wide{r}") for r in range(self.RING)]

    def constants(self, dve):
        dve.memset(self.pick[:], 0.0).then_inc(self.set, 1)
        dve.wait_ge(self.set, 1)
        for g in range(self.n):
            dve.memset(self.pick[:, g, g:g + 1], self.weight[g]).then_inc(self.set, 1)

    def root(self, act):
        return act.activation(self.rows[:].rearrange("p (n t) -> p n t", n=NT), self.sums[:, :, 0:TW], ACT.Sqrt,
                              bias=self.eps[:])

    def sum(self, pe, b, squares):
        for n in range(NT):
            mm = pe.matmul(self.sums[:, n, 0:TW], self.pick[:, self.group[b], :], squares[:, n * TW:(n + 1) * TW],
                           start=(b == 0), stop=(b == len(self.group) - 1))
        return mm

    def spread(self, sp, ready, used):
        sp.wait_ge(*ready)
        sp.dma_start(self.dram[0:self.n], self.rows[:]).then_inc(self.sent, 16)
        sp.wait_ge(self.sent, 16)
        for g in range(self.n):
            if g >= self.RING:
                sp.wait_ge(used, g - self.RING + 1)
            sp.dma_start(self.wide[:, g % self.RING, :], self.dram[g].partition_broadcast(P)
                         ).then_inc(self.loaded[g % self.RING], 16)

    def row(self, dve, g):
        dve.wait_ge(self.loaded[g % self.RING], 16 * (g // self.RING + 1))
        return self.wide[:, g % self.RING, :]


class Columns:

    def __init__(self, m):
        self.g, self.beta = m.sb("col_g", [CH, NCH + 1, NR]), m.sb("col_beta", [CH, NCH, HA])
        self.dt, self.er = m.sb("col_dt", [CH, NCH, HB]), m.sb("col_er", [CH, NCH, NR])


def qk_norm_phase(nc, qkv, xbc, rows, columns, masks, xbc_dram, norm_dram):
    CB = 4
    with ExitStack() as stack:
        m = Memory(nc, stack)
        NQK = 2 * HA
        sq = m.sb("n_sq", [P, 2, T])
        norm = RowNorm(m, "n", NQK, list(range(NQK)), [float(DK)] * HA + [1.0] * HA, norm_dram)
        xbc_back, rooted = m.sem("n_xbc"), m.sem("n_rooted")
        squared, scaled = m.sem("n_squared"), m.sem("n_scaled")
        pe_done, turned, cols_done = m.sem("n_pe"), m.sem("n_turned"), m.sem("n_cols")
        cols_ps, gr = m.ps("n_cols_ps", [P, CB, 512]), slice(ROW_G, ROW_G + NR)
        block = stack.enter_context(nc.Block())

        @block.sync
        def _(sp):
            sp.dma_start(xbc[:], xbc_dram.rearrange("b p t -> p b t")).then_inc(xbc_back, 16)
            norm.spread(sp, (rooted, 2), scaled)
            sp.wait_ge(xbc_back, 16)

        @block.scalar
        def _(act):
            for b in range(NQK):
                if b >= 2:
                    act.wait_ge(pe_done, b - 1)
                act.activation(sq[:, b % 2, :], qkv[:, b, :], ACT.Square).then_inc(squared, 1)
            act.wait_ge(norm.set, 3 + NQK)
            act.wait_ge(pe_done, NQK)
            norm.root(act).then_inc(rooted, 1)
            for c in range(NCH):
                act.wait_ge(turned, c + 1)
                at = cols_ps[0:CH, c % CB, 0:3 * P].rearrange("p (r c) -> p r c", r=3)
                act.copy(columns.g[:, c, :], at[:, 0, gr])
                act.copy(columns.beta[:, c, :], at[:, 0, 0:HA])
                act.activation(columns.er[:, c, :], at[:, 1, gr], ACT.Exp)
                act.copy(columns.dt[:, c, :], at[:, 2, ROW_G + HA:ROW_G + NR]).then_inc(cols_done, 1)

        @block.tensor
        def _(pe):
            pe.wait_ge(norm.set, 1 + NQK)
            for b in range(NQK):
                pe.wait_ge(squared, b + 1)
                norm.sum(pe, b, sq[:, b % 2, :]).then_inc(pe_done, 1)
            for c in range(NCH):
                if c >= CB:
                    pe.wait_ge(cols_done, c - CB + 1)
                for i, row in enumerate(rows):
                    mm = pe.transpose(cols_ps[0:CH, c % CB, i * P:(i + 1) * P], row[:, c * CH:(c + 1) * CH],
                                      masks[:, 0, :])
                mm.then_inc(turned, 1)

        @block.vector
        def _(dve):
            norm.constants(dve)
            dve.memset(norm.eps[:], EPS).then_inc(norm.set, 1)
            dve.wait_ge(norm.set, 2 + NQK)
            dve.memset(norm.eps[0:HA], DK * EPS).then_inc(norm.set, 1)
            dve.wait_ge(rooted, 1)
            dve.reciprocal(norm.rows[:], norm.rows[:]).then_inc(rooted, 1)
            for b in range(NQK):
                dve.tensor_tensor(qkv[:, b, :], qkv[:, b, :], norm.row(dve, b), ALU.mult).then_inc(scaled, 1)


REC_PE = ["k", "v", "kk", "qk", "mt0", "mt1", "m2_0", "m2t0", "m2_1", "m2t1", "xt", "m4_0", "m4t0", "r1_0",
          "m4_1", "m4t1", "r1_1", "btcb", "m8_0", "r2_0", "m8_1", "r2_1", "r3_0", "r3_1", "sy",
          "td0", "y0", "yt0", "td1", "y1", "yt1", "sds", "y2_0", "y2t0", "y2_1", "y2t1", "y4_0", "z1_0", "y4_1", "z1_1",
          "z2_0", "z2_1", "tt0", "tt1", "u0", "wk0", "u1", "wk1", "w0", "w1", "o0", "ds0", "o1", "ds1"]
REC_DVE = ["mk", "m", "m16", "kbg", "kd", "vb", "r0_0", "r0_1", "lm", "m2t0", "m2t1", "qkt", "xdt",
           "m4t0", "r1_0", "m4t1", "r1_1", "bt", "cbt", "r2_0", "r2_1", "qg", "xdd", "cs", "r3_0", "r3_1",
           "yt0", "vv0", "yt1", "vv1", "sy", "y2t0", "y2t1", "s_decayed", "ss_decayed", "z1_0", "z1_1", "ss",
           "z2_0", "z2_1", "u0", "u1", "w0", "w1", "s0", "s1"]
REC_ACT = ["mt0", "mt1", "m2_0", "m2_1", "m4_0", "m4_1", "eb", "m8_0", "m8_1", "td0", "y0", "td1", "y1",
           "y2_0", "y2_1", "y4_0", "y4_1", "tt0", "tt1", "wk0", "wk1", "o0", "o1"]
REC_POOL = ["k_st", "v_st", "b_st", "x_st"]


def recurrence_phase(nc, io, qkv, xbc, columns, g_dram, masks, slots_dram):
    L, HP, HPG = CH, HA // 2, HB // GB
    with ExitStack() as stack:
        m = Memory(nc, stack)
        p, v, a = Steps(m, "rc_pe", REC_PE), Steps(m, "rc_dve", REC_DVE), Steps(m, "rc_act", REC_ACT)
        q = Steps(m, "rc_pool", REC_POOL)
        dp, da = Steps(m, "rc_dpool", ["all", "all_masked", "diff", "diff_masked"]), Steps(m, "rc_dact", ["dec_t", "dec"])
        gb_loaded, eb_loaded, const_loaded, moved = m.sem("rc_gb"), m.sem("rc_ebl"), m.sem("rc_const"), m.sem("rc_moved")
        zeros_sent, dve_set, kb_exp = m.sem("rc_zsent"), m.sem("rc_set"), m.sem("rc_kb")

        def sb(name, shape):
            return m.sb("rc_" + name, shape)

        heads = [L, HA, L]
        g_all, beta_all, dt_all, er_all = columns.g, columns.beta, columns.dt, columns.er
        kb_all = sb("kball", [L, NCH, HA])
        gb, eb = sb("gb", [L, NR, L]), sb("eb", [P, NR, L])
        dec_t, dec = sb("dect", [L, NR, L]), sb("dec", heads)
        kst, vst, bst, xst = sb("kst", [P, HA, L]), sb("vst", [P, HA, L]), sb("bst", [P, GB, L]), sb("xst", [P, 4, L])
        kbg, kd, vb = sb("kbg", [L, HA, DK]), sb("kd", [L, HA, DK]), sb("vb", [L, HA, DK])
        M, M16, lm = sb("m", heads), sb("m16", heads), sb("lm", heads)
        mt, m2, m2t, m4, m4t, m8 = (sb(x, heads) for x in ("mt", "m2", "m2t", "m4", "m4t", "m8"))
        r0, r1, r2, r3, td = (sb(x, heads) for x in ("r0", "r1", "r2", "r3", "td"))
        y, yt, y2, y2t, y4 = m2, m2t, m4, m4t, m8
        vv, z1, z2, tt = r0, r1, r2, mt
        qkt, qg = sb("qkt", heads), sb("qg", [P, HA, L])
        U, wk, w = sb("u", [L, HA, DK]), sb("wk", [P, HA, L]), sb("w", [L, HA, DK])
        S, S1 = sb("s", [P, HA, DK]), sb("s1", [P, HA, DK])
        bt, xdt, xdd = sb("bt", [L, GB, NB]), sb("xdt", [L, HB, PB]), sb("xdd", [L, HB, PB])
        cbt, cs = sb("cbt", [L, HB, L]), sb("cs", [P, HB, L])
        SS, SS1, skip = sb("ss", [P, HB, PB]), sb("ss1", [P, HB, PB]), sb("skip", [P, 4])
        zeros = sb("zeros", [P, D])
        zero_tiles = slots_dram.rearrange("(c n p) d -> c p n d", p=P, c=NCH)

        bank = [m.ps(f"rc_ps{i}", [P, 512]) for i in range(8)]
        X, Y, Z = (5, 0), (6, 1), (7, 2)
        K, V, KK, QK = bank[1], bank[2], bank[3], bank[4]

        def sq_(b, n=HP):
            return b[0:L, 0:n * L].rearrange("p (h t) -> p h t", h=n)

        def wide(b, n=HP):
            return b[0:L, 0:n * DK].rearrange("p (h t) -> p h t", h=n)

        def tall(b):
            return b[:, 0:HP * L].rearrange("p (h t) -> p h t", h=HP)

        xt_ps = KK[0:L, :].rearrange("p (h t) -> p h t", t=PB)
        cb_ps = QK[0:L, 0:GB * L].rearrange("p (g t) -> p g t", g=GB)
        bt_ps = QK[0:L, GB * L:GB * (L + NB)].rearrange("p (g s) -> p g s", g=GB)
        sy_ps = KK[:, 0:4 * L].rearrange("p (n t) -> p n t", n=4)
        full, ident, neg_t, neg = masks[:, 0, :], masks[0:L, 0, 0:L], masks[0:L, 1, 0:L], masks[0:L, 2, 0:L]
        same16 = masks[0:L, 3, 0:L]

        def pair(g):
            return slice(g * HP, (g + 1) * HP)

        def over(mask, n):
            return mask.unsqueeze(1).to_broadcast([L, n, L])

        def tokens(ap, c):
            return ap[:, :, bass.ds(c * CH, CH)]

        block = stack.enter_context(nc.Block())

        @block.sync
        def _(sp):
            sp.dma_start(skip[:], io["d_skip"]).then_inc(const_loaded, 16)
            sp.dma_start(gb[:], g_dram[:, 0:CH].partition_broadcast(L)).then_inc(gb_loaded, 16)
            sp.wait_ge(dve_set, 1)
            with sp.Fori(0, NCH) as c:
                sp.wait_ge(v.sem, v.at(c, "ss_decayed", 1))
                sp.dma_start(eb[:], g_dram[:, bass.ds(c * CH, CH)].partition_broadcast(P)).then_inc(eb_loaded, 16)
                sp.wait_ge(dp.sem, dp.at(c, "diff"))
                sp.dma_start(gb[:], g_dram[:, bass.ds(c * CH + CH, CH)].partition_broadcast(L)).then_inc(gb_loaded, 16)
                sp.dma_start(zero_tiles[bass.ds(c, 1)].rearrange("c p n d -> (c p) n d"),
                             zeros[:].unsqueeze(1).to_broadcast([P, zero_tiles.shape[2], D])).then_inc(zeros_sent, 16)
            sp.wait_ge(v.sem, v.at(NCH - 1, "s1"))
            sp.dma_start(io["new_gdn_p"], S[:]).then_inc(moved, 16)
            sp.dma_start(io["new_ssd_p"], SS[:]).then_inc(moved, 16)
            sp.wait_ge(moved, 32)
            sp.wait_ge(zeros_sent, 16 * NCH)

        @block.gpsimd
        def _(pool):
            q.start(pool)
            dp.start(pool)

            def wait(steps, c, name, back=0):
                pool.wait_ge(steps.sem, steps.at(c, name, back))

            def differences(r):
                pool.wait_ge(gb_loaded, r * 16 + 16)
                g = one(g_all, r)
                pool.tensor_tensor(dec_t[:], gb[:], bc(g, L), ALU.subtract).then_inc(dp.sem, 1)
                wait(dp, r, "all")
                pool.tensor_tensor(dec_t[:], dec_t[:], over(neg_t, NR), ALU.add).then_inc(dp.sem, 1)
                pool.tensor_tensor(dec[:], bc(g[:, 0:HA], L), gb[:, 0:HA, :], ALU.subtract).then_inc(dp.sem, 1)
                wait(dp, r, "diff")
                pool.tensor_tensor(dec[:], dec[:], over(neg, HA), ALU.add).then_inc(dp.sem, 1)

            def stage(c):
                pool.tensor_copy(kst[:], tokens(qkv[:, HA:2 * HA], c)).then_inc(q.sem, 1)
                pool.tensor_copy(vst[:], tokens(qkv[:, 2 * HA:3 * HA], c)).then_inc(q.sem, 1)
                pool.tensor_copy(bst[:], tokens(xbc[:, AT_B:AT_B + GB], c)).then_inc(q.sem, 1)
                pool.tensor_copy(xst[:], tokens(xbc[:, AT_X:AT_X + 4], c)).then_inc(q.sem, 1)

            stage(0)
            pool.wait_ge(dve_set, 2)
            differences(0)
            with pool.Fori(0, NCH - 1) as c:
                wait(v, c, "cbt")
                differences(c + 1)
                stage(c + 1)
            wait(v, NCH - 1, "cbt")
            differences(NCH)

        @block.scalar
        def _(act):
            a.start(act)
            da.start(act)

            def wait(steps, c, name, back=0):
                act.wait_ge(steps.sem, steps.at(c, name, back))

            def decays(r):
                wait(dp, r, "all_masked")
                act.activation(dec_t[:], dec_t[:], ACT.Exp).then_inc(da.sem, 1)
                wait(dp, r, "diff_masked")
                act.activation(dec[:], dec[:], ACT.Exp).then_inc(da.sem, 1)

            act.activation(kb_all[:], g_all[:, 0:NCH, 0:HA], ACT.Exp).then_inc(kb_exp, 1)
            decays(0)

            with act.Fori(0, NCH) as c:
                def take(names, dst, bank_of, view):
                    for g in range(2):
                        wait(p, c, f"{names}{g}")
                        act.copy(dst[:, pair(g), :], view(bank[bank_of[g]])).then_inc(a.sem, 1)

                take("mt", mt, X, sq_)
                take("m2_", m2, Y, sq_)
                take("m4_", m4, Y, sq_)
                act.wait_ge(eb_loaded, c * 16 + 16)
                act.activation(eb[:], eb[:], ACT.Exp).then_inc(a.sem, 1)
                take("m8_", m8, Y, sq_)
                for g in range(2):
                    wait(p, c, f"td{g}")
                    act.copy(td[:, pair(g), :], sq_(bank[Y[g]])).then_inc(a.sem, 1)
                    wait(p, c, f"y{g}")
                    act.copy(y[:, pair(g), :], sq_(bank[Z[g]])).then_inc(a.sem, 1)
                take("y2_", y2, Y, sq_)
                take("y4_", y4, Y, sq_)
                decays(c + 1)
                take("tt", tt, Y, sq_)
                for g in range(2):
                    wait(p, c, f"wk{g}")
                    act.mul(wk[:, pair(g), :], tall(bank[Z[g]]), -1.0).then_inc(a.sem, 1)
                for g in range(2):
                    wait(p, c, f"o{g}")
                    act.copy(tokens(qkv[:, pair(g)], c), tall(bank[X[g]])).then_inc(a.sem, 1)

        @block.vector
        def _(dve):
            v.start(dve)

            def wait(steps, c, name, back=0):
                dve.wait_ge(steps.sem, steps.at(c, name, back))

            def tt_(dst, x, z, op):
                dve.tensor_tensor(dst, x, z, op).then_inc(v.sem, 1)

            dve.memset(zeros[:], 0.0).then_inc(dve_set, 1)
            dve.memset(g_all[:, NCH, :], 0.0).then_inc(dve_set, 1)
            dve.memset(S[:], 0.0).then_inc(dve_set, 1)
            dve.memset(SS[:], 0.0).then_inc(dve_set, 1)
            dve.wait_ge(const_loaded, 16)
            dve.wait_ge(dve_set, 4)
            dve.wait_ge(kb_exp, 1)
            dve.tensor_tensor(kb_all[:], kb_all[:], beta_all[:], ALU.mult).then_inc(dve_set, 1)
            dve.wait_ge(dve_set, 5)

            with dve.Fori(0, NCH) as c:
                beta, kb, dt, er = one(beta_all, c), one(kb_all, c), one(dt_all, c), one(er_all, c)

                def add(name, dst, bank_of, other):
                    for g in range(2):
                        wait(p, c, f"{name}{g}")
                        tt_(dst[:, pair(g), :], sq_(bank[bank_of[g]]), other[:, pair(g), :], ALU.add)

                def take(name, dst, bank_of, view=sq_):
                    for g in range(2):
                        wait(p, c, f"{name}{g}")
                        dve.tensor_copy(dst[:, pair(g), :], view(bank[bank_of[g]])).then_inc(v.sem, 1)

                wait(da, c, "dec")
                wait(p, c, "kk")
                dve.scalar_tensor_tensor(M[:], sq_(KK, HA), -1.0, dec[:], ALU.mult, ALU.mult).then_inc(v.sem, 1)
                wait(v, c, "mk")
                tt_(M[:], M[:], bc(beta, L), ALU.mult)
                wait(v, c, "m")
                tt_(M16[:], M[:], over(same16, HA), ALU.mult)
                tt_(kbg[:], wide(K, HA), bc(kb, DK), ALU.mult)
                tt_(kd[:], wide(K, HA), bc(er[:, 0:HA], DK), ALU.mult)
                tt_(vb[:], wide(V, HA), bc(beta, DK), ALU.mult)
                for g in range(2):
                    wait(a, c, f"mt{g}")
                    tt_(r0[:, pair(g), :], mt[:, pair(g), :], over(ident, HP), ALU.add)
                wait(v, c, "m16")
                tt_(lm[:], M[:], M16[:], ALU.subtract)
                take("m2t", m2t, Z)
                wait(p, c, "qk")
                tt_(qkt[:], sq_(QK, HA), dec_t[:, 0:HA, :], ALU.mult)
                wait(p, c, "xt")
                tt_(xdt[:], xt_ps, bc(dt, PB), ALU.mult)
                for g in range(2):
                    wait(p, c, f"m4t{g}")
                    dve.tensor_copy(m4t[:, pair(g), :], sq_(bank[Z[g]])).then_inc(v.sem, 1)
                    wait(p, c, f"r1_{g}")
                    tt_(r1[:, pair(g), :], sq_(bank[X[g]]), r0[:, pair(g), :], ALU.add)
                wait(p, c, "btcb")
                dve.tensor_copy(bt[:], bt_ps).then_inc(v.sem, 1)
                for g in range(GB):
                    hs = slice(g * HPG, (g + 1) * HPG)
                    ins = dve.tensor_tensor(cbt[:, hs, :], cb_ps[:, g:g + 1, :].to_broadcast([L, HPG, L]),
                                            dec_t[:, HA + g * HPG:HA + (g + 1) * HPG, :], ALU.mult)
                ins.then_inc(v.sem, 1)
                wait(v, c, "r1_1")
                add("r2_", r2, Z, r1)
                wait(a, c, "eb")
                tt_(qg[:], tokens(qkv[:, 0:HA], c), eb[:, 0:HA, :], ALU.mult)
                wait(v, c, "xdt")
                tt_(xdd[:], xdt[:], bc(er[:, HA:NR], PB), ALU.mult)
                for g in range(GB):
                    hs = slice(g * HPG, (g + 1) * HPG)
                    cg = tokens(xbc[:, AT_C + g:AT_C + g + 1], c)
                    ins = dve.tensor_tensor(cs[:, hs, :], cg.to_broadcast([P, HPG, L]),
                                            eb[:, HA + g * HPG:HA + (g + 1) * HPG, :], ALU.mult)
                ins.then_inc(v.sem, 1)
                wait(v, c, "r2_1")
                add("r3_", r3, X, r2)
                for g in range(2):
                    wait(p, c, f"yt{g}")
                    dve.tensor_copy(yt[:, pair(g), :], sq_(bank[X[g]])).then_inc(v.sem, 1)
                    tt_(vv[:, pair(g), :], sq_(bank[X[g]]), over(ident, HP), ALU.add)
                wait(p, c, "sy")
                for n in range(4):
                    x = tokens(xbc[:, AT_X + n:AT_X + n + 1], c)
                    ins = dve.scalar_tensor_tensor(x, x, skip[:, n:n + 1], sy_ps[:, n:n + 1, :], ALU.mult, ALU.add)
                ins.then_inc(v.sem, 1)
                take("y2t", y2t, Z)
                wait(v, c, "s1", 1)
                tt_(S1[:], S[:], eb[:, 0:HA, L - 1:L].to_broadcast([P, HA, DK]), ALU.mult)
                tt_(SS1[:], SS[:], eb[:, HA:NR, L - 1:L].to_broadcast([P, HB, PB]), ALU.mult)
                wait(v, c, "vv1")
                add("z1_", z1, X, vv)
                wait(p, c, "sds")
                wait(v, c, "ss_decayed")
                tt_(SS[:], QK[:].rearrange("p (h t) -> p h t", t=PB), SS1[:], ALU.add)
                wait(v, c, "z1_1")
                add("z2_", z2, Z, z1)
                take("u", U, X, wide)
                wait(v, c, "u1")
                for g in range(2):
                    wait(p, c, f"w{g}")
                    tt_(w[:, pair(g), :], wide(bank[Y[g]]), U[:, pair(g), :], ALU.add)
                for g in range(2):
                    wait(p, c, f"ds{g}")
                    tt_(S[:, pair(g), :], (KK, QK)[g][:, 0:HP * DK].rearrange("p (h t) -> p h t", h=HP),
                        S1[:, pair(g), :], ALU.add)

        @block.tensor
        def _(pe):
            p.start(pe)

            def wait(steps, c, name, back=0):
                pe.wait_ge(steps.sem, steps.at(c, name, back))

            def products(dst, lhs, rhs, hs):
                for j, h in enumerate(hs):
                    mm = pe.matmul(dst[:, j, :], lhs[:, h, :], rhs[:, h, :], start=True, stop=True)
                return mm

            def turn(dst, src, ident_, hs):
                for j, h in enumerate(hs):
                    mm = pe.transpose(dst[:, j, :], src[:, h, :], ident_)
                return mm

            pe.wait_ge(dve_set, 4)

            with pe.Fori(0, NCH) as c:
                H = (range(0, HP), range(HP, HA))

                def prod(bank_of, lhs, rhs, g, view=sq_):
                    products(view(bank[bank_of[g]]), lhs, rhs, H[g]).then_inc(p.sem, 1)

                wait(q, c, "k_st")
                wait(v, c, "w1", 1)
                turn(wide(K, HA), kst, full, range(HA)).then_inc(p.sem, 1)
                wait(q, c, "v_st")
                wait(a, c, "wk1", 1)
                turn(wide(V, HA), vst, full, range(HA)).then_inc(p.sem, 1)
                wait(v, c, "s1", 1)
                products(sq_(KK, HA), kst, kst, range(HA)).then_inc(p.sem, 1)
                for h in range(HA):
                    mm = pe.matmul(sq_(QK, HA)[:, h, :], kst[:, h, :], qkv[:, h, bass.ds(c * CH, CH)], start=True, stop=True)
                mm.then_inc(p.sem, 1)
                wait(v, c, "m16")
                wait(a, c, "o1", 1)
                for g in range(2):
                    turn(sq_(bank[X[g]]), M16, ident, H[g]).then_inc(p.sem, 1)
                for g in range(2):
                    wait(a, c, f"mt{g}")
                    if g == 1:
                        wait(v, c, "vb")
                    prod(Y, mt, M16, g)
                    prod(Z, M16, mt, g)
                wait(q, c, "x_st")
                for n in range(4):
                    mm = pe.transpose(KK[0:L, n * P:(n + 1) * P], xst[:, n, :], full)
                mm.then_inc(p.sem, 1)
                for g in range(2):
                    wait(a, c, f"m2_{g}")
                    wait(v, c, f"m2t{g}")
                    prod(Y, m2t, m2, g)
                    prod(Z, m2, m2t, g)
                    prod(X, m2, r0, g)
                wait(v, c, "qkt")
                for g in range(GB):
                    pe.transpose(bt_ps[:, g, :], bst[:, g, :], full)
                for g in range(GB):
                    mm = pe.matmul(cb_ps[:, g, :], bst[:, g, :], xbc[:, AT_C + g, bass.ds(c * CH, CH)],
                                   start=True, stop=True)
                mm.then_inc(p.sem, 1)
                for g in range(2):
                    wait(a, c, f"m4_{g}")
                    wait(v, c, f"r1_{g}")
                    prod(Y, m4t, m4, g)
                    prod(Z, m4, r1, g)
                for g in range(2):
                    wait(a, c, f"m8_{g}")
                    wait(v, c, f"r2_{g}")
                    prod(X, m8, r2, g)
                wait(v, c, "cs")
                for h in range(HB):
                    half = slice((h % 2) * PB, (h % 2 + 1) * PB)
                    pe.matmul(sy_ps[half, h // 2, :], xdt[:, h, :], cbt[:, h, :], start=True, stop=False)
                    mm = pe.matmul(sy_ps[half, h // 2, :], SS[:, h, :], cs[:, h, :], start=False, stop=True)
                mm.then_inc(p.sem, 1)
                for g in range(2):
                    wait(v, c, f"r3_{g}")
                    turn(sq_(bank[Y[g]]), r3, ident, H[g]).then_inc(p.sem, 1)
                    prod(Z, r3, lm, g)
                    prod(X, lm, r3, g)
                W = HPG * PB
                for g in range(GB):
                    mm = pe.matmul(QK[:, g * W:(g + 1) * W], bt[:, g, :],
                                   xdd[:, g * HPG:(g + 1) * HPG, :].rearrange("p h t -> p (h t)"), start=True, stop=True)
                mm.then_inc(p.sem, 1)
                for g in range(2):
                    wait(a, c, f"y{g}")
                    wait(v, c, f"yt{g}")
                    prod(Y, yt, y, g)
                    prod(Z, y, yt, g)
                for g in range(2):
                    wait(a, c, f"y2_{g}")
                    wait(v, c, f"y2t{g}")
                    prod(Y, y2t, y2, g)
                    prod(X, y2, vv, g)
                for g in range(2):
                    wait(a, c, f"y4_{g}")
                    wait(v, c, f"z1_{g}")
                    prod(Z, y4, z1, g)
                for g in range(2):
                    wait(v, c, f"z2_{g}")
                    prod(Y, td, z2, g)
                for g in range(2):
                    wait(a, c, f"tt{g}")
                    prod(X, tt, vb, g, wide)
                    prod(Z, kbg, tt, g, tall)
                for g in range(2):
                    wait(a, c, f"wk{g}")
                    prod(Y, wk, S, g, wide)
                for g in range(2):
                    wait(v, c, f"w{g}")
                    o = tall(bank[X[g]])
                    for j, h in enumerate(H[g]):
                        pe.matmul(o[:, j, :], S[:, h, :], qg[:, h, :], start=True, stop=False)
                        mm = pe.matmul(o[:, j, :], w[:, h, :], qkt[:, h, :], start=False, stop=True)
                    mm.then_inc(p.sem, 1)
                    if g == 0:
                        wait(v, c, "ss")
                    products((KK, QK)[g][:, 0:HP * DK].rearrange("p (h t) -> p h t", h=HP), kd, w, H[g]
                             ).then_inc(p.sem, 1)


SAM_PE = ["rows", "k", "v", "kk", "qk", "mt", "m2", "m2t", "bt", "xt", "cb", "m4", "r1", "r2", "u", "wk",
          "w_state", "w_turned", "o", "o_state", "sy", "sy_state"] + [f"ds{h}" for h in range(HA)] + ["sds0", "sds1"]
SAM_DVE = ["diff_t", "masked_t", "diff", "masked", "kb", "kbg", "kd", "vb", "qkt", "qg", "mk", "m", "r0", "m2t", "r1",
           "r2", "xdt", "xdd", "cbt", "cs", "u", "decayed0", "decayed1", "sspread0", "w", "spread0", "spread1", "o",
           "sy_skip", "sy", "s0", "spread2", "decayed2", "s1", "spread3", "decayed3", "s2", "s3",
           "ss_decayed", "ss0", "sspread1", "ss1"]
SAM_ACT = ["rows_st", "cols", "ecol", "ercol", "eb", "dec_t", "dec", "mt", "m2", "bt", "m4", "wk", "w_state", "o_state",
           "sy_state"]
SAM_POOL = ["k_st", "v_st", "b_st", "x_st"]


def sampled_phase(nc, io, qkv, xbc, rows, g_dram, masks):
    L, HPG = TS, HB // GB
    W = HPG * PB
    with ExitStack() as stack:
        m = Memory(nc, stack)
        p, v, a = Steps(m, "ds_pe", SAM_PE, 0), Steps(m, "ds_dve", SAM_DVE, 0), Steps(m, "ds_act", SAM_ACT, 0)
        q = Steps(m, "ds_pool", SAM_POOL, 0)
        gb_loaded, state_moved, sstate_moved = m.sem("ds_gb"), m.sem("ds_state"), m.sem("ds_sstate")
        skip_loaded = m.sem("ds_skipl")

        def sb(name, shape):
            return m.sb("ds_" + name, shape)

        heads = [L, HA, L]
        kst, vst, bst, xst = sb("kst", [P, HA, L]), sb("vst", [P, HA, L]), sb("bst", [P, GB, L]), sb("xst", [P, 4, L])
        rst = sb("rst", [P, 3, L])
        gb, eb, diff_t, diff = sb("gb", [P, NR, L]), sb("eb", [P, NR, L]), sb("difft", [L, NR, L]), sb("diff", heads)
        cols, ecol, ercol, kb = sb("cols", [L, 3, 64]), sb("ecol", [L, NR]), sb("ercol", [L, NR]), sb("kb", [L, HA])
        kbg, kd, vb = sb("kbg", [L, HA, DK]), sb("kd", [L, HA, DK]), sb("vb", [L, HA, DK])
        qkt, qg = sb("qkt", heads), sb("qg", [P, HA, L])
        M, mt, r0, r1 = (sb(x, heads) for x in ("m", "mt", "r0", "r1"))
        m2, m2t, m4 = sb("m2", heads), sb("m2t", heads), sb("m4", heads)
        r2 = m2t
        U, wk, w = sb("u", [L, HA, DK]), sb("wk", [P, HA, L]), sb("w", [L, HA, DK])
        S, S1, spread = sb("s", [P, NSEQ, HA, DK]), sb("s1", [P, 2, NSEQ, DK]), sb("spread", [L, 2, NSEQ, DK])
        wst, ost = sb("wst", [P, HA, L]), sb("ost", [P, HA, L])
        bt, xdt, xdd = sb("bt", [L, GB, NB]), sb("xdt", [L, HB, PB]), sb("xdd", [L, HB, PB])
        cbt, cs, skip = sb("cbt", [L, HB, L]), sb("cs", [P, HB, L]), sb("skip", [P, 4])
        yst = wst
        SS, sspread = sb("ss", [P, NSEQ, HB, PB]), sb("sspread", [L, NSEQ, W])
        bank = [m.ps(f"ds_ps{i}", [P, 512]) for i in range(8)]

        def sq_(i):
            return bank[i][0:L, 0:HA * L].rearrange("p (h t) -> p h t", h=HA)

        def wide(i):
            return bank[i][0:L, :].rearrange("p (h t) -> p h t", h=HA)

        def tall(i):
            return bank[i][:, 0:HA * L].rearrange("p (h t) -> p h t", h=HA)

        xt_ps = bank[2][0:L, :].rearrange("p (h t) -> p h t", t=PB)
        cb_ps = bank[3][0:L, 0:GB * L].rearrange("p (g t) -> p g t", g=GB)
        full, ident, neg_t, neg = masks[:, 0, :], masks[0:L, 0, 0:L], masks[0:L, 4, 0:L], masks[0:L, 5, 0:L]
        col_g, col_b, col_dt = cols[:, 0, ROW_G:ROW_G + NR], cols[:, 0, 0:HA], cols[:, 2, ROW_G + HA:ROW_G + NR]
        seq_of = masks[0:TS, 6, 0:NSEQ].unsqueeze(2)

        def over(mask, n):
            return mask.unsqueeze(1).to_broadcast([L, n, L])

        def sampled(ap):
            return ap[..., TP:T]

        def waiter(eng):
            return lambda steps, name: eng.wait_ge(steps.sem, steps.at(0, name))

        block = stack.enter_context(nc.Block())

        @block.sync
        def _(sp):
            wait = waiter(sp)
            sp.dma_start(gb[:], g_dram[:, TP:T].partition_broadcast(P)).then_inc(gb_loaded, 16)
            sp.dma_start(S[:], io["state_gdn"]).then_inc(state_moved, 16)
            sp.dma_start(SS[:], io["state_ssd"]).then_inc(sstate_moved, 16)
            sp.dma_start(skip[:], io["d_skip"]).then_inc(skip_loaded, 16)
            wait(v, f"s{HA - 1}")
            sp.dma_start(io["new_gdn_s"], S[:]).then_inc(state_moved, 16)
            wait(v, "ss1")
            sp.dma_start(io["new_ssd_s"], SS[:]).then_inc(sstate_moved, 16)
            sp.wait_ge(state_moved, 32)
            sp.wait_ge(sstate_moved, 32)

        @block.gpsimd
        def _(pool):
            pool.tensor_copy(kst[:], sampled(qkv[:, HA:2 * HA])).then_inc(q.sem, 1)
            pool.tensor_copy(vst[:], sampled(qkv[:, 2 * HA:3 * HA])).then_inc(q.sem, 1)
            pool.tensor_copy(bst[:], sampled(xbc[:, AT_B:AT_B + GB])).then_inc(q.sem, 1)
            pool.tensor_copy(xst[:], sampled(xbc[:, AT_X:AT_X + 4])).then_inc(q.sem, 1)

        @block.scalar
        def _(act):
            wait = waiter(act)

            def copy(dst, src):
                act.copy(dst, src).then_inc(a.sem, 1)

            def exp(dst, src):
                act.activation(dst, src, ACT.Exp).then_inc(a.sem, 1)

            for i, row in enumerate(rows):
                ins = act.copy(rst[:, i, :], row[:, TP:T])
            ins.then_inc(a.sem, 1)
            wait(p, "rows")
            copy(cols[:], bank[0][0:L, 0:3 * P].rearrange("p (r c) -> p r c", r=3)[:, :, 0:64])
            wait(a, "cols")
            exp(ecol[:], col_g)
            exp(ercol[:], cols[:, 1, ROW_G:ROW_G + NR])
            act.wait_ge(gb_loaded, 16)
            exp(eb[:], gb[:])
            wait(v, "masked_t")
            exp(diff_t[:], diff_t[:])
            wait(v, "masked")
            exp(diff[:], diff[:])
            wait(p, "mt")
            copy(mt[:], sq_(5))
            wait(p, "m2")
            copy(m2[:], sq_(6))
            wait(p, "bt")
            copy(bt[:], bank[1][0:L, 0:GB * NB].rearrange("p (g s) -> p g s", g=GB))
            wait(p, "m4")
            copy(m4[:], sq_(6))
            wait(p, "wk")
            act.mul(wk[:], tall(7), -1.0).then_inc(a.sem, 1)
            wait(p, "w_state")
            copy(wst[:], tall(0))
            wait(p, "o_state")
            copy(ost[:], tall(4))
            wait(p, "sy_state")
            copy(yst[:], tall(1))

        @block.vector
        def _(dve):
            wait = waiter(dve)

            def tt_(dst, x, z, op):
                dve.tensor_tensor(dst, x, z, op).then_inc(v.sem, 1)

            def spread_xdd(g):
                flat = xdd[:, g * HPG:(g + 1) * HPG, :].rearrange("p h t -> p (h t)").unsqueeze(1)
                tt_(sspread[:], flat.to_broadcast([TS, NSEQ, W]), seq_of.to_broadcast([TS, NSEQ, W]), ALU.mult)

            dve.wait_ge(gb_loaded, 16)
            wait(a, "cols")
            tt_(diff_t[:], gb[0:L], bc(col_g, L), ALU.subtract)
            wait(v, "diff_t")
            tt_(diff_t[:], diff_t[:], over(neg_t, NR), ALU.add)
            tt_(diff[:], bc(col_g[:, 0:HA], L), gb[0:L, 0:HA], ALU.subtract)
            wait(v, "diff")
            tt_(diff[:], diff[:], over(neg, HA), ALU.add)
            wait(a, "ecol")
            tt_(kb[:], col_b, ecol[:, 0:HA], ALU.mult)
            wait(v, "kb")
            wait(p, "k")
            tt_(kbg[:], wide(1), bc(kb[:], DK), ALU.mult)
            wait(a, "ercol")
            tt_(kd[:], wide(1), bc(ercol[:, 0:HA], DK), ALU.mult)
            wait(p, "v")
            tt_(vb[:], wide(2), bc(col_b, DK), ALU.mult)
            wait(a, "dec_t")
            wait(p, "qk")
            tt_(qkt[:], sq_(4), diff_t[:, 0:HA], ALU.mult)
            wait(a, "eb")
            tt_(qg[:], sampled(qkv[:, 0:HA]), eb[:, 0:HA], ALU.mult)
            wait(a, "dec")
            wait(p, "kk")
            dve.scalar_tensor_tensor(M[:], sq_(3), -1.0, diff[:], ALU.mult, ALU.mult).then_inc(v.sem, 1)
            wait(v, "mk")
            tt_(M[:], M[:], bc(col_b, L), ALU.mult)
            wait(a, "mt")
            tt_(r0[:], mt[:], over(ident, HA), ALU.add)
            wait(p, "m2t")
            dve.tensor_copy(m2t[:], sq_(7)).then_inc(v.sem, 1)
            wait(v, "r0")
            wait(p, "r1")
            tt_(r1[:], sq_(5), r0[:], ALU.add)
            wait(v, "r1")
            wait(p, "r2")
            tt_(r2[:], sq_(7), r1[:], ALU.add)
            wait(p, "xt")
            tt_(xdt[:], xt_ps, bc(col_dt, PB), ALU.mult)
            wait(v, "xdt")
            tt_(xdd[:], xdt[:], bc(ercol[:, HA:NR], PB), ALU.mult)
            wait(p, "cb")
            for g in range(GB):
                hs = slice(g * HPG, (g + 1) * HPG)
                ins = dve.tensor_tensor(cbt[:, hs, :], cb_ps[:, g:g + 1, :].to_broadcast([L, HPG, L]),
                                        diff_t[:, HA + g * HPG:HA + (g + 1) * HPG, :], ALU.mult)
            ins.then_inc(v.sem, 1)
            for g in range(GB):
                hs = slice(g * HPG, (g + 1) * HPG)
                ins = dve.tensor_tensor(cs[:, hs, :], sampled(xbc[:, AT_C + g:AT_C + g + 1]).to_broadcast([P, HPG, L]),
                                        eb[:, HA + g * HPG:HA + (g + 1) * HPG, :], ALU.mult)
            ins.then_inc(v.sem, 1)
            wait(p, "u")
            dve.tensor_copy(U[:], wide(5)).then_inc(v.sem, 1)

            def decay(h):
                last = eb[:, h, :].rearrange("p (b t) -> p b t", t=LSEQ)[:, :, LSEQ - 1:LSEQ]
                tt_(S1[:, h % 2], S[:, :, h, :], last.to_broadcast([P, NSEQ, DK]), ALU.mult)

            def spread_w(h):
                tt_(spread[:, h % 2], w[:, h, :].unsqueeze(1).to_broadcast([TS, NSEQ, DK]),
                    seq_of.to_broadcast([TS, NSEQ, DK]), ALU.mult)

            dve.wait_ge(state_moved, 16)
            decay(0)
            decay(1)
            wait(v, "xdd")
            spread_xdd(0)
            wait(v, "u")
            wait(p, "w_turned")
            tt_(w[:], wide(1), U[:], ALU.add)
            wait(v, "w")
            spread_w(0)
            spread_w(1)
            wait(a, "o_state")
            wait(p, "o")
            tt_(sampled(qkv[:, 0:HA]), tall(2), ost[:], ALU.add)
            wait(p, "sy")
            dve.wait_ge(skip_loaded, 16)
            for n in range(4):
                x = sampled(xbc[:, AT_X + n:AT_X + n + 1])
                ins = dve.scalar_tensor_tensor(x, x, skip[:, n:n + 1], tall(0)[:, n:n + 1, :], ALU.mult, ALU.add)
            ins.then_inc(v.sem, 1)
            wait(a, "sy_state")
            wait(v, "sy_skip")
            x = sampled(xbc[:, AT_X:AT_X + 4])
            tt_(x, x, yst[:], ALU.add)
            for h in range(HA):
                wait(v, f"decayed{h}")
                wait(p, f"ds{h}")
                for half in range(2):
                    ins = dve.tensor_tensor(
                        S[:, 4 * half:4 * half + 4, h, :],
                        bank[(h % 2) * 2 + 4 + half][:].rearrange("p (b t) -> p b t", t=DK),
                        S1[:, h % 2, 4 * half:4 * half + 4], ALU.add)
                ins.then_inc(v.sem, 1)
                if h + 2 < HA:
                    spread_w(h + 2)
                    wait(v, f"s{h}")
                    decay(h + 2)
            dve.wait_ge(sstate_moved, 16)
            last = eb[:, HA:NR, :].rearrange("p h (b t) -> p b h t", t=LSEQ)[:, :, :, LSEQ - 1:LSEQ]
            tt_(SS[:], SS[:], last.to_broadcast([P, NSEQ, HB, PB]), ALU.mult)
            wait(v, "ss_decayed")
            for g in range(GB):
                wait(p, f"sds{g}")
                for j in range(4):
                    new = SS[:, 2 * j:2 * j + 2, g * HPG:(g + 1) * HPG, :]
                    ins = dve.tensor_tensor(new, bank[4 * g + j][:].rearrange("p (b h t) -> p b h t", b=2, t=PB), new,
                                            ALU.add)
                ins.then_inc(v.sem, 1)
                if g == 0:
                    spread_xdd(1)

        @block.tensor
        def _(pe):
            wait = waiter(pe)

            def each(dst, lhs, rhs):
                for h in range(HA):
                    mm = pe.matmul(dst[:, h, :], lhs(h), rhs(h), start=True, stop=True)
                mm.then_inc(p.sem, 1)

            def prod(dst, lhs, rhs):
                each(dst, lambda h: lhs[:, h, :], lambda h: rhs[:, h, :])

            def turn(dst, src, ident_):
                for h in range(HA):
                    mm = pe.transpose(dst[:, h, :], src[:, h, :], ident_)
                mm.then_inc(p.sem, 1)

            def with_states(dst, src):
                for h in range(HA):
                    for b in range(NSEQ):
                        cut = slice(b * LSEQ, (b + 1) * LSEQ)
                        mm = pe.matmul(dst[:, h, cut], S[:, b, h, :], src[:, h, cut], start=True, stop=True)
                mm.then_inc(p.sem, 1)

            wait(a, "rows_st")
            for i in range(3):
                mm = pe.transpose(bank[0][0:L, i * P:(i + 1) * P], rst[:, i, :], full)
            mm.then_inc(p.sem, 1)
            wait(q, "k_st")
            turn(wide(1), kst, full)
            wait(q, "v_st")
            turn(wide(2), vst, full)
            prod(sq_(3), kst, kst)
            each(sq_(4), lambda h: kst[:, h, :], lambda h: qkv[:, h, TP:T])
            wait(v, "m")
            turn(sq_(5), M, ident)
            wait(a, "mt")
            prod(sq_(6), mt, M)
            prod(sq_(7), M, mt)
            wait(q, "x_st")
            for g in range(GB):
                mm = pe.transpose(bank[1][0:L, g * NB:(g + 1) * NB], bst[:, g, :], full)
            mm.then_inc(p.sem, 1)
            for n in range(4):
                mm = pe.transpose(bank[2][0:L, n * P:(n + 1) * P], xst[:, n, :], full)
            mm.then_inc(p.sem, 1)
            for g in range(GB):
                mm = pe.matmul(cb_ps[:, g, :], bst[:, g, :], xbc[:, AT_C + g, TP:T], start=True, stop=True)
            mm.then_inc(p.sem, 1)
            wait(a, "m2")
            wait(v, "m2t")
            prod(sq_(6), m2t, m2)
            prod(sq_(5), m2, r0)
            wait(a, "m4")
            wait(v, "r1")
            prod(sq_(7), m4, r1)
            wait(v, "r2")
            prod(wide(5), r2, vb)
            prod(tall(7), kbg, r2)
            wait(a, "wk")
            pe.wait_ge(state_moved, 16)
            with_states(tall(0), wk)
            wait(a, "w_state")
            wait(v, "cs")
            turn(wide(1), wst, full)
            wait(v, "w")
            prod(tall(2), w, qkt)
            with_states(tall(4), qg)
            for h in range(HB):
                half = slice((h % 2) * PB, (h % 2 + 1) * PB)
                mm = pe.matmul(tall(0)[half, h // 2, :], xdt[:, h, :], cbt[:, h, :], start=True, stop=True)
            mm.then_inc(p.sem, 1)
            pe.wait_ge(sstate_moved, 16)
            for h in range(HB):
                half = slice((h % 2) * PB, (h % 2 + 1) * PB)
                for b in range(NSEQ):
                    cut = slice(b * LSEQ, (b + 1) * LSEQ)
                    mm = pe.matmul(tall(1)[half, h // 2, cut], SS[:, b, h, :], cs[:, h, cut], start=True, stop=True)
            mm.then_inc(p.sem, 1)
            wait(a, "o_state")
            for h in range(HA):
                wait(v, f"spread{h}")
                if h >= 2:
                    wait(v, f"s{h - 2}")
                for half in range(2):
                    mm = pe.matmul(bank[(h % 2) * 2 + 4 + half][:], kd[:, h, :],
                                   spread[:, h % 2, 4 * half:4 * half + 4, :].rearrange("p b t -> p (b t)"),
                                   start=True, stop=True)
                mm.then_inc(p.sem, 1)
            for g in range(GB):
                if g:
                    wait(v, "sspread1")
                for j in range(4):
                    mm = pe.matmul(bank[4 * g + j][:], bt[:, g, :],
                                   sspread[:, 2 * j:2 * j + 2, :], start=True, stop=True)
                mm.then_inc(p.sem, 1)


AT_Z = 4


def gate_phase(nc, io, qkv, xbc, norm_dram, z_dram, mixed_dram):
    with ExitStack() as stack:
        m = Memory(nc, stack)
        ow, yw = m.sb("m_ow", [P, 1]), m.sb("m_yw", [P, 4])
        sq = m.sb("m_sq", [P, 2, T])
        group = list(range(HA)) + [HA, HA, HA + 1, HA + 1]
        norm = RowNorm(m, "mn", HA + GB, group, [1.0 / P] * HA + [0.5 / P] * GB, norm_dram)
        z_loaded, loaded, rooted, sent = m.sem("m_z"), m.sem("m_loaded"), m.sem("m_rooted"), m.sem("m_sent")
        squared, scaled, gated = m.sem("m_squared"), m.sem("m_scaled"), m.sem("m_gated")
        pe_done = m.sem("m_pe")
        block = stack.enter_context(nc.Block())
        NB8 = HA + 4
        blocks = [qkv[:, c, :] for c in range(HA)] + [xbc[:, AT_X + j, :] for j in range(4)]

        def members(g):
            return [j for j, of in enumerate(group) if of == g]

        @block.sync
        def _(sp):
            for j in range(4):
                sp.dma_start(xbc[:, AT_Z + j, :], z_dram[4 + j]).then_inc(z_loaded, 16)
            sp.wait_ge(z_loaded, 64)
            sp.dma_start(ow[:], io["onorm_a"]).then_inc(loaded, 16)
            sp.dma_start(yw[:], io["onorm_b"]).then_inc(loaded, 16)
            sp.dma_start(qkv[:, AT_Z:AT_Z + 4, :], z_dram[0:4].rearrange("a p t -> p a t")).then_inc(loaded, 16)
            sp.wait_ge(loaded, 48)
            norm.spread(sp, (rooted, 2), scaled)
            for g in range(HA + GB):
                sp.wait_ge(scaled, g + 1)
                for j in members(g):
                    sp.dma_start(mixed_dram[j], blocks[j]).then_inc(sent, 16)
            sp.wait_ge(sent, 16 * NB8)

        @block.scalar
        def _(act):
            for j, b in enumerate(blocks):
                if j >= 2:
                    act.wait_ge(pe_done, j - 1)
                if j >= HA:
                    act.wait_ge(gated, j - HA + 1)
                act.activation(sq[:, j % 2, :], b, ACT.Square).then_inc(squared, 1)
            act.wait_ge(norm.set, 2 + HA + GB)
            act.wait_ge(pe_done, NB8)
            norm.root(act).then_inc(rooted, 1)

        @block.tensor
        def _(pe):
            pe.wait_ge(norm.set, 1 + HA + GB)
            for j in range(NB8):
                pe.wait_ge(squared, j + 1)
                norm.sum(pe, j, sq[:, j % 2, :]).then_inc(pe_done, 1)

        @block.vector
        def _(dve):
            norm.constants(dve)
            dve.memset(norm.eps[:], EPS).then_inc(norm.set, 1)
            dve.wait_ge(z_loaded, 64)
            for j in range(4):
                y = blocks[HA + j]
                dve.tensor_tensor(y, y, xbc[:, AT_Z + j, :], ALU.mult).then_inc(gated, 1)
            dve.wait_ge(rooted, 1)
            dve.reciprocal(norm.rows[:], norm.rows[:]).then_inc(rooted, 1)
            dve.wait_ge(loaded, 48)
            for c in range(HA):
                o = blocks[c]
                dve.scalar_tensor_tensor(o, qkv[:, AT_Z + c, :], ow[:, 0:1], o, ALU.mult, ALU.mult).then_inc(gated, 1)
            for g in range(HA + GB):
                r = norm.row(dve, g)
                if g < HA:
                    dve.wait_ge(gated, 4 + g + 1)
                for j in members(g):
                    x = blocks[j]
                    if g < HA:
                        ins = dve.tensor_tensor(x, x, r, ALU.mult)
                    else:
                        ins = dve.scalar_tensor_tensor(x, x, yw[:, j - HA:j - HA + 1], r,
                                                       ALU.mult, ALU.mult)
                ins.then_inc(scaled, 1)


def out_projection_phase(nc, io, mixed_dram, yc_dram, x2):
    RING = 3
    with ExitStack() as stack:
        m = Memory(nc, stack)
        w = m.sb("o_w", [P, 2, NMIX, P])
        w_r = [m.sb(f"o_w{x}", [P, 2, NMIX, P], F32R) for x in ("hi", "lo")]
        mix = m.sb("o_mix", [P, RING, T])
        mixed = [m.sb(f"o_mix{x}", [P, NMIX, T], F32R) for x in ("hi", "lo")]
        ps = m.ps("o_ps", [P, 2, NT, 512])
        x_loaded, mix_hi, mix_lo = m.sem("o_x"), m.sem("o_mixhi"), m.sem("o_mixlo")

        w_loaded = [m.sem(f"o_w{h}") for h in range(2)]
        mix_loaded = [m.sem(f"o_mixl{r}") for r in range(RING)]
        w_hi, w_lo, done, added = m.sem("o_whi"), m.sem("o_wlo"), m.sem("o_pe"), m.sem("o_dve")
        block = stack.enter_context(nc.Block())
        PAIRS = KD // 2

        @block.sync
        def _(sp):
            sp.dma_start(w[:, 0], io["w_out"][0]).then_inc(w_loaded[0], 16)
            for k in range(NMIX):
                if k == RING:
                    sp.dma_start(w[:, 1], io["w_out"][1]).then_inc(w_loaded[1], 16)
                if k >= RING:
                    sp.wait_ge(mix_lo, k - RING + 1)
                src = mixed_dram[k] if k < NMIX - NC else yc_dram[k - (NMIX - NC)]
                sp.dma_start(mix[:, k % RING, :], src).then_inc(mix_loaded[k % RING], 16)
            sp.dma_start(x2[:], io["xT"]).then_inc(x_loaded, 16)
            for i in range(1, PAIRS):
                for h in range(2):
                    sp.wait_ge(w_lo, 2 * i + h - 1)
                    sp.dma_start(w[:, h], io["w_out"][2 * i + h]).then_inc(w_loaded[h], 16)

        @block.tensor
        def _(pe):
            for i in range(PAIRS):
                for h in range(2):
                    pe.wait_ge(w_lo, 2 * i + h + 1)
                    if i:
                        pe.wait_ge(added, 2 * i + h - 1)
                    if i == 0 and h == 0:
                        for k in range(NMIX):
                            pe.wait_ge(mix_lo, k + 1)
                            for n in range(NT):
                                for x, z in PARTS:
                                    mm = pe.matmul(ps[:, h, n, 0:TW], w_r[x][:, h, k, :],
                                                   mixed[z][:, k, n * TW:(n + 1) * TW], start=(k == 0 and (x, z) == PARTS[0]),
                                                   stop=(k == NMIX - 1 and (x, z) == PARTS[-1]))
                    else:
                        for n in range(NT):
                            mm = exact_product(pe, ps[:, h, n, 0:TW], lambda x, k: w_r[x][:, h, k, :],
                                               lambda z, k: mixed[z][:, k, n * TW:(n + 1) * TW], NMIX)
                    mm.then_inc(done, 1)

        def split_w_hi(act, i, h):
            act.wait_ge(w_loaded[h], 16 * i + 16)
            if i:
                act.wait_ge(done, 2 * i + h - 1)
            copy_hi(act, w_r[0][:, h], w[:, h]).then_inc(w_hi, 1)

        def split_w_lo(dve, i, h):
            dve.wait_ge(w_hi, 2 * i + h + 1)
            take_lo(dve, w_r[1][:, h], w[:, h], w_r[0][:, h]).then_inc(w_lo, 1)

        @block.scalar
        def _(act):
            split_w_hi(act, 0, 0)
            for k in range(NMIX):
                act.wait_ge(mix_loaded[k % RING], 16 * (k // RING + 1))
                copy_hi(act, mixed[0][:, k, :], mix[:, k % RING, :]).then_inc(mix_hi, 1)
            split_w_hi(act, 0, 1)
            for i in range(1, PAIRS):
                for h in range(2):
                    split_w_hi(act, i, h)

        @block.vector
        def _(dve):
            split_w_lo(dve, 0, 0)
            for k in range(NMIX):
                dve.wait_ge(mix_hi, k + 1)
                take_lo(dve, mixed[1][:, k, :], mix[:, k % RING, :], mixed[0][:, k, :]).then_inc(mix_lo, 1)
            split_w_lo(dve, 0, 1)
            dve.wait_ge(x_loaded, 16)
            for i in range(PAIRS):
                for h in range(2):
                    if i + 1 < PAIRS:
                        split_w_lo(dve, i + 1, h)
                    dve.wait_ge(done, 2 * i + h + 1)
                    x = x2[:, i * 2 + h, :].rearrange("p (n t) -> p n t", n=NT)
                    dve.tensor_tensor(x, x, ps[:, h, :, 0:TW], ALU.add).then_inc(added, 1)


RT, RL = 12, T // 12
BLK = 256
NBLK = (TOPK * T - NE) // BLK + NE
SLOTS = NBLK * BLK


def routing_phase(nc, io, x2t, x2, wts, idx, expert_of, masks, ones, slots_dram, x2_dram):
    with ExitStack() as stack:
        m = Memory(nc, stack)
        NL = NG + NE
        w2c, w2r = m.sb("r_w2c", [P, KD]), m.sb("r_w2r", [P, D])
        wr, consts = m.sb("r_w", [P, KD, NL]), m.sb("r_consts", [NE, io["route_consts"].shape[1]])
        xw = m.sb("r_xw", [P, 2, T])
        lt = m.sb("r_lt", [NL, T])
        lg = m.sb("r_lg", [RL, RT, NL])
        h2 = m.sb("r_h2", [RL, 4, D])
        junk = m.sb("r_junk", [RL, D])
        rs = m.sb("r_rs", [RL, RT, 1])

        def sb(name, *shape):
            return m.sb("r_" + name, [RL, RT, *shape])

        mx, e, s, pt, eq, hot, left = (sb("mx", 1), sb("e", NG), sb("s", 1), sb("pt", 1), sb("eq", NG),
                                       sb("hot", NG), sb("left", 1))
        prod, ls = sb("prod", NG, EPG), sb("ls", EPG)
        hots = [sb("hot1", EPG), sb("hot2", EPG)]
        vals = [sb("v1", 1), sb("v2", 1)]
        both = [sb("both1", NG, EPG), sb("both2", NG, EPG)]
        sel, slot_t, slot_f = sb("sel", NE), sb("slott", NE), sb("slotf", TOPK)
        sel_rows, pos = m.sb("r_selrows", [NE, T]), m.sb("r_pos", [NE, T])
        one_rows = m.sb("r_onerows", [NE, T])
        gt, n_blocks, base = m.sb("r_gt", [NE, 8]), m.sb("r_nblocks", [NE, 1]), m.sb("r_base", [NE, 1])
        ended, owner = m.sb("r_ended", [NE, NBLK + 1]), m.sb("r_owner", [1, NBLK + 1])
        ps = m.ps("r_ps", [P, NT, 512])
        ps2, ps3 = m.ps("r_ps2", [P, 512]), m.ps("r_ps3", [P, NT, 512])
        loaded, xw_s, summed, pe_s, dve_s = m.sem("r_l"), m.sem("r_xw"), m.sem("r_summed"), m.sem("r_pe"), m.sem("r_dve")
        ready, back, squares = m.sem("r_ready"), m.sem("r_back"), m.sem("r_squares")
        x2_sent, turned, copied = m.sem("r_x2sent"), m.sem("r_turned"), m.sem("r_copied")
        first_loaded = m.sem("r_fl")
        h2_ready, sent = m.sem("r_h2s"), [m.sem(f"r_sent{i}") for i in range(4)]
        block = stack.enter_context(nc.Block())
        thresholds, block_ids, upto = consts[:, 0:8], consts[:, 8:9 + NBLK], consts[:, 9 + NBLK:9 + NBLK + NE]
        per = RT // NT

        @block.sync
        def _(sp):
            sp.dma_start(w2c[:], io["norm2_w"]).then_inc(first_loaded, 16)
            sp.dma_start(wr[:], io["w_router"]).then_inc(first_loaded, 16)
            sp.dma_start(w2r[:], io["norm2_row"].partition_broadcast(P)).then_inc(loaded, 16)
            sp.dma_start(consts[:], io["route_consts"]).then_inc(loaded, 16)
            sp.wait_ge(copied, 2 * RT)
            sp.dma_start(x2_dram.rearrange("(t p) d -> p t d", p=RL), x2[:]).then_inc(x2_sent, 16)
            sp.wait_ge(x2_sent, 16)

        @block.tensor
        def _(pe):
            for r in range(2 * RT):
                if r >= NT:
                    pe.wait_ge(copied, r - NT + 1)
                for k in range(4):
                    mm = pe.transpose(ps3[0:RL, r % NT, k * P:(k + 1) * P],
                                      x2t[:, (r % 2) * 4 + k, (r // 2) * RL:(r // 2 + 1) * RL], masks[:, 0, :])
                mm.then_inc(turned, 1)
                if r % 3 < 2:
                    continue
                k = r // 3
                pe.wait_ge(xw_s, k + 1)
                for n in range(NT):
                    mm = pe.matmul(ps[0:NL, n, 0:TW], wr[:, k, :], xw[:, k % 2, n * TW:(n + 1) * TW],
                                   start=(k == 0), stop=(k == KD - 1))
                mm.then_inc(summed, 1)
            pe.wait_ge(back, 1)
            for t in range(RT):
                mm = pe.transpose(ps2[0:RL, t * NL:(t + 1) * NL], lt[:, t * RL:(t + 1) * RL], masks[0:NL, 0, 0:NL])
            mm.then_inc(pe_s, 1)
            pe.wait_ge(ready, 3)
            for t in range(RT):
                mm = pe.transpose(ps3[0:NE, t // per, (t % per) * RL:(t % per + 1) * RL],
                                  sel[:, t, :], masks[0:RL, 0, 0:RL])
            mm.then_inc(pe_s, 1)
            pe.wait_ge(loaded, 32)
            pe.wait_ge(ready, 4)
            pe.matmul(ps[0:NE, 0, 0:1], upto, n_blocks[:], start=True, stop=True).then_inc(pe_s, 1)
            pe.wait_ge(ready, 5)
            pe.matmul(ps[0:1, 1, 0:NBLK + 1], ones[0:NE, 0:1], ended[:], start=True, stop=True).then_inc(pe_s, 1)
            pe.wait_ge(ready, 6)
            for t in range(RT):
                mm = pe.transpose(ps2[0:RL, t * NE:(t + 1) * NE], pos[:, t * RL:(t + 1) * RL], masks[0:NE, 0, 0:NE])
            mm.then_inc(pe_s, 1)

        @block.scalar
        def _(act):
            for t in range(RT):
                for half in range(2):
                    act.wait_ge(turned, 2 * t + half + 1)
                    act.copy(x2[:, t, half * 512:(half + 1) * 512], ps3[0:RL, (2 * t + half) % NT, :]).then_inc(copied, 1)
                act.wait_ge(copied, 2 * t + 2)
                if t:
                    act.wait_ge(squares, t)
                act.activation(junk[:], x2[:, t, :], ACT.Square, accum_out=rs[:, t, :]).then_inc(squares, 1)
            act.wait_ge(squares, RT + 1)
            act.activation(rs[:], rs[:], ACT.Sqrt).then_inc(squares, 1)
            act.wait_ge(summed, KD)
            act.copy(lt[:].rearrange("p (n t) -> p n t", n=NT), ps[0:NL, :, 0:TW]).then_inc(back, 1)
            act.wait_ge(ready, 1)
            act.activation(e[:], e[:], ACT.Exp).then_inc(back, 1)
            act.wait_ge(ready, 2)
            act.activation(ls[:], ls[:], ACT.Exp).then_inc(back, 1)
            act.wait_ge(pe_s, 2)
            act.copy(sel_rows[:].rearrange("p (n t) -> p n t", n=NT), ps3[0:NE, :, 0:TW]).then_inc(back, 1)

        @block.gpsimd
        def _(pool):
            pool.wait_ge(ready, 7)
            for t in range(RT):
                pool.wait_ge(h2_ready, t + 1)
                for k in range(TOPK):
                    pool.indirect_dma_start(slots_dram, bass.IndirectOffsetOnAxis(ap=idx[:, t, k:k + 1], axis=0),
                                            h2[:, t % 4, :], None).then_inc(sent[t % 4], 16)
            for q in sent:
                pool.wait_ge(q, 16 * TOPK * RT // 4)

        @block.vector
        def _(dve):
            count = [0]

            def link(ins):
                count[0] += 1
                ins.then_inc(dve_s, 1)
                dve.wait_ge(dve_s, count[0])

            def wide(ap, n):
                return ap.to_broadcast([RL, RT, n])

            def first_max(hot_, val, n):
                link(dve.tensor_reduce(mx[:], val[:], AX.X, ALU.max))
                dve.memset(left[:], 1.0)
                link(dve.tensor_tensor(eq[:], val[:], wide(mx[:], n), ALU.is_ge))
                for i in range(n):
                    link(dve.tensor_tensor(hot_[:, :, i:i + 1], eq[:, :, i:i + 1], left[:], ALU.mult))
                    link(dve.tensor_tensor(left[:], left[:], hot_[:, :, i:i + 1], ALU.subtract))

            dve.wait_ge(first_loaded, 32)
            for k in range(KD):
                if k >= 2:
                    dve.wait_ge(summed, k - 1)
                dve.tensor_scalar(xw[:, k % 2, :], x2t[:, k, :], w2c[:, k:k + 1], None, ALU.mult).then_inc(xw_s, 1)
            dve.wait_ge(squares, RT)
            dve.tensor_scalar(rs[:], rs[:], 1.0 / D, EPS, ALU.mult, ALU.add).then_inc(squares, 1)
            dve.wait_ge(loaded, 32)
            dve.memset(one_rows[:], 1.0)
            dve.wait_ge(squares, RT + 2)
            link(dve.reciprocal(rs[:], rs[:]))
            dve.wait_ge(pe_s, 1)
            link(dve.tensor_tensor(lg[:], ps2[0:RL, 0:RT * NL].rearrange("p (t l) -> p t l", l=NL),
                                   wide(rs[:], NL), ALU.mult))
            link(dve.tensor_reduce(mx[:], lg[:, :, 0:NG], AX.X, ALU.max))
            dve.tensor_tensor(e[:], lg[:, :, 0:NG], wide(mx[:], NG), ALU.subtract).then_inc(ready, 1)
            dve.wait_ge(back, 2)
            link(dve.tensor_reduce(s[:], e[:], AX.X, ALU.add))
            first_max(hot, e, NG)
            link(dve.reciprocal(pt[:], s[:]))
            link(dve.tensor_tensor(pt[:], pt[:], mx[:], ALU.mult))
            link(dve.tensor_tensor(prod[:], lg[:, :, NG:].rearrange("p t (g e) -> p t g e", g=NG),
                                   hot[:].unsqueeze(3).to_broadcast([RL, RT, NG, EPG]), ALU.mult))
            link(dve.tensor_reduce(ls[:].unsqueeze(3), prod[:].rearrange("p t g e -> p t e g"), AX.X, ALU.add))
            link(dve.tensor_reduce(mx[:], ls[:], AX.X, ALU.max))
            dve.tensor_tensor(ls[:], ls[:], wide(mx[:], EPG), ALU.subtract).then_inc(ready, 1)
            dve.wait_ge(back, 3)
            link(dve.tensor_reduce(s[:], ls[:], AX.X, ALU.add))
            link(dve.reciprocal(s[:], s[:]))
            link(dve.tensor_tensor(ls[:], ls[:], wide(s[:], EPG), ALU.mult))
            for k in range(TOPK):
                first_max(hots[k], ls, EPG)
                dve.tensor_copy(vals[k][:], mx[:])
                link(dve.tensor_tensor(both[k][:], hot[:].unsqueeze(3).to_broadcast([RL, RT, NG, EPG]),
                                       hots[k][:].unsqueeze(2).to_broadcast([RL, RT, NG, EPG]), ALU.mult))
                if k == 0:
                    link(dve.scalar_tensor_tensor(ls[:], hots[0][:], -4.0, ls[:], ALU.mult, ALU.add))
            flat = [b[:].rearrange("p t g e -> p t (g e)") for b in both]
            dve.tensor_tensor(sel[:], flat[0], flat[1], ALU.add).then_inc(ready, 1)
            link(dve.tensor_tensor(s[:], vals[0][:], vals[1][:], ALU.add))
            link(dve.reciprocal(s[:], s[:]))
            link(dve.tensor_tensor(s[:], s[:], pt[:], ALU.mult))
            for k in range(TOPK):
                link(dve.tensor_tensor(wts[:, :, k:k + 1], vals[k][:], s[:], ALU.mult))
            dve.wait_ge(back, 4)
            link(dve.tensor_tensor_scan(pos[:], one_rows[:], sel_rows[:], 0.0, ALU.mult, ALU.add))
            link(dve.tensor_tensor(gt[:], pos[:, T - 1:T].to_broadcast([NE, 8]), thresholds, ALU.is_gt))
            dve.tensor_reduce(n_blocks[:], gt[:], AX.X, ALU.add).then_inc(ready, 1)
            dve.wait_ge(pe_s, 3)
            link(dve.tensor_copy(base[:], ps[0:NE, 0, 0:1]))
            dve.tensor_tensor(ended[:], block_ids, base[:].to_broadcast([NE, NBLK + 1]), ALU.is_ge).then_inc(ready, 1)
            dve.wait_ge(ready, 5)
            link(dve.tensor_tensor(base[:], base[:], n_blocks[:], ALU.subtract))
            link(dve.tensor_scalar(base[:], base[:], float(BLK), -1.0, ALU.mult, ALU.add))
            dve.tensor_scalar(pos[:], pos[:], base[:], None, ALU.add).then_inc(ready, 1)
            dve.wait_ge(pe_s, 4)
            link(dve.tensor_scalar(owner[:], ps[0:1, 1, 0:NBLK + 1], float(NE - 1), None, ALU.min))
            link(dve.tensor_copy(expert_of[:], owner[:]))
            dve.wait_ge(pe_s, 5)
            link(dve.tensor_copy(slot_t[:], ps2[0:RL, 0:RT * NE].rearrange("p (t l) -> p t l", l=NE)))
            for k in range(TOPK):
                link(dve.tensor_tensor(sel[:], slot_t[:], flat[k], ALU.mult))
                link(dve.tensor_reduce(slot_f[:, :, k:k + 1], sel[:], AX.X, ALU.add))
            dve.tensor_copy(idx[:], slot_f[:]).then_inc(ready, 1)
            for t in range(RT):
                if t >= 4:
                    dve.wait_ge(sent[t % 4], 16 * TOPK * (t // 4))
                dve.scalar_tensor_tensor(h2[:, t % 4, :], x2[:, t, :], rs[:, t, :], w2r[0:RL, :], ALU.mult,
                                         ALU.mult).then_inc(h2_ready, 1)


def expert_phase(nc, io, expert_of, masks, slots_dram, y_dram):
    with ExitStack() as stack:
        m = Memory(nc, stack)
        win, wdn = m.sb("e_win", [P, KD, 512]), m.sb("e_wdn", [P, 2, D])
        win_r = [m.sb(f"e_win{x}", [P, 2, KD, 512], F32R) for x in ("hi", "lo")]
        wdn_r = [m.sb(f"e_wdn{x}", [P, 2, 2, D], F32R) for x in ("hi", "lo")]
        xs = m.sb("e_xs", [P, 2, D])
        ht = [m.sb(f"e_ht{x}", [P, 2, KD, BLK], F32R) for x in ("hi", "lo")]
        s, gated = m.sb("e_s", [P, 2, FF]), m.sb("e_gated", [P, 2, FF])
        at = [m.sb(f"e_at{x}", [P, 2, 2, P], F32R) for x in ("hi", "lo")]
        ys = m.sb("e_ys", [P, 2, 2, D])
        ps_t, ps_g, ps_a, ps_d = (m.ps("e_pst", [P, 2, 512]), m.ps("e_psg", [P, 2, 512]), m.ps("e_psa", [P, 2, 512]),
                                  m.ps("e_psd", [P, 2, 512]))
        turned = ps_a[:, :, 0:FF].rearrange("p t (f s) -> p t f s", f=2)
        pp = Steps(m, "e_ppe", ["t0", "t1", "t2", "t3"])
        pa = Steps(m, "e_pact", ["in0", "in1", "dn", "t0", "t1", "t2", "t3"])
        pv = Steps(m, "e_pdve", ["in0", "in1", "dn", "t0", "t1", "t2", "t3"])
        p = Steps(m, "e_pe", ["g0", "g1", "a0", "a1", "d0", "d1", "d2", "d3"], ahead=2)
        a = Steps(m, "e_act", ["s0", "s1", "a0", "a1", "y0", "y2"])
        v = Steps(m, "e_dve", ["h0", "h1", "a0", "a1", "y1", "y3"])
        in_loaded, dn_loaded, x_loaded = m.sem("e_inl"), m.sem("e_dnl"), m.sem("e_xl")
        y_sent, y_free = [m.sem(f"e_ysent{h}") for h in range(2)], [m.sem(f"e_yfree{h}") for h in range(2)]
        rows_of = slots_dram.rearrange("(n t p) d -> n p t d", t=2, p=P)
        y_of = y_dram.rearrange("(n t p) d -> n p t d", t=2, p=P)
        block = stack.enter_context(nc.Block())

        this_round = [None]

        def rounds_before():
            return this_round[0]

        def waiter(eng):
            return lambda steps, r, name, back=0: eng.wait_ge(steps.sem, steps.at(r, name, back))

        def loop(eng, main, prepare):
            prepare(0, 0, [0, 1, 2])
            with eng.Fori(0, NBLK // 2) as i:
                for h in range(2):
                    this_round[0] = i + 1
                    main(i * 2 + h, h, lambda part, i=i, h=h: prepare(i * 2 + (h + 1), 1 - h, [part]))

        @block.sync
        def _(sp):
            wait = waiter(sp)
            with sp.Fori(0, NBLK + 1) as r:
                e = sp.value_load(expert_of[0:1, bass.ds(r, 1)], min_val=0, max_val=NE - 1)
                wait(pv, r, "in1", 1)
                sp.dma_start(win[:], io["w_gate_up"][bass.ds(e, 1)].rearrange("a p k f -> (a p) k f")
                             ).then_inc(in_loaded, 16)
                wait(pv, r, "dn", 1)
                sp.dma_start(wdn[:], io["w_down"][bass.ds(e, 1)].rearrange("a p k d -> (a p) k d")
                             ).then_inc(dn_loaded, 16)
                wait(pp, r, "t3", 1)
                sp.dma_start(xs[:], rows_of[bass.ds(r, 1)].rearrange("a p t d -> (a p) t d")).then_inc(x_loaded, 16)

        @block.gpsimd
        def _(pool):
            wait = waiter(pool)
            for h in range(2):
                pool.sem_inc(y_free[h], 1)
            with pool.Fori(0, NBLK // 2) as i:
                for h in range(2):
                    wait(a, i * 2 + h, "y2")
                    wait(v, i * 2 + h, "y3")
                    pool.dma_start(y_of[bass.ds(i * 2 + h, 1)].rearrange("a p t d -> (a p) t d"), ys[:, h]
                                   ).then_inc(y_sent[h], 16)
                    pool.wait_ge(y_sent[h], i * 16 + 16)
                    pool.sem_inc(y_free[h], 1)

        @block.tensor
        def _(pe):
            wait = waiter(pe)
            pp.start(pe)
            p.start(pe)

            def prepare(r, q, parts):
                for part in parts:
                    if part == 0:
                        pe.wait_ge(x_loaded, r * 16 + 16)
                    for g in range(4):
                        if g // 2 != part:
                            continue
                        bank = g % 2
                        wait(pa, r, f"t{g - 2}" if g >= 2 else f"t{g + 2}", 0 if g >= 2 else 1)
                        wait(pv, r, f"t{g - 2}" if g >= 2 else f"t{g + 2}", 0 if g >= 2 else 1)
                        for k in range(4):
                            at_ = ((g % 2) * 4 + k) * P
                            mm = pe.transpose(ps_t[:, bank, k * P:(k + 1) * P], xs[:, g // 2, at_:at_ + P],
                                              masks[:, 0, :])
                        mm.then_inc(pp.sem, 1)

            def passes(dst, lhs, rhs, ks):
                for n, (x, z) in enumerate(PARTS):
                    for k in range(ks):
                        mm = pe.matmul(dst, lhs(x, k), rhs(z, k), start=(n == 0 and k == 0),
                                       stop=(n == 2 and k == ks - 1))
                mm.then_inc(p.sem, 1)

            def main(j, q, prepare_next):
                wait(pv, j, "in1")
                wait(pv, j, "t3")
                wait(pa, j, "t3")
                for t in range(2):
                    wait(v, j, f"h{t}", 1)
                    passes(ps_g[:, t, :], lambda x, k: ht[x][:, q, k, t * P:(t + 1) * P],
                           lambda z, k: win_r[z][:, q, k, :], KD)
                prepare_next(0)
                for t in range(2):
                    wait(v, j, f"h{t}")
                    wait(a, j, f"a{t}", 1)
                    wait(v, j, f"a{t}", 1)
                    for f in range(2):
                        mm = pe.transpose(turned[:, t, f, :], gated[:, t, f * P:(f + 1) * P], masks[:, 0, :])
                    mm.then_inc(p.sem, 1)
                prepare_next(1)
                wait(pv, j, "dn")
                for d in range(4):
                    t = d // 2
                    wait(v, j, f"a{t}")
                    wait((a, v)[d % 2], j, f"y{(d + 2) % 4}", 0 if d >= 2 else 1)
                    passes(ps_d[:, d % 2, :], lambda x, k: at[x][:, t, k, :],
                           lambda z, k: wdn_r[z][:, q, k, (d % 2) * 512:(d % 2 + 1) * 512], 2)

            loop(pe, main, prepare)

        def group_dst(part, q, g):
            k0 = (g % 2) * 4
            return ht[part][:, q, k0:k0 + 4, (g // 2) * P:(g // 2 + 1) * P]

        def group_src(g):
            return ps_t[:, g % 2, :].rearrange("p (k s) -> p k s", k=4)

        @block.scalar
        def _(act):
            wait = waiter(act)
            pa.start(act)
            a.start(act)

            def prepare(r, q, parts):
                if 0 in parts:
                    act.wait_ge(in_loaded, r * 16 + 16)
                    wait(p, r, "g1", 2)
                    for h in range(2):
                        act.copy(win_r[0][:, q, h * 4:h * 4 + 4, :], win[:, h * 4:h * 4 + 4, :]).then_inc(pa.sem, 1)
                    act.wait_ge(dn_loaded, r * 16 + 16)
                    wait(p, r, "d3", 2)
                    act.copy(wdn_r[0][:, q], wdn[:]).then_inc(pa.sem, 1)
                for part in (1, 2):
                    if part in parts:
                        for g in (2 * part - 2, 2 * part - 1):
                            wait(pp, r, f"t{g}")
                            act.copy(group_dst(0, q, g), group_src(g)).then_inc(pa.sem, 1)

            def main(j, q, prepare_next):
                prepare_next(0)
                for t in range(2):
                    wait(p, j, f"g{t}")
                    act.activation(s[:, t, :], ps_g[:, t, 0:FF], ACT.Silu).then_inc(a.sem, 1)
                prepare_next(1)
                for t in range(2):
                    wait(p, j, f"a{t}")
                    act.copy(at[0][:, t], turned[:, t]).then_inc(a.sem, 1)
                prepare_next(2)
                act.wait_ge(y_free[q], rounds_before())
                for d in (0, 2):
                    wait(p, j, f"d{d}")
                    act.copy(ys[:, q, d // 2, 0:512], ps_d[:, d % 2, :]).then_inc(a.sem, 1)

            loop(act, main, prepare)

        @block.vector
        def _(dve):
            wait = waiter(dve)
            pv.start(dve)
            v.start(dve)

            def prepare(r, q, parts):
                if 0 in parts:
                    for h in range(2):
                        wait(pa, r, f"in{h}")
                        ks = slice(h * 4, h * 4 + 4)
                        dve.tensor_tensor(win_r[1][:, q, ks, :], win[:, ks, :], win_r[0][:, q, ks, :].bitcast(F32),
                                          ALU.subtract).then_inc(pv.sem, 1)
                    wait(pa, r, "dn")
                    dve.tensor_tensor(wdn_r[1][:, q], wdn[:], wdn_r[0][:, q].bitcast(F32),
                                      ALU.subtract).then_inc(pv.sem, 1)
                for part in (1, 2):
                    if part in parts:
                        for g in (2 * part - 2, 2 * part - 1):
                            wait(pa, r, f"t{g}")
                            dve.tensor_tensor(group_dst(1, q, g), group_src(g), group_dst(0, q, g).bitcast(F32),
                                              ALU.subtract).then_inc(pv.sem, 1)

            def main(j, q, prepare_next):
                prepare_next(0)
                for t in range(2):
                    wait(a, j, f"s{t}")
                    dve.tensor_tensor(gated[:, t, :], s[:, t, :], ps_g[:, t, FF:], ALU.mult).then_inc(v.sem, 1)
                prepare_next(1)
                for t in range(2):
                    wait(a, j, f"a{t}")
                    dve.tensor_tensor(at[1][:, t], turned[:, t], at[0][:, t].bitcast(F32), ALU.subtract).then_inc(v.sem, 1)
                prepare_next(2)
                dve.wait_ge(y_free[q], rounds_before())
                for d in (1, 3):
                    wait(p, j, f"d{d}")
                    dve.tensor_copy(ys[:, q, d // 2, 512:], ps_d[:, d % 2, :]).then_inc(v.sem, 1)

            loop(dve, main, prepare)


def combine_phase(nc, io, wts, idx, x2_dram, y_dram):
    BUFS = 3
    with ExitStack() as stack:
        m = Memory(nc, stack)
        wf = m.sb("f_w", [P, D])
        x, r1, r2 = m.sb("f_x", [RL, BUFS, D]), m.sb("f_r1", [RL, BUFS, D]), m.sb("f_r2", [RL, BUFS, D])
        junk, q = m.sb("f_junk", [RL, D]), m.sb("f_q", [RL, RT, 1])
        w_loaded = m.sem("f_wl")
        loaded, gathered = [m.sem(f"f_l{i}") for i in range(BUFS)], [m.sem(f"f_g{i}") for i in range(BUFS)]
        sent = [m.sem(f"f_sent{i}") for i in range(BUFS)]
        one_s, two_s, inverse_s, out_s = m.sem("f_one"), m.sem("f_two"), m.sem("f_inverse"), m.sem("f_out")
        square_s, root_s = m.sem("f_square"), m.sem("f_root")
        eps = m.sb("f_eps_col", [RL, 1])
        block = stack.enter_context(nc.Block())

        @block.sync
        def _(sp):
            sp.dma_start(wf[:], io["final_row"].partition_broadcast(P)).then_inc(w_loaded, 16)
            for t in range(RT + 2):
                if t < RT:
                    if t >= BUFS:
                        sp.wait_ge(sent[t % BUFS], 16 * (t // BUFS))
                    sp.dma_start(x[:, t % BUFS, :], x2_dram[t * RL:(t + 1) * RL, :]).then_inc(loaded[t % BUFS], 16)
                if t >= 2:
                    o = t - 2
                    sp.wait_ge(out_s, o + 1)
                    sp.dma_start(io["y"][o * RL:(o + 1) * RL, :], x[:, o % BUFS, :]).then_inc(sent[o % BUFS], 16)
            for b in range(BUFS):
                sp.wait_ge(sent[b], 16 * (RT // BUFS))

        @block.gpsimd
        def _(pool):
            for t in range(RT):
                if t >= BUFS:
                    pool.wait_ge(two_s, t - BUFS + 1)
                for k, r in enumerate((r1, r2)):
                    pool.indirect_dma_start(r[:, t % BUFS, :], None, y_dram,
                                            bass.IndirectOffsetOnAxis(ap=idx[:, t, k:k + 1], axis=0)
                                            ).then_inc(gathered[t % BUFS], 16)

        @block.scalar
        def _(act):
            for t in range(RT):
                act.wait_ge(two_s, t + 1)
                if t:
                    act.wait_ge(square_s, t)
                act.activation(junk[:], x[:, t % BUFS, :], ACT.Square, accum_out=q[:, t, :]).then_inc(square_s, 1)
                act.wait_ge(square_s, t + 1)
                act.activation(q[:, t, :], q[:, t, :], ACT.Sqrt, scale=1.0 / D, bias=eps[:]).then_inc(root_s, 1)

        @block.vector
        def _(dve):
            dve.memset(eps[:], EPS)
            dve.wait_ge(w_loaded, 16)
            for t in range(RT + 1):
                if t < RT:
                    b = t % BUFS
                    xt = x[:, b, :]
                    dve.wait_ge(loaded[b], 16 * (t // BUFS + 1))
                    dve.wait_ge(gathered[b], 32 * (t // BUFS + 1))
                    dve.scalar_tensor_tensor(xt, r1[:, b, :], wts[:, t, 0:1], xt, ALU.mult, ALU.add).then_inc(one_s, 1)
                    dve.wait_ge(one_s, t + 1)
                    dve.scalar_tensor_tensor(xt, r2[:, b, :], wts[:, t, 1:2], xt, ALU.mult, ALU.add).then_inc(two_s, 1)
                if t:
                    o = t - 1
                    xo = x[:, o % BUFS, :]
                    dve.wait_ge(root_s, o + 1)
                    dve.reciprocal(q[:, o, :], q[:, o, :]).then_inc(inverse_s, 1)
                    dve.wait_ge(inverse_s, o + 1)
                    dve.scalar_tensor_tensor(xo, xo, q[:, o, :], wf[0:RL, :], ALU.mult, ALU.mult).then_inc(out_s, 1)


def program(nc, io):
    def dram(name, *shape):
        return nc.dram_tensor(name, shape, F32, kind="Internal").ap()

    z_dram, yc_dram, g_dram = dram("z_rows", NZ, P, T), dram("yc_rows", NC, P, T), dram("g_rows", NR, TP + CH)
    xbc_dram, x2_dram = dram("xbc_rows", NCONV - NQKV, P, T), dram("x2_rows", T, D)
    norm_drams = dram("qk_norm_rows", 2 * HA, T), dram("gate_norm_rows", 2 * HA, T)
    mixed_dram = dram("mixed_rows", NMIX - NC, P, T)
    slots_dram, y_dram = dram("slot_rows", SLOTS + BLK, D), dram("expert_rows", SLOTS, D)
    with ExitStack() as stack:
        m = Memory(nc, stack)
        ones = m.sb("ones", [P, P])
        masks = m.sb("masks", [P, 7, P])
        wts, idx = m.sb("wts", [RL, RT, TOPK]), m.sb("idx", [RL, RT, TOPK], mybir.dt.uint32)
        expert_of = m.sb("expert_of", [1, NBLK + 1], mybir.dt.int32)
        with ExitStack() as mixers:
            mm = Memory(nc, mixers)
            qkv = mm.sb("qkv", [P, NQKV, T])
            rows = [mm.sb(f"rows_{x}", [P, T]) for x in "abc"]
            with ExitStack() as first:
                hn = [Memory(nc, first).sb(f"hn_{x}", [P, KD, T], F32R) for x in ("hi", "lo")]
                gates = Gates(io, Memory(nc, first), hn, rows, g_dram)
                norm1_phase(nc, io, hn, gates, ones, masks)
                projection_phase(nc, io, hn, gates, qkv, xbc_dram, z_dram, yc_dram)
            xbc = mm.sb("xbc", [P, NCONV - NQKV, T])
            columns = Columns(mm)
            qk_norm_phase(nc, qkv, xbc, rows, columns, masks, xbc_dram, norm_drams[0])
            recurrence_phase(nc, io, qkv, xbc, columns, g_dram, masks, slots_dram)
            sampled_phase(nc, io, qkv, xbc, rows, g_dram, masks)
            gate_phase(nc, io, qkv, xbc, norm_drams[1], z_dram, mixed_dram)
        with ExitStack() as residual:
            mm = Memory(nc, residual)
            x2t = mm.sb("x2t", [P, KD, T])
            out_projection_phase(nc, io, mixed_dram, yc_dram, x2t)
            x2 = mm.sb("x2", [RL, RT, D])
            routing_phase(nc, io, x2t, x2, wts, idx, expert_of, masks, ones, slots_dram, x2_dram)
        expert_phase(nc, io, expert_of, masks, slots_dram, y_dram)
        combine_phase(nc, io, wts, idx, x2_dram, y_dram)


def channel_blocks(a):
    b, r, c = a.shape[1:]
    return a[0].reshape(b, r, c // P, P).transpose(3, 2, 0, 1)


def from_channel_blocks(a):
    p, n, b, r = a.shape
    return np.ascontiguousarray(a.transpose(2, 3, 1, 0).reshape(1, b, r, n * p))


def mask_constants():
    i = np.arange(P)
    later = i[None, :] >= i[:, None]
    below = i[:, None] > i[None, :]
    seq = i[:, None] // LSEQ == i[None, :] // LSEQ
    none = np.float32(NEG)
    zero = np.float32(0)
    out = np.stack([
        np.eye(P, dtype=np.float32),
        np.where(later, zero, none), np.where(below, zero, none),
        (i[:, None] // 16 == i[None, :] // 16).astype(np.float32),
        np.where(later & seq, zero, none), np.where(below & seq, zero, none),
        (i[:, None] // LSEQ == i[None, :]).astype(np.float32)], axis=1)
    return np.ascontiguousarray(out.astype(np.float32))


def route_constants():
    out = np.zeros((NE, 9 + NBLK + NE), np.float32)
    out[:, 0:8] = np.arange(8) * BLK
    out[:, 8:9 + NBLK] = np.arange(NBLK + 1)
    out[:, 9 + NBLK:] = np.arange(NE)[:, None] <= np.arange(NE)[None, :]
    return out


def lay_out(x):
    f = lambda n: np.asarray(x[n], dtype=np.float32)
    tokens = np.concatenate([f("meta_tokens"), f("x_prompt")[0], f("x_sample").reshape(TS, D)])
    w = f("w_in")[0]
    at = {}
    start = 0
    for name, n in (("qkv", 1536), ("z_a", 512), ("b", HA), ("a", HA), ("xbc", 1024), ("z_b", 512), ("dt", HB),
                    ("h", 512), ("c", 512), ("bb", 512)):
        at[name] = w[:, start:start + n]
        start += n
    short = [at[n][:, c * P:(c + 1) * P] for c in range(NC) for n in ("h", "c", "bb")]
    blocks = np.concatenate([at["qkv"], at["xbc"], at["z_a"], at["z_b"], *short], axis=1)
    gates = np.zeros((D, P), np.float32)
    gates[:, 0:HA], gates[:, ROW_G:ROW_G + HA], gates[:, ROW_G + HA:ROW_G + NR] = at["b"], at["a"], at["dt"]
    bias, alog = np.zeros((64, 1), np.float32), np.zeros((64, 1), np.float32)
    bias[ROW_G:ROW_G + HA, 0], bias[ROW_G + HA:ROW_G + NR, 0] = f("dt_bias_a")[0], f("dt_bias_b")[0]
    alog[ROW_G:ROW_G + HA, 0], alog[ROW_G + HA:ROW_G + NR, 0] = f("a_log_a")[0], f("a_log_b")[0]

    def columns(v):
        return v.reshape(-1, P).T

    def stationary(v, n):
        return v.reshape(-1, P, n, v.shape[1] // n).transpose(2, 1, 0, 3)

    taps = np.zeros((P, NCONV, W_A + 1), np.float32)
    taps[:, :12, :W_A] = f("conv_a_w")[0].reshape(W_A, 12, P).transpose(2, 1, 0)
    taps[:, 12:, :W_A] = f("conv_b_w")[0].reshape(W_A, 8, P).transpose(2, 1, 0)
    taps[:, 12:, W_A] = columns(f("conv_b_b")[0])
    io = {
        "xT": tokens.T.reshape(KD, P, T).transpose(1, 0, 2),
        "masks": mask_constants(),
        "norm1_w": columns(f("norm1_w")[0]), "norm2_w": columns(f("norm2_w")[0]),
        "w_gates": gates.reshape(KD, P, P).transpose(1, 0, 2), "gate_bias": bias, "gate_alog": alog,
        "w_in": stationary(blocks, NCONV + NZ + 3 * NC),
        "taps": taps, "taps_c": f("conv_c_w")[0].reshape(W_C, NC, P).transpose(2, 1, 0),
        "hist_ab": np.concatenate([channel_blocks(f("state_gdn_conv")), channel_blocks(f("state_ssd_conv"))], axis=1),
        "hist_c": channel_blocks(f("state_sconv")),
        "state_gdn": f("state_gdn")[0].transpose(2, 0, 1, 3),
        "state_ssd": f("state_ssd")[0].transpose(3, 0, 1, 2),
        "d_skip": columns(np.repeat(f("d_skip_b")[0], PB)),
        "onorm_a": columns(f("onorm_a_w")[0]), "onorm_b": columns(f("onorm_b_w")[0]),
        "w_out": stationary(f("w_out")[0], KD),
        "w_router": np.concatenate([f("w_router_g")[0], f("w_router_e")[0]], axis=1).reshape(KD, P, -1).transpose(1, 0, 2),
        "w_gate_up": np.concatenate([f("w_gate")[0], f("w_up")[0]], axis=2).reshape(NE, KD, P, 2 * FF).transpose(0, 2, 1, 3),
        "w_down": f("w_down")[0].reshape(NE, 2, P, D).transpose(0, 2, 1, 3),
        "norm2_row": f("norm2_w")[0], "final_row": f("final_norm_w"), "route_consts": route_constants(),
    }
    return {k: np.ascontiguousarray(v) for k, v in io.items()}


OUTPUTS = {
    "y": (T, D), "new_hist_ab": (P, NCONV, 1 + NSEQ, HIST), "new_hist_c": (P, NC, 1 + NSEQ, HISTC),
    "new_gdn_p": (P, HA, DK), "new_gdn_s": (P, NSEQ, HA, DK), "new_ssd_p": (P, HB, PB), "new_ssd_s": (P, NSEQ, HB, PB),
}


def kernel(**inputs):
    import concourse.bacc as bacc
    from concourse.bass_utils import run_bass_kernel_spmd

    nc = bacc.Bacc("TRN2", target_bir_lowering=False, num_devices=1)
    arrays = lay_out(inputs)
    io = {n: nc.dram_tensor("in_" + n, a.shape, F32, kind="ExternalInput").ap() for n, a in arrays.items()}
    io |= {n: nc.dram_tensor(n, s, F32, kind="ExternalOutput").ap() for n, s in OUTPUTS.items()}
    program(nc, io)
    got = run_bass_kernel_spmd(nc, [{"in_" + n: a for n, a in arrays.items()}], core_ids=[0]).results[0]

    y = got["y"]
    hist = got["new_hist_ab"]
    na = 3 * HA
    out = (
        y[N_META:TP][None], y[TP:].reshape(NSEQ, LSEQ, D),
        got["new_gdn_p"].transpose(1, 0, 2)[None, None],
        from_channel_blocks(hist[:, :na, :1]), got["new_ssd_p"].transpose(1, 2, 0)[None, None],
        from_channel_blocks(hist[:, na:, :1]), from_channel_blocks(got["new_hist_c"][:, :, :1]),
        got["new_gdn_s"].transpose(1, 2, 0, 3)[None],
        from_channel_blocks(hist[:, :na, 1:]), got["new_ssd_s"].transpose(1, 2, 3, 0)[None],
        from_channel_blocks(hist[:, na:, 1:]), from_channel_blocks(got["new_hist_c"][:, :, 1:]),
    )
    return tuple(np.ascontiguousarray(a) for a in out)
```
